# Optimizing a Trainium2 kernel written in Bass

```python
import math
import jax
import jax.numpy as jnp
from jax import lax
import numpy as np

D_MODEL = 1024
BATCH = 1
SEQ = 1024
DEPTH = 1
DEC_BATCH = 8
DEC_SEQ = 4
PAST_LEN = 8192
PAGE_SIZE = 128

S5_WIDTH = D_MODEL // 4
S5_GROUP = 16
S5_GROUPS = S5_WIDTH // S5_GROUP
S5_STATE = 64
S5_DT_MIN = 1e-3
S5_DT_MAX = 1e-1
RW_WIDTH = D_MODEL // 2
RW_HEAD = 64
RW_HEADS = RW_WIDTH // RW_HEAD
RW_DECAY_LORA = 32
RW_AAA_LORA = 32
RW_GATE_LORA = 64
RW_COLS = 3 * RW_WIDTH + RW_DECAY_LORA + RW_AAA_LORA + RW_GATE_LORA
RW_SPLITS = (RW_WIDTH, 2 * RW_WIDTH, 3 * RW_WIDTH, 3 * RW_WIDTH + RW_DECAY_LORA,
             3 * RW_WIDTH + RW_DECAY_LORA + RW_AAA_LORA)
RW_GN_EPS = 1e-5 * RW_HEAD
HG_WIDTH = D_MODEL // 4
HG_HEAD = 64
HG_HEADS = HG_WIDTH // HG_HEAD
HG_CHUNK = 16
HG_GATE_FLOOR = 1e-30
N_BRANCH = 3
IN_COLS = S5_WIDTH + RW_COLS + 4 * HG_WIDTH + N_BRANCH * D_MODEL
IN_SPLITS = (S5_WIDTH, S5_WIDTH + RW_COLS, S5_WIDTH + RW_COLS + HG_WIDTH,
             S5_WIDTH + RW_COLS + 2 * HG_WIDTH, S5_WIDTH + RW_COLS + 3 * HG_WIDTH,
             S5_WIDTH + RW_COLS + 4 * HG_WIDTH)
D_FF = 256 * ((8 * D_MODEL // 3 + 255) // 256)
CONV_W = 3
RMS_EPS = 1e-6
F32 = jnp.float32

kernel_name = 'hybrid_s5_rwkv7_hgrn2_convffn_step'

def rms_norm(x, g):
    xf = x.astype(F32)
    return xf * lax.rsqrt(jnp.mean(xf * xf, axis=-1, keepdims=True) + RMS_EPS) * g.astype(F32)

def modulate(x, g, shift, scale):
    return rms_norm(x, g) * (1.0 + scale[:, None, :]) + shift[:, None, :]

def _complex_affine_combine(e1, e2):
    a1r, a1i, b1r, b1i = e1
    a2r, a2i, b2r, b2i = e2
    return (a2r * a1r - a2i * a1i, a2r * a1i + a2i * a1r,
            a2r * b1r - a2i * b1i + b2r, a2r * b1i + a2i * b1r + b2i)

def s5_mixer(u, s_prev, lam_re, lam_im, log_dt, b_re, b_im, c_re, c_im, d_skip, w_glu, b_glu):
    n, l, _ = u.shape
    ug = u.astype(F32).reshape(n, l, S5_GROUPS, S5_GROUP)
    lr = lam_re.astype(F32)
    li = lam_im.astype(F32)
    dt = jnp.exp(log_dt.astype(F32))[:, None]
    mag = jnp.exp(lr * dt)
    ar = mag * jnp.cos(li * dt)
    ai = mag * jnp.sin(li * dt)
    den = lr * lr + li * li
    zr = ((ar - 1.0) * lr + ai * li) / den
    zi = (ai * lr - (ar - 1.0) * li) / den
    bbr = zr[..., None] * b_re - zi[..., None] * b_im
    bbi = zr[..., None] * b_im + zi[..., None] * b_re
    er = jnp.einsum('nlgc,gpc->nlgp', ug, bbr)
    ei = jnp.einsum('nlgc,gpc->nlgp', ug, bbi)
    pr = s_prev[..., 0].astype(F32)
    pi = s_prev[..., 1].astype(F32)
    er = er.at[:, 0].add(ar * pr - ai * pi)
    ei = ei.at[:, 0].add(ar * pi + ai * pr)
    ar_t = jnp.broadcast_to(ar, er.shape)
    ai_t = jnp.broadcast_to(ai, ei.shape)
    _, _, sr, si = lax.associative_scan(_complex_affine_combine, (ar_t, ai_t, er, ei), axis=1)
    y = jnp.einsum('nlgp,gcp->nlgc', sr, c_re) - jnp.einsum('nlgp,gcp->nlgc', si, c_im)
    y = y.reshape(n, l, S5_WIDTH) + d_skip * u
    y = jax.nn.gelu(y)
    y = y * jax.nn.sigmoid(y @ w_glu + b_glu)
    return y, jnp.stack([sr[:, -1], si[:, -1]], axis=-1)

def rwkv7_mixer(p, shift_prev, s_prev, mu, w0, w2, a0, a2, g2, k_k, k_a, r_k, ln_w, ln_b):
    n, l, _ = p.shape
    p = p.astype(F32)
    p_prev = jnp.concatenate([shift_prev[:, None, :].astype(F32), p[:, :-1]], axis=1)
    xm = p + (p_prev - p) * mu
    r, k, v, wd, ad, gd = jnp.split(xm, RW_SPLITS, axis=-1)
    w = -jax.nn.softplus(-(w0 + jnp.tanh(wd) @ w2)) - 0.5
    decay = jnp.exp(-jnp.exp(w))
    a = jax.nn.sigmoid(a0 + ad @ a2)
    g = jax.nn.sigmoid(gd) @ g2

    def hd(t):
        return t.reshape(n, l, RW_HEADS, RW_HEAD)

    kk = hd(k * k_k)
    kk = kk / jnp.maximum(jnp.sqrt(jnp.sum(kk * kk, axis=-1, keepdims=True)), 1e-12)
    k = hd(k * (1.0 + (a - 1.0) * k_a))
    r, v, decay, a = hd(r), hd(v), hd(decay), hd(a)
    seq = tuple(jnp.moveaxis(t, 1, 0) for t in (r, decay, k, v, -kk, kk * a))

    def step(s, inp):
        r_t, w_t, k_t, v_t, a_t, b_t = inp
        sa = jnp.einsum('nhvk,nhk->nhv', s, a_t)
        s = (s * w_t[:, :, None, :] + sa[..., None] * b_t[:, :, None, :]
             + v_t[..., None] * k_t[:, :, None, :])
        return s, jnp.einsum('nhvk,nhk->nhv', s, r_t)

    s_last, y = lax.scan(step, s_prev.astype(F32), seq)
    y = jnp.moveaxis(y, 0, 1)
    mean = jnp.mean(y, axis=-1, keepdims=True)
    var = jnp.mean(jnp.square(y - mean), axis=-1, keepdims=True)
    y = ((y - mean) * lax.rsqrt(var + RW_GN_EPS)).reshape(n, l, RW_WIDTH) * ln_w + ln_b
    bonus = jnp.sum(r * k * r_k, axis=-1, keepdims=True) * v
    y = (y + bonus.reshape(n, l, RW_WIDTH)) * g
    return y, p[:, -1], s_last

def hgrn2_mixer(q, f, i, og, s_prev, lower, norm_g):
    n, l, _ = q.shape
    lower = lower.astype(F32)
    sig_f = jax.nn.sigmoid(f.astype(F32))
    fgate = lower + (1.0 - lower) * sig_f
    log_f = jnp.log(jnp.maximum(fgate, HG_GATE_FLOOR))
    k = 1.0 - fgate
    q = jax.nn.silu(q.astype(F32))
    pad = (-l) % HG_CHUNK
    nc = (l + pad) // HG_CHUNK

    def to_blocks(t):
        t = t.reshape(n, l, HG_HEADS, HG_HEAD)
        t = jnp.pad(t, ((0, 0), (0, pad), (0, 0), (0, 0)))
        return t.reshape(n, nc, HG_CHUNK, HG_HEADS, HG_HEAD).transpose(1, 0, 3, 2, 4)

    causal = jnp.tril(jnp.ones((HG_CHUNK, HG_CHUNK), dtype=bool))[:, :, None]

    def step(s, blk):
        qc, kc, vc, gc = blk
        b = jnp.cumsum(gc, axis=2)
        o_inter = jnp.einsum('nhtk,nhkv->nhtv', qc * jnp.exp(b), s)
        diff = b[:, :, :, None, :] - b[:, :, None, :, :]
        dec = jnp.where(causal, jnp.exp(jnp.where(causal, diff, 0.0)), 0.0)
        att = jnp.einsum('nhtk,nhsk,nhtsk->nhts', qc, kc, dec)
        o_intra = jnp.einsum('nhts,nhsv->nhtv', att, vc)
        b_end = b[:, :, -1]
        s = (jnp.exp(b_end)[..., None] * s
             + jnp.einsum('nhsk,nhsv->nhkv', kc * jnp.exp(b_end[:, :, None, :] - b), vc))
        return s, o_inter + o_intra

    blocks = tuple(to_blocks(t) for t in (q, k, i.astype(F32), log_f))
    s_last, o = lax.scan(step, s_prev.astype(F32), blocks)
    o = o.transpose(1, 0, 3, 2, 4).reshape(n, nc * HG_CHUNK, HG_HEADS, HG_HEAD)[:, :l]
    o = o * lax.rsqrt(jnp.mean(o * o, axis=-1, keepdims=True) + RMS_EPS)
    o = o.reshape(n, l, HG_WIDTH) * norm_g * jax.nn.sigmoid(og)
    return o, s_last

def causal_dwconv(buf, w, b, l):
    out = b + w[0] * buf[:, 0:l]
    for j in range(1, CONV_W):
        out = out + w[j] * buf[:, j:j + l]
    return out

def run_trunk(x, c, st_s5, st_shift, st_rw, st_hg, st_conv, lower, final_g, prm):
    n, l, _ = x.shape
    cs = jax.nn.silu(c.astype(F32))
    h_res = x.astype(F32)
    out_s5, out_shift, out_rw, out_hg, out_conv = [], [], [], [], []
    for layer in range(DEPTH):
        p = {name: arr[layer] for name, arr in prm.items()}
        mod = cs @ p['w_ada'] + p['b_ada']
        sh1, sc1, gt1, sh2, sc2, gt2 = jnp.split(mod, 6, axis=-1)
        h = modulate(h_res, p['g_mix'], sh1, sc1)
        z = h @ p['w_in']
        u_a, p_b, q_c, f_c, i_c, og_c, gate_logits = jnp.split(z, IN_SPLITS, axis=-1)
        y_a, s5_new = s5_mixer(u_a, st_s5[layer], p['s5_lambda_re'], p['s5_lambda_im'],
                               p['s5_log_dt'], p['s5_b_re'], p['s5_b_im'], p['s5_c_re'],
                               p['s5_c_im'], p['s5_d'], p['s5_w_glu'], p['s5_b_glu'])
        y_b, shift_new, rw_new = rwkv7_mixer(p_b, st_shift[layer], st_rw[layer], p['rw_mu'],
                                             p['rw_w0'], p['rw_w2'], p['rw_a0'], p['rw_a2'],
                                             p['rw_g2'], p['rw_k_k'], p['rw_k_a'], p['rw_r_k'],
                                             p['rw_ln_w'], p['rw_ln_b'])
        y_c, hg_new = hgrn2_mixer(q_c, f_c, i_c, og_c, st_hg[layer], lower[layer], p['hg_norm'])
        gates = jax.nn.sigmoid(gate_logits).reshape(n, l, N_BRANCH, D_MODEL)
        merged = (gates[:, :, 0] * (y_a @ p['w_lift_a'])
                  + gates[:, :, 1] * (y_b @ p['w_lift_b'])
                  + gates[:, :, 2] * (y_c @ p['w_lift_c']))
        h_res = h_res + gt1[:, None, :] * (merged @ p['w_out'])
        h2 = modulate(h_res, p['g_ffn'], sh2, sc2)
        up = h2 @ p['w_up']
        buf = jnp.concatenate([st_conv[layer].astype(F32), up], axis=1)
        conv = causal_dwconv(buf, p['conv_w'], p['conv_b'], l)
        a_ff, b_ff = jnp.split(conv, 2, axis=-1)
        h_res = h_res + gt2[:, None, :] * ((jax.nn.gelu(a_ff) * b_ff) @ p['w_down'])
        out_s5.append(s5_new)
        out_shift.append(shift_new)
        out_rw.append(rw_new)
        out_hg.append(hg_new)
        out_conv.append(buf[:, -(CONV_W - 1):])
    y = rms_norm(h_res, final_g).astype(x.dtype)
    return y, (jnp.stack(out_s5), jnp.stack(out_shift), jnp.stack(out_rw),
               jnp.stack(out_hg), jnp.stack(out_conv))

def setup_inputs(seed: int = 0) -> dict:
    keys = iter(jax.random.split(jax.random.key(seed), 64))

    def nrm(shape, std):
        return std * jax.random.normal(next(keys), shape, F32)

    def unif(shape, lo, hi):
        return jax.random.uniform(next(keys), shape, F32, lo, hi)

    L = DEPTH
    d_in = D_MODEL ** -0.5
    n_idx = jnp.arange(S5_STATE, dtype=F32)
    return {
        'x_prompt': nrm((BATCH, SEQ, D_MODEL), 1.0),
        'x_sample': nrm((DEC_BATCH, DEC_SEQ, D_MODEL), 1.0),
        'c_prompt': nrm((BATCH, D_MODEL), 1.0),
        'c_sample': nrm((DEC_BATCH, D_MODEL), 1.0),
        'state_s5': nrm((L, DEC_BATCH, S5_GROUPS, S5_STATE, 2), 0.2),
        'state_rwkv_shift': nrm((L, DEC_BATCH, RW_COLS), 1.0),
        'state_rwkv': nrm((L, DEC_BATCH, RW_HEADS, RW_HEAD, RW_HEAD), 0.3),
        'state_hgrn': nrm((L, DEC_BATCH, HG_HEADS, HG_HEAD, HG_HEAD), 0.5),
        'state_ffn_conv': nrm((L, DEC_BATCH, CONV_W - 1, 2 * D_FF), 1.0),
        'w_ada': nrm((L, D_MODEL, 6 * D_MODEL), 0.5 * d_in),
        'b_ada': nrm((L, 6 * D_MODEL), 0.01),
        'g_mix': 1.0 + nrm((L, D_MODEL), 0.1),
        'g_ffn': 1.0 + nrm((L, D_MODEL), 0.1),
        'w_in': nrm((L, D_MODEL, IN_COLS), d_in),
        's5_lambda_re': -0.5 + nrm((L, S5_GROUPS, S5_STATE), 0.01),
        's5_lambda_im': math.pi * n_idx + nrm((L, S5_GROUPS, S5_STATE), 0.01),
        's5_log_dt': unif((L, S5_GROUPS), math.log(S5_DT_MIN), math.log(S5_DT_MAX)),
        's5_b_re': nrm((L, S5_GROUPS, S5_STATE, S5_GROUP), (2 * S5_GROUP) ** -0.5),
        's5_b_im': nrm((L, S5_GROUPS, S5_STATE, S5_GROUP), (2 * S5_GROUP) ** -0.5),
        's5_c_re': nrm((L, S5_GROUPS, S5_GROUP, S5_STATE), 0.5),
        's5_c_im': nrm((L, S5_GROUPS, S5_GROUP, S5_STATE), 0.5),
        's5_d': nrm((L, S5_WIDTH), 0.5),
        's5_w_glu': nrm((L, S5_WIDTH, S5_WIDTH), S5_WIDTH ** -0.5),
        's5_b_glu': nrm((L, S5_WIDTH), 0.01),
        'rw_mu': unif((L, RW_COLS), 0.0, 1.0),
        'rw_w0': unif((L, RW_WIDTH), -6.0, 1.0),
        'rw_w2': nrm((L, RW_DECAY_LORA, RW_WIDTH), 0.1),
        'rw_a0': nrm((L, RW_WIDTH), 0.5),
        'rw_a2': nrm((L, RW_AAA_LORA, RW_WIDTH), 0.1),
        'rw_g2': nrm((L, RW_GATE_LORA, RW_WIDTH), RW_GATE_LORA ** -0.5),
        'rw_k_k': 0.85 + nrm((L, RW_WIDTH), 0.1),
        'rw_k_a': 1.0 + nrm((L, RW_WIDTH), 0.1),
        'rw_r_k': nrm((L, RW_HEADS, RW_HEAD), 0.1),
        'rw_ln_w': 1.0 + nrm((L, RW_WIDTH), 0.1),
        'rw_ln_b': nrm((L, RW_WIDTH), 0.01),
        'hg_lb': nrm((L, HG_WIDTH), 1.0),
        'hg_norm': 1.0 + nrm((L, HG_WIDTH), 0.1),
        'w_lift_a': nrm((L, S5_WIDTH, D_MODEL), S5_WIDTH ** -0.5),
        'w_lift_b': nrm((L, RW_WIDTH, D_MODEL), RW_WIDTH ** -0.5),
        'w_lift_c': nrm((L, HG_WIDTH, D_MODEL), HG_WIDTH ** -0.5),
        'w_out': nrm((L, D_MODEL, D_MODEL), d_in),
        'w_up': nrm((L, D_MODEL, 2 * D_FF), d_in),
        'conv_w': nrm((L, CONV_W, 2 * D_FF), CONV_W ** -0.5),
        'conv_b': nrm((L, 2 * D_FF), 0.01),
        'w_down': nrm((L, D_FF, D_MODEL), D_FF ** -0.5),
        'final_g': 1.0 + nrm((D_MODEL,), 0.1),
    }

def reference(x_prompt, x_sample, c_prompt, c_sample, state_s5, state_rwkv_shift, state_rwkv,
              state_hgrn, state_ffn_conv, w_ada, b_ada, g_mix, g_ffn, w_in, s5_lambda_re,
              s5_lambda_im, s5_log_dt, s5_b_re, s5_b_im, s5_c_re, s5_c_im, s5_d, s5_w_glu,
              s5_b_glu, rw_mu, rw_w0, rw_w2, rw_a0, rw_a2, rw_g2, rw_k_k, rw_k_a, rw_r_k,
              rw_ln_w, rw_ln_b, hg_lb, hg_norm, w_lift_a, w_lift_b, w_lift_c, w_out, w_up,
              conv_w, conv_b, w_down, final_g):
    prm = {
        'w_ada': w_ada, 'b_ada': b_ada, 'g_mix': g_mix, 'g_ffn': g_ffn, 'w_in': w_in,
        's5_lambda_re': s5_lambda_re, 's5_lambda_im': s5_lambda_im, 's5_log_dt': s5_log_dt,
        's5_b_re': s5_b_re, 's5_b_im': s5_b_im, 's5_c_re': s5_c_re, 's5_c_im': s5_c_im,
        's5_d': s5_d, 's5_w_glu': s5_w_glu, 's5_b_glu': s5_b_glu,
        'rw_mu': rw_mu, 'rw_w0': rw_w0, 'rw_w2': rw_w2, 'rw_a0': rw_a0, 'rw_a2': rw_a2,
        'rw_g2': rw_g2, 'rw_k_k': rw_k_k, 'rw_k_a': rw_k_a, 'rw_r_k': rw_r_k,
        'rw_ln_w': rw_ln_w, 'rw_ln_b': rw_ln_b, 'hg_norm': hg_norm,
        'w_lift_a': w_lift_a, 'w_lift_b': w_lift_b, 'w_lift_c': w_lift_c, 'w_out': w_out,
        'w_up': w_up, 'conv_w': conv_w, 'conv_b': conv_b, 'w_down': w_down,
    }
    lbp = jax.nn.softmax(hg_lb.astype(F32), axis=0)
    lower = jnp.cumsum(lbp, axis=0) - lbp[0]

    nb = x_prompt.shape[0]
    z_s5 = jnp.zeros((DEPTH, nb) + state_s5.shape[2:], F32)
    z_shift = jnp.zeros((DEPTH, nb) + state_rwkv_shift.shape[2:], F32)
    z_rw = jnp.zeros((DEPTH, nb) + state_rwkv.shape[2:], F32)
    z_hg = jnp.zeros((DEPTH, nb) + state_hgrn.shape[2:], F32)
    z_conv = jnp.zeros((DEPTH, nb) + state_ffn_conv.shape[2:], F32)

    y_prompt, (s5_p, shift_p, rw_p, hg_p, conv_p) = run_trunk(
        x_prompt, c_prompt, z_s5, z_shift, z_rw, z_hg, z_conv, lower, final_g, prm)
    y_sample, (s5_s, shift_s, rw_s, hg_s, conv_s) = run_trunk(
        x_sample, c_sample, state_s5, state_rwkv_shift, state_rwkv, state_hgrn, state_ffn_conv,
        lower, final_g, prm)
    return (y_prompt, y_sample, s5_p, shift_p, rw_p, hg_p, conv_p, s5_s, shift_s, rw_s, hg_s, conv_s)


_drawn_inputs = setup_inputs


def setup_inputs(seed=0):
    import zlib

    import numpy as np

    out = dict(_drawn_inputs(seed))
    spreads = {}
    factors = {'s5_lambda_re': 11.768,
     's5_b_glu': 64.0,
     'rw_ln_w': 6.179,
     'rw_ln_b': 64.0,
     'hg_norm': 5.686,
     'conv_b': 22.431,
     's5_w_glu': 3.284}
    for name, (base, spread) in spreads.items():
        noise = np.random.default_rng([zlib.crc32(name.encode()), seed]).standard_normal(out[name].shape)
        drawn = base * np.exp(spread * noise) if base else spread * noise
        out[name] = jnp.asarray(drawn.astype(out[name].dtype))
    for name, factor in factors.items():
        out[name] = (out[name] * factor).astype(out[name].dtype)
    return out
```

```python
import math
from contextlib import ExitStack

import concourse.bass as bass
from concourse import mybir

F32 = mybir.dt.float32
BF16 = mybir.dt.bfloat16
ALU = mybir.AluOpType
ACT = mybir.ActivationFunctionType
MUL, ADD, SUB, MAX = ALU.mult, ALU.add, ALU.subtract, ALU.max

P = 128
D = 1024
KT = D // P
TP = 1024
NS, LS = 8, 4
TS = NS * LS
T = TP + TS
G, GW = 3, T // 3
NSEQ = 1 + NS
SW = 256
NJ = 8
RC = 1664
RT = RC // P
HW = 256
FF = 2816
FT = FF // P
HC = 16
HN = TP // HC + NS
HT = HN * HC
RCH = 64
RN = TP // RCH + NS
LEVELS = 6
C_DECAY = math.exp(-0.5)
TWO_PI_HI = 6.28125
TWO_PI_LO = 2 * math.pi - 6.28125
ROUND = 12582912.0
PI_SAFE = 3.1415925
RMS_EPS = 1e-6
GN_EPS = 1e-5 * 64
RING_OUT = 23 * G
RING_UP = 31 * G
N_SMALL = 26
HALVES = ((0, 12), (12, 22))

ROWS = (
    (("b_ada", 48), ("g_mix", 8), ("g_ffn", 8), ("final_g", 8), ("rw_mu", 13), ("rw_w0", 4), ("rw_a0", 4),
     ("rw_k_k", 4), ("rw_k_a", 4), ("rw_r_k", 4), ("rw_ln_w", 4), ("rw_ln_b", 4), ("hg_lb", 2), ("hg_norm", 2),
     ("s5_d", 2), ("s5_b_glu", 2)),
    (("s5_log_dt", 8), ("s5_lambda_re", 8), ("s5_lambda_im", 8), ("conv_b", 44), ("conv_w2", 44)),
    (("conv_w0", 44), ("conv_w1", 44)),
)


def weight_chunks():
    out = [("ada", c, 1) for c in range(12)]
    out += [("s5", 0, 2 * G), ("hg", 0, 4 * G), ("hg", 1, 4 * G), ("lora", 0, G)]
    out += [("rkv", j, 3 * G) for j in range(4)]
    out += [("merge", n, 3 * G) for n in range(KT)]
    out += [("out", c, 4 * G) for c in range(2)]
    for m0, m1 in HALVES:
        out += [("up", m, 4 * G) for m in range(m0, m1, 2)]
        out += [("down", (m0, c), 2 * G) for c in range(4)]
    return out


def trunk(nc, I, O):
    ctx = ExitStack()

    def sb(name, shape, dt=F32):
        return ctx.enter_context(nc.sbuf_tensor(name, shape, dt))

    with ctx:
        hT = sb("hT", [P, KT, T])
        Y = sb("Y", [P, KT, T])
        W = sb("W", [P, 2, 4096])
        PAR = sb("PAR", [P, 3, P])
        MOD = sb("MOD", [P, 48, NSEQ])
        GSC = sb("GSC", [P, 2, KT, NSEQ])
        csT = sb("csT", [P, KT, NSEQ])
        ident = sb("ident", [P, P])
        ones = sb("ones", [P, P])
        hones = sb("hones", [P, P])
        m_ar = sb("m_ar", [P, 2, RCH])
        m_lt = sb("m_lt", [P, LEVELS, RCH])
        m_l0 = sb("m_l0", [P, RCH])
        idS = sb("idS", [P, RCH])
        m16 = sb("m16", [P, 8])
        resets = sb("resets", [P, T], BF16)
        shT = sb("shT", [P, RT, NS])
        shO = sb("shO", [P, RT, NSEQ])
        st5 = sb("st5", [P, 2, NJ, NS])
        ls5 = sb("ls5", [P, 2, NJ, NSEQ])
        s5v = sb("s5v", [P, 24, NJ])
        wpw = sb("wpw", [P, 10, 2, NJ])
        inj = sb("inj", [P, 2, NJ, NS])
        inj_t = sb("inj_t", [P, NJ, NS])
        low = sb("low", [P, 4, 2])
        AR = 24220
        arena = sb("arena", [P, AR])

        def carve(off, *shape):
            n = math.prod(shape)
            assert off + n <= AR, (off, shape)
            a = arena[:, off:off + n]
            if len(shape) == 1:
                return a
            names = "abcd"[:len(shape)]
            return a.rearrange(f"p ({' '.join(names)}) -> p {' '.join(names)}", **dict(zip(names, shape)))

        ps = ctx.enter_context(nc.psum_tensor("ps", [P, 8, 512], F32))
        pb = [ps[:, i, :] for i in range(8)]

        sems = {}

        def sem(name):
            if name not in sems:
                sems[name] = ctx.enter_context(nc.semaphore(name))
            return sems[name]

        def par(name, j=0, n=1, lo=0, hi=P):
            for t, rows in enumerate(ROWS):
                at = 0
                for nm, k in rows:
                    if nm == name:
                        return PAR[lo:hi, t, at + j:at + j + n]
                    at += k
            raise KeyError(name)

        xT = carve(0, KT, T)
        xr = carve(8448, 2, D)
        sq = carve(10496, 2, T)
        rstd = carve(12608, T)
        hn = carve(13664, T)
        rows = carve(14720, 3, P)
        crow = carve(15104, D)
        shrow = carve(16128, RC)
        s5row = carve(17792, 2048)
        U5 = carve(0, 2, T)
        ZH = carve(2112, 4, 2, HT)
        tc, ts = carve(11328, T), carve(12384, T)
        e0, e1, t0, t1 = (carve(13440 + T * i, T) for i in range(4))
        Mg = carve(17664, T)
        BTl = carve(18720, 2, NJ, P)
        CTl = carve(20768, 2, NJ, P)
        BB = carve(13440, 2, NJ, P)
        BRI = carve(22816, 2, NJ, 16)
        CRI = carve(23072, 2, 2, 2, 64)
        BBt = carve(23584, 2, NJ, 16)
        wglu = carve(17664, 2, SW)
        s5out = carve(18720, NJ, P, 2)
        K0, K1, Hp0, Hp1, Ht0, Ht1, Ho, HD, HK = (carve(11328 + HT * i, HT) for i in range(9))
        tok = carve(11328, 2, 2, P)
        Vblk = carve(11840, 2, 8, 64)
        Sx = carve(12864, 81, 64)
        assert 12864 + 81 * 64 <= 11328 + 6 * HT
        Z = [carve(1065 * i, 1065) for i in range(4)]
        ARp = carve(4260, RN, 2, RCH)
        Bp = carve(7332, RN, RCH)
        Kp = carve(8868, RN, RCH)
        Vp = carve(10404, RN, RCH)
        Rc, Kc, C1, C2 = (carve(11940 + T * i, T) for i in range(4))
        Vt, Bt, Kt_ = (carve(16164 + 512 * i, 8, RCH) for i in range(3))
        LA = carve(17700, 8, 2, RCH)
        KA = carve(18724, 8, 2, RCH)
        X, XT, Yb, LTm = (carve(19748 + 512 * i, 8, RCH) for i in range(4))
        Gb = carve(21796, RCH)
        Ub = carve(21860, RCH)
        S2 = carve(21924, 2, RCH)
        SPc = carve(22052, RCH)
        Sin = carve(22116, 8, RCH)
        Sout = carve(11940, 8, RCH)
        PC = carve(22628, RN)
        Lw = carve(22652, 512)
        Lx = carve(23164, T)
        SR = C1[:, 0:512].rearrange("p (a b) -> p a b", a=8)
        SO = C1[:, 0:576].rearrange("p (a b) -> p a b", a=9)
        MG = carve(10496, KT, T)
        sig = carve(18944, 3, GW)
        mt = carve(20000, 3, GW)
        shrow2 = carve(21056, RC)
        FFh = carve(10496, 12, T)
        Yf = Y[:, :, :].rearrange("p a b -> p (a b)")
        UL = 2 + TP + 6 * NS
        Uab = [Yf[:, UL * i:UL * (i + 1)] for i in range(4)]
        Cab = [Yf[:, 4 * UL + T * i:4 * UL + T * (i + 1)] for i in range(3)]
        crw = Yf[:, 7464:7976]
        cob = Yf[:, 7976:8048].rearrange("p (a b) -> p a b", a=4)
        cvr = carve(23168, 2, 512)
        yrow = carve(10496, 2, D)
        sq2, rstd2, hn2 = carve(18944, 2, T), carve(21056, T), carve(22112, T)

        chunks = weight_chunks()
        index = {(k, c): i for i, (k, c, _) in enumerate(chunks)}
        signals = [0]
        for _, _, n in chunks:
            signals.append(signals[-1] + n)

        w_in, w_up, w_down = I["w_in"][0], I["w_up"][0], I["w_down"][0]

        def wsrc(kind, c):
            if kind == "ada":
                return [(0, 8, 512, I["w_ada"][0][:, c * 512:(c + 1) * 512])]
            if kind == "s5":
                return [(0, 8, 256, w_in[:, 0:256])]
            if kind == "hg":
                return [(0, 8, 512, w_in[:, SW + RC + 512 * c:SW + RC + 512 * (c + 1)])]
            if kind == "lora":
                return [(0, 8, 128, w_in[:, SW + 1536:SW + RC])]
            if kind == "rkv":
                return [(1024 * b, 8, 128, w_in[:, SW + 512 * b + 128 * c:SW + 512 * b + 128 * (c + 1)])
                        for b in range(3)]
            if kind == "merge":
                g0 = SW + RC + 4 * HW
                return [(1024 * b, 8, 128, w_in[:, g0 + D * b + P * c:g0 + D * b + P * (c + 1)]) for b in range(3)] + [
                    (3072, 2, 128, I["w_lift_a"][0][:, P * c:P * (c + 1)]),
                    (3328, 4, 128, I["w_lift_b"][0][:, P * c:P * (c + 1)]),
                    (3840, 2, 128, I["w_lift_c"][0][:, P * c:P * (c + 1)])]
            if kind == "out":
                return [(0, 8, 512, I["w_out"][0][:, c * 512:(c + 1) * 512])]
            if kind == "up":
                return [(0, 8, 256, w_up[:, P * c:P * (c + 2)]), (2048, 8, 256, w_up[:, FF + P * c:FF + P * (c + 2)])]
            m0, q = c
            m1 = dict(HALVES)[m0]
            return [(0, m1 - m0, 256, w_down[P * m0:P * m1, 256 * q:256 * (q + 1)])]

        loads = []
        total = [0, 0]
        for i, (k, c, _) in enumerate(chunks):
            total[i % 2] += 16 * len(wsrc(k, c))
            loads.append(total[i % 2])

        def wslot(i, off, n, cols):
            return W[:, i % 2, off:off + n * cols].rearrange("p (k c) -> p k c", k=n)

        def gcol(g):
            return slice(g * GW, (g + 1) * GW)

        XQ = 9

        def xrows(i):
            return P if i < 8 else TS


        Hn = K0
        K_tmp = carve(17664, 2, NJ, 16)
        chunk_decay = sb("chunk_decay", [P, HN])
        res_t = sb("res_t", [P, TS])
        ldt = sb("ldt", [NJ, 2])
        flag = sb("flag", [P, 1])

        def lt_count(j, bt, l):
            return 11 * j + 5 * bt + l

        def lag_out(v, dve, step, tt, cv, t, d, v_):
            w, bs = HC - d, 3 * (d % 2)
            dve.wait_ge(sem("att_done"), HC * t + d + 1)
            att = ps[:, bs:bs + 3, 0:24 * w].rearrange("p g (c t) -> p g c t", t=w)
            vs = cv(v_)[:, :, 0:w].rearrange("p (g c) t -> p g c t", g=3)
            if d == 0:
                step(tt(cv(Ho).rearrange("p (g c) t -> p g c t", g=3), att, vs, MUL), "att_ev")
            else:
                tmp = cv(Ht0)[:, :, 0:w]
                step(tt(tmp.rearrange("p (g c) t -> p g c t", g=3), att, vs, MUL), "att_ev")
                step(tt(cv(Ho)[:, :, d:], cv(Ho)[:, :, d:], tmp, ADD))

        def state_out(v, dve, step, stt, t, b):
            dve.wait_ge(sem("u_done"), 9 * t + b + 1)
            for c in range(8):
                ci = 8 * b + c
                s, o = (Sx[:, ci], Sx[:, ci + 1]) if b < 8 else (Sx[:, 65 + c], Sx[:, 73 + c])
                step(stt(o, s, chunk_decay[:, ci:ci + 1], pb[b % 2][:, 64 * c:64 * c + 64], MUL, ADD),
                     "u_ev" if c == 7 else "dve_step")

        block = ctx.enter_context(nc.Block())

        @block.sync
        def _(sp):
            n_small = [0]

            def small(dst, src):
                n_small[0] += 1
                sp.dma_start(dst, src).then_inc(sem("small_in"), 16)

            def vec(a):
                while len(a.shape) > 1:
                    a = a[0] if a.shape[0] == 1 else a.rearrange("a b -> (a b)")
                return a.rearrange("(r c) -> r c", c=P)

            sp.wait_ge(sem("rows_zeroed"), 1)
            for t, rws in enumerate(ROWS):
                at = 0
                for nm, k in rws:
                    dst = rows[at:at + k, t, :]
                    if nm == "s5_log_dt":
                        sp.dma_start(ldt[:], I[nm][0].rearrange("(j g) -> j g", g=2)).then_inc(sem("ldt_in"), 16)
                    elif nm.startswith("conv_w"):
                        small(dst, I["conv_w"][0][int(nm[-1])].rearrange("(r c) -> r c", c=P))
                    else:
                        small(dst, vec(I[nm]))
                    at += k
            small(crow[0:1, :], I["c_prompt"])
            small(crow[1:NSEQ, :], I["c_sample"])
            small(shrow[0:NS, :], I["state_rwkv_shift"][0])
            small(s5row[0:NS, :], I["state_s5"][0].rearrange("n g p c -> n (g p c)"))
            assert n_small[0] == N_SMALL, n_small

            def load_x(base, i):
                src = I["x_prompt"][0][P * i:P * (i + 1), :] if i < 8 else I["x_sample"].rearrange("n t d -> (n t) d")
                sp.dma_start(xr[0:xrows(i), i % 2, :], src).then_inc(sem(f"x_in{i % 2}"), 16)

            def weights(i):
                k, c, _ = chunks[i]
                if i >= 2:
                    sp.wait_ge(sem("gemm_done"), signals[i - 1])
                for off, n, cols, src in wsrc(k, c):
                    sp.dma_start(wslot(i, off, n, cols), src.rearrange("(k p) c -> p k c", p=P))\
                        .then_inc(sem(f"w_in{i % 2}"), 16)

            for i in range(2):
                load_x(0, i)
            for i in range(2):
                weights(i)
            for i in range(2, XQ):
                sp.wait_ge(sem("x_turned"), i - 1)
                load_x(0, i)
            for i in range(2, index[("s5", 0)] + 1):
                weights(i)
            sp.wait_ge(sem("h_ready"), 1)
            for ri, nm in enumerate(("s5_b_re", "s5_b_im")):
                sp.dma_start(BRI[:, ri], I[nm][0].rearrange("(j g) p c -> (g p) j c", g=2)).then_inc(sem("s5_in"), 16)
            for ri, nm in enumerate(("s5_c_re", "s5_c_im")):
                src = I[nm][0].rearrange("(a g) c p -> (g c) a p", a=2)
                for dup in range(2):
                    sp.dma_start(CRI[:, ri, :, dup, :], src).then_inc(sem("s5_in"), 16)
            for c in range(2):
                weights(index[("hg", c)])
            sp.wait_ge(sem("s5_scanned"), NJ)
            sp.dma_start(wglu, I["s5_w_glu"][0].rearrange("(k p) c -> p k c", p=P)).then_inc(sem("glu_in"), 16)
            for t in range(2):
                sp.wait_ge(sem("lags_done"), t + 1)
                for h in range(2):
                    sp.dma_start(Sx[64 * h:64 * h + 64, 65:73, :],
                                 I["state_hgrn"][0][:, 2 * t + h].rearrange("n k v -> k n v")).then_inc(sem("hs_in"), 16)
            weights(index[("lora", 0)])
            sp.wait_ge(sem("hg_done"), 2)
            sp.wait_ge(sem("hg_stored"), 128)
            for lo, hi, nm in ((0, 32, "rw_w2"), (32, 64, "rw_a2"), (64, 128, "rw_g2")):
                sp.dma_start(Lw[lo:hi, :], I[nm][0]).then_inc(sem("lw_in"), 16)
            for j in range(4):
                weights(index[("rkv", j)])
                if j:
                    sp.wait_ge(sem("rw_stored"), 64 * j)
                for h in range(2):
                    sp.dma_start(SR[64 * h:64 * h + 64, :, :],
                                 I["state_rwkv"][0][:, 2 * j + h].rearrange("n v k -> v n k")).then_inc(sem("sr_in"), 16)
            weights(index[("merge", 0)])
            sp.wait_ge(sem("rw_done"), 4)
            for i in range(2):
                load_x(1, i)
            for i in range(2, XQ):
                sp.wait_ge(sem("x_turned"), XQ + i - 1)
                load_x(1, i)
            for i in range(index[("merge", 1)], len(chunks)):
                k, c, _ = chunks[i]
                weights(i)
                if k == "up":
                    n = c // 2
                    if n:
                        sp.wait_ge(sem("conv_turned"), n)
                    for b in range(2):
                        sp.dma_start(crw[0:16, 256 * b:256 * b + 256],
                                     I["state_ffn_conv"][0][:, :, FF * b + P * c:FF * b + P * (c + 2)]
                                     .rearrange("n r c -> (n r) c")).then_inc(sem("conv_in"), 16)

        @block.gpsimd
        def _(pool):
            done = [0]

            def step(ins):
                done[0] += 1
                ins.then_inc(sem("pool_step"), 1)
                pool.wait_ge(sem("pool_step"), done[0])

            pool.memset(rows[:, :, :], 0.0).then_inc(sem("rows_zeroed"), 1)
            step(pool.memset(ones[:], 1.0))
            for m in (ident, hones, m_lt, m_l0, idS):
                step(pool.memset(m[:], 0.0))
            step(pool.memset(m_ar[:], 1.0))
            step(pool.memset(m16[:], 1.0))
            step(pool.memset(hones[0:64, 0:64], 1.0))
            step(pool.memset(hones[64:128, 64:128], 1.0))
            step(pool.affine_select(out=ident[:], in_=ident[:], compare_op=ALU.not_equal, fill=1.0, base=0,
                                    pattern=[[-1, P]], channel_multiplier=1))
            step(pool.affine_select(out=m16[:], in_=m16[:], compare_op=ALU.is_ge, fill=0.0, base=0,
                                    pattern=[[-16, 8]], channel_multiplier=1))
            step(pool.affine_select(out=m16[:], in_=m16[:], compare_op=ALU.is_ge, fill=0.0, base=15,
                                    pattern=[[16, 8]], channel_multiplier=-1))
            for h in range(2):
                hp = slice(64 * h, 64 * h + 64)
                step(pool.affine_select(out=idS[hp], in_=idS[hp], compare_op=ALU.not_equal, fill=1.0, base=0,
                                        pattern=[[-1, RCH]], channel_multiplier=1))
                step(pool.affine_select(out=m_ar[hp, 0], in_=m_ar[hp, 0], compare_op=ALU.is_gt, fill=0.0, base=0,
                                        pattern=[[1, RCH]], channel_multiplier=-1))
                step(pool.affine_select(out=m_ar[hp, 1], in_=m_ar[hp, 1], compare_op=ALU.is_ge, fill=0.0, base=0,
                                        pattern=[[1, RCH]], channel_multiplier=-1))
                v = m_l0[hp, :].rearrange("p (b i) -> p b i", i=2)[:, :, 0]
                step(pool.affine_select(out=v, in_=v, compare_op=ALU.not_equal, fill=1.0, base=-1,
                                        pattern=[[-2, RCH // 2]], channel_multiplier=1))
                for l in range(LEVELS):
                    B = 1 << l
                    v = m_lt[hp, l, :].rearrange("p (b i r) -> p b i r", i=2, r=B)[:, :, 1, :]
                    step(pool.memset(v, 1.0))
                    step(pool.affine_select(out=v, in_=v, compare_op=ALU.is_ge, fill=0.0, base=0,
                                            pattern=[[-2 * B, RCH // (2 * B)], [0, B]], channel_multiplier=1))
                    step(pool.affine_select(out=v, in_=v, compare_op=ALU.is_ge, fill=0.0, base=B - 1,
                                            pattern=[[2 * B, RCH // (2 * B)], [0, B]], channel_multiplier=-1))
            step(pool.memset(resets[:], 1.0))
            step(pool.memset(resets[:, 0:TP].rearrange("p (c t) -> p c t", t=RCH)[:, :, 0], 0.0))
            pool.memset(resets[:, TP:T].rearrange("p (c t) -> p c t", t=LS)[:, :, 0], 0.0)\
                .then_inc(sem("consts_ready"), 1)
            pool.wait_ge(sem("ldt_in"), 16)
            pool.tensor_copy(rows[0:NJ, 1, :].rearrange("p (g c) -> p g c", g=2),
                             ldt[:].unsqueeze(2).to_broadcast([NJ, 2, 64])).then_inc(sem("ldt_spread"), 1)
            stored = {}

            def out(name, dst, src):
                stored[name] = stored.get(name, 0) + 16
                pool.dma_start(dst, src).then_inc(sem(name), 16)

            pool.wait_ge(sem("s5_rows"), 4)
            flat = s5out.rearrange("p a b c -> p (a b c)")
            out("s5_stored", O["s5_p"].rearrange("l n g p c -> (l n) (g p c)"), flat[0:1, :])
            out("s5_stored", O["s5_s"].rearrange("l n g p c -> (l n) (g p c)"), flat[1:NSEQ, :])
            for t in range(2):
                pool.wait_ge(sem("hg_states"), t + 1)
                for h in range(2):
                    hp = slice(64 * h, 64 * h + 64)
                    out("hg_stored", O["hg_p"][0, 0, 2 * t + h], Sx[hp, 64, :])
                    out("hg_stored", O["hg_s"][0][:, 2 * t + h].rearrange("n k v -> k n v"), Sx[hp, 73:81, :])
            for j in range(4):
                pool.wait_ge(sem("rw_rows"), 2 * (j + 1))
                for h in range(2):
                    hp = slice(64 * h, 64 * h + 64)
                    out("rw_stored", O["rw_p"][0, 0, 2 * j + h], SO[hp, 8, :])
                    out("rw_stored", O["rw_s"][0][:, 2 * j + h].rearrange("n v k -> v n k"), SO[hp, 0:8, :])
            pool.wait_ge(sem("sh_rows"), 4)
            out("sh_stored", O["sh_p"].rearrange("l n c -> (l n) c"), shrow2[0:1, :])
            out("sh_stored", O["sh_s"].rearrange("l n c -> (l n) c"), shrow2[1:NSEQ, :])
            for n in range(FT // 2):
                pool.wait_ge(sem("conv_rows"), n + 1)
                for b in range(2):
                    cs = slice(FF * b + 2 * P * n, FF * b + 2 * P * (n + 1))
                    src = cvr[:, n % 2, 256 * b:256 * b + 256]
                    out(f"conv_stored{n % 2}", O["cv_p"][0, 0][:, cs], src[0:2, :])
                    out(f"conv_stored{n % 2}", O["cv_s"][0][:, :, cs].rearrange("n r c -> (n r) c"), src[2:18, :])
            for i in range(XQ):
                pool.wait_ge(sem("y_rows"), 2 * (i + 1))
                dst = O["y_p"][0][P * i:P * (i + 1), :] if i < 8 else O["y_s"].rearrange("n t d -> (n t) d")
                out(f"y_stored{i % 2}", dst, yrow[0:xrows(i), i % 2, :])
            for name, n in stored.items():
                pool.wait_ge(sem(name), n)


        @block.tensor
        def _(pe):
            readers = {}
            last_read = {}

            def take(*banks):
                for b in banks:
                    if b in last_read:
                        pe.wait_ge(sem(last_read[b][0]), last_read[b][1])

            def give(name, *banks):
                readers[name] = readers.get(name, 0) + 1
                for b in banks:
                    last_read[b] = (name, readers[name])

            def mm(out, lhsT, rhs, start=True, stop=True):
                return nc.tensor.matmul(out, lhsT, rhs, start=start, stop=stop, skip_group_check=True)

            def turn(out, in_):
                n = in_.shape[0]
                return nc.tensor.transpose(out, in_, ident[0:n, 0:n])

            ring = [0]

            def gemm(w, c0, nk, rhs, reader):
                for g in range(G):
                    b = ring[0] % 6
                    ring[0] += 1
                    take(b)
                    for k in range(nk):
                        m = mm(pb[b][:, 0:GW], w[:, k, c0:c0 + P], rhs(k)[:, gcol(g)], k == 0, k == nk - 1)
                    m.then_inc(sem("gemm_done"), 1)
                    give(reader, b)

            def arrived(i):
                pe.wait_ge(sem(f"w_in{i % 2}"), loads[i])

            pe.wait_ge(sem("consts_ready"), 1)
            pe.wait_ge(sem("ldt_spread"), 1)
            pe.wait_ge(sem("small_in"), 16 * N_SMALL)
            for t in range(3):
                m = turn(pb[6][:, P * t:P * (t + 1)], rows[:, t, :])
            m.then_inc(sem("par_turned"), 1)
            give("par_ready", 6)
            for k in range(KT):
                m = turn(pb[7][:, NSEQ * k:NSEQ * (k + 1)], crow[0:NSEQ, P * k:P * (k + 1)])
            m.then_inc(sem("c_turned"), 1)
            give("cs_ready", 7)
            take(6)
            for k in range(RT):
                turn(pb[6][:, NS * k:NS * (k + 1)], shrow[0:NS, P * k:P * (k + 1)])
            for ri in range(2):
                for j in range(NJ):
                    m = turn(pb[6][:, 128 + NS * (NJ * ri + j):128 + NS * (NJ * ri + j + 1)],
                             s5row[0:NS, 256 * j + ri:256 * (j + 1):2])
            m.then_inc(sem("st_turned"), 1)
            give("st_ready", 6)

            def turn_x(base):
                for i in range(XQ):
                    n = xrows(i)
                    pe.wait_ge(sem(f"x_in{i % 2}"), 16 * (i // 2 + 1 + base * (5 - i % 2)))
                    for half in range(2):
                        b = 2 * (i % 3) + half
                        take(b)
                        for q in range(4):
                            k = 4 * half + q
                            m = turn(pb[b][:, P * q:P * q + n], xr[0:n, i % 2, P * k:P * (k + 1)])
                        if half == 0:
                            m.then_inc(sem("x_half"), 1)
                        else:
                            m.then_inc(sem("x_turned"), 1)
                        give("x_ev", b)

            turn_x(0)
            take(7)
            for c in range(12):
                arrived(c)
                w = wslot(c, 0, 8, 512)
                for q in range(4):
                    t = 4 * c + q
                    for k in range(KT):
                        m = mm(pb[7][:, NSEQ * t:NSEQ * (t + 1)], w[:, k, P * q:P * (q + 1)], csT[:, k, :],
                               k == 0, k == KT - 1)
                m.then_inc(sem("gemm_done"), 1)
            give("mod_ready", 7)

            def norm(n):
                take(0, 1, 2)
                for k in range(KT):
                    pe.wait_ge(sem("sq_ready"), KT * n + k + 1)
                    for g in range(G):
                        m = mm(pb[g][:, 0:GW], ones[:], (sq if n == 0 else sq2)[:, k % 2, gcol(g)], k == 0, k == KT - 1)
                    m.then_inc(sem("sq_used"), 1)
                give("rstd_ready", 0, 1, 2)

            norm(0)
            pe.wait_ge(sem("h_ready"), 1)
            h = lambda k: hT[:, k, :]
            i = index[("s5", 0)]
            arrived(i)
            for t in range(2):
                gemm(wslot(i, 0, 8, 256), P * t, 8, h, "z_ev")
            pe.wait_ge(sem("s5_bb"), 1)
            for q in range(4):
                b = 6 + q % 2
                take(b)
                for r in range(4):
                    m = turn(pb[b][:, P * r:P * (r + 1)], BB[:, q // 2, 4 * (q % 2) + r, :])
                m.then_inc(sem("bt_turned"), 1)
                give("bt_ev", b)
            take(6)
            pe.wait_ge(sem("s5_in"), 16 * 6)
            for ri in range(2):
                for a in range(2):
                    m = turn(pb[6][:, P * (2 * ri + a):P * (2 * ri + a + 1)],
                             CRI[:, ri, a, :, :].rearrange("p a b -> p (a b)"))
            m.then_inc(sem("ct_turned"), 1)
            give("ct_ev", 6)
            for c in range(2):
                i = index[("hg", c)]
                arrived(i)
                for q in range(4):
                    gemm(wslot(i, 0, 8, 512), P * q, 8, h, "z_ev")
            pe.wait_ge(sem("bt_ev"), 4)
            pe.wait_ge(sem("z_ev"), 2 * G)
            misc = [0]

            def misc_bank():
                misc[0] += 1
                take(6 + misc[0] % 2)
                return 6 + misc[0] % 2

            for j in range(NJ):
                for g in range(G):
                    for ri in range(2):
                        b = misc_bank()
                        mm(pb[b][:, 0:GW], BTl[:, ri, j, :], U5[:, j // 4, gcol(g)]).then_inc(sem("e_done"), 1)
                        give("e_ev", b)
                pe.wait_ge(sem("s5_scanned"), j + 1)
                for g in range(G):
                    b = misc_bank()
                    mm(pb[b][:, 0:GW], CTl[:, 0, j, :], e0[:, gcol(g)], True, False)
                    mm(pb[b][:, 0:GW], CTl[:, 1, j, :], e1[:, gcol(g)], False, True).then_inc(sem("y5_done"), 1)
                    give("y5_ev", b)
            for q in range(4):
                b = misc_bank()
                for r in range(4):
                    m = turn(pb[b][0:NSEQ, P * r:P * (r + 1)], ls5[:, q // 2, 4 * (q % 2) + r, :])
                m.then_inc(sem("s5_lturned"), 1)
                give("s5_rows", b)
            pe.wait_ge(sem("glu_in"), 16)
            pe.wait_ge(sem("gelu_ready"), 2)
            for m_ in range(2):
                for g in range(G):
                    b = misc_bank()
                    for k, x in enumerate((t0, t1)):
                        m = mm(pb[b][:, 0:GW], wglu[:, k, P * m_:P * (m_ + 1)], x[:, gcol(g)], k == 0, k == 1)
                    m.then_inc(sem("glu_done"), 1)
                    give("glu_ev", b)
            for t in range(2):
                for d in range(HC):
                    w, bs = HC - d, 3 * (d % 2)
                    pe.wait_ge(sem("prod_ready"), HC * t + d + 1)
                    take(bs, bs + 1, bs + 2)
                    src = (Hp0, Hp1)[d % 2].rearrange("p (c t) -> p c t", t=HC)
                    for q in range(3):
                        m = mm(pb[bs + q][:, 0:24 * w].rearrange("p (c t) -> p c t", t=w), hones[:],
                               src[:, 24 * q:24 * (q + 1), d:HC])
                    m.then_inc(sem("att_done"), 1)
                    give("att_ev", bs, bs + 1, bs + 2)
                pe.wait_ge(sem("hk_ready"), t + 1)

                def tokens(b):
                    k = 6 + b % 2
                    take(k)
                    turn(pb[k][:, 0:P], HK[:, P * b:P * (b + 1)])
                    turn(pb[k][:, P:2 * P], ZH[:, 2, t, P * b:P * (b + 1)]).then_inc(sem("tok_done"), 1)
                    give("tok_ev", k)

                tokens(0)
                for b in range(9):
                    if b < 8:
                        tokens(b + 1)
                    pe.wait_ge(sem("vblk_ready"), 9 * t + b + 1)
                    take(b % 2)
                    for hh in range(2):
                        m = mm(pb[b % 2][64 * hh:64 * hh + 64, :], tok[:, b % 2, 0, 64 * hh:64 * hh + 64],
                               Vblk[:, hh, :, :].rearrange("p a b -> p (a b)"))
                    m.then_inc(sem("u_done"), 1)
                    give("u_ev", b % 2)
                pe.wait_ge(sem("hg_states"), t + 1)
                take(3, 4, 5)
                qd = HD.rearrange("p (c t) -> p c t", t=HC)
                for c in range(HN):
                    s = c if c < 64 else c + 1
                    for hh in range(2):
                        hp = slice(64 * hh, 64 * hh + 64)
                        m = mm(pb[3 + c // 24][hp, HC * (c % 24):HC * (c % 24 + 1)], Sx[hp, s, :], qd[hp, c, :])
                m.then_inc(sem("oi_done"), 1)
                give("oi_ev", 3, 4, 5)
                pe.wait_ge(sem("hsq_ready"), t + 1)
                take(0, 1, 2)
                for q in range(3):
                    m = mm(pb[q][:, 0:384], hones[:], HK[:, 384 * q:384 * (q + 1)])
                m.then_inc(sem("hn_done"), 1)
                give("hn_ev", 0, 1, 2)
            i = index[("lora", 0)]
            arrived(i)
            gemm(wslot(i, 0, 8, 128), 0, 8, h, "z_ev")

            def heads(fn):
                for hh in range(2):
                    m = fn(slice(64 * hh, 64 * hh + 64))
                return m

            for j in range(4):
                i = index[("rkv", j)]
                arrived(i)
                for q in range(3):
                    gemm(wslot(i, 1024 * q, 8, 128), 0, 8, h, "z_ev")
                pe.wait_ge(sem("sr_in"), 32 * (j + 1))
                take(6)
                for n in range(NS):
                    m = heads(lambda hp: mm(pb[6][hp, 64 * n:64 * n + 64], SR[hp, n, :], idS[hp, :]))
                m.then_inc(sem("sin_done"), 1)
                give("sin_ev", 6)
                pe.wait_ge(sem("lora_ready"), 2)
                pe.wait_ge(sem("lw_in"), 48)
                take(0, 1, 2, 3, 4, 5)
                for g in range(G):
                    m = mm(pb[g][:, 0:GW], Lw[0:32, P * j:P * (j + 1)], Lx[0:32, gcol(g)])
                m.then_inc(sem("wl_done"), 1)
                give("wl_ev", 0, 1, 2)
                for g in range(G):
                    m = mm(pb[3 + g][:, 0:GW], Lw[32:64, P * j:P * (j + 1)], Lx[32:64, gcol(g)])
                m.then_inc(sem("al_done"), 1)
                give("al_ev", 3, 4, 5)
                pe.wait_ge(sem("ksq_ready"), j + 1)
                take(0, 1, 2)
                for g in range(G):
                    m = mm(pb[g][:, 0:GW], hones[:], Y[:, 2 + j, gcol(g)])
                m.then_inc(sem("kn_done"), 1)
                give("kn_ev", 0, 1, 2)
                pe.wait_ge(sem("rk_ready"), j + 1)
                take(3, 4, 5)
                for g in range(G):
                    m = mm(pb[3 + g][:, 0:GW], hones[:], Rc[:, gcol(g)])
                m.then_inc(sem("bn_done"), 1)
                give("bn_ev", 3, 4, 5)
                pe.wait_ge(sem("pads_ready"), j + 1)
                for bt in range(3):
                    for x, (b, src) in enumerate(((0, Vp), (1, Bp), (2, Kp))):
                        take(b)
                        for c in range(8):
                            m = heads(lambda hp: mm(pb[b][hp, 64 * c:64 * c + 64], src[hp, 8 * bt + c, :], idS[hp, :]))
                        m.then_inc(sem("tk_done"), 1)
                        give("tk_ev", b)
                    for half in range(2):
                        take(3 + half)
                        for q in range(4):
                            c = 8 * bt + 4 * half + q
                            m = heads(lambda hp: mm(pb[3 + half][hp, P * q:P * (q + 1)], Bp[hp, c, :],
                                                    ARp[hp, c, :, :].rearrange("p a b -> p (a b)")))
                        m.then_inc(sem("la_done"), 1)
                        give("la_ev", 3 + half)
                    for half in range(2):
                        take(5 + half)
                        for q in range(4):
                            c = 8 * bt + 4 * half + q
                            m = heads(lambda hp: mm(pb[5 + half][hp, P * q:P * (q + 1)], Kp[hp, c, :],
                                                    ARp[hp, c, :, :].rearrange("p a b -> p (a b)")))
                        m.then_inc(sem("ka_done"), 1)
                        give("ka_ev", 5 + half)
                    take(7)
                    for c in range(8):
                        m = heads(lambda hp: mm(pb[7][hp, 64 * c:64 * c + 64], ARp[hp, 8 * bt + c, 0, :],
                                                Bp[hp, 8 * bt + c, :]))
                    m.then_inc(sem("l_done"), 1)
                    give("l_ev", 7)
                    last = 5 if bt < 2 else 1
                    for l in range(1, last + 1):
                        n = lt_count(j, bt, l)
                        pe.wait_ge(sem("lt_ready"), n)
                        take(0)
                        for c in range(8):
                            m = heads(lambda hp: mm(pb[0][hp, 64 * c:64 * c + 64], LTm[hp, c, :], X[hp, c, :]))
                        m.then_inc(sem("yy_done"), 1)
                        give("yy_ev", 0)
                        pe.wait_ge(sem("yy_ev"), n)
                        take(1)
                        for c in range(8):
                            m = heads(lambda hp: mm(pb[1][hp, 64 * c:64 * c + 64], XT[hp, c, :], Yb[hp, c, :]))
                        m.then_inc(sem("zx_done"), 1)
                        give("zx_ev", 1)
                        take(2)
                        for c in range(8):
                            m = heads(lambda hp: mm(pb[2][hp, 64 * c:64 * c + 64], Yb[hp, c, :], XT[hp, c, :]))
                        m.then_inc(sem("zt_done"), 1)
                        give("zt_ev", 2)
                    pe.wait_ge(sem("zt_ev"), lt_count(j, bt, last))
                    pe.wait_ge(sem("tk_ev"), 3 * (3 * j + bt + 1))
                    pe.wait_ge(sem("ka_ev"), 2 * (3 * j + bt + 1))
                    pe.wait_ge(sem("la_ev"), 2 * (3 * j + bt + 1))
                    take(3, 4, 5, 7)
                    for c in range(8):
                        n = RN * j + 8 * bt + c
                        ci = 8 * bt + c
                        S0 = S2[:, ci % 2, :] if bt < 2 else Sin[:, c, :]
                        pe.wait_ge(sem("s_ready"), n + 1)
                        take(3)

                        def g_(hp):
                            mm(pb[3][hp, 0:64], ARp[hp, ci, 0, :], S0[hp, :], True, False)
                            return mm(pb[3][hp, 0:64], KA[hp, c, 0, :], Vt[hp, c, :], False, True)
                        heads(g_).then_inc(sem("g_done"), 1)
                        give("g_ev", 3)
                        pe.wait_ge(sem("g_ev"), n + 1)
                        take(4)
                        heads(lambda hp: mm(pb[4][hp, 0:64], XT[hp, c, :], Gb[hp, :])).then_inc(sem("ub_done"), 1)
                        give("ub_ev", 4)
                        pe.wait_ge(sem("ub_ev"), n + 1)
                        take(5)

                        def ds_(hp):
                            mm(pb[5][hp, 0:64], Bt[hp, c, :], Ub[hp, :], True, False)
                            return mm(pb[5][hp, 0:64], Kt_[hp, c, :], Vt[hp, c, :], False, True)
                        heads(ds_).then_inc(sem("ds_done"), 1)
                        give("ds_ev", 5)

                        def y_(hp):
                            o = pb[7][hp, 64 * c:64 * c + 64]
                            mm(o, S0[hp, :], ARp[hp, ci, 1, :], True, False)
                            mm(o, Ub[hp, :], LA[hp, c, 1, :], False, False)
                            return mm(o, Vt[hp, c, :], KA[hp, c, 1, :], False, True)
                        m = heads(y_)
                    m.then_inc(sem("ry_done"), 1)
                    give("ry_ev", 7)
                pe.wait_ge(sem("ry_ev"), 3 * (j + 1))
                take(0, 1, 2)
                for g in range(G):
                    m = mm(pb[g][:, 0:GW], hones[:], Y[:, 2 + j, gcol(g)])
                m.then_inc(sem("mn_done"), 1)
                give("mn_ev", 0, 1, 2)
                pe.wait_ge(sem("ds_ev"), RN * (j + 1))
                take(6, 7)
                for n in range(NS):
                    m = heads(lambda hp: mm(pb[6][hp, 64 * n:64 * n + 64], Sout[hp, n, :], idS[hp, :]))
                m.then_inc(sem("so_done"), 1)
                give("rw_rows", 6)
                heads(lambda hp: mm(pb[7][hp, 0:64], S2[hp, 0, :], idS[hp, :])).then_inc(sem("so_done"), 1)
                give("rw_rows", 7)
                pe.wait_ge(sem("ysq_ready"), j + 1)
                take(3, 4, 5)
                for g in range(G):
                    m = mm(pb[3 + g][:, 0:GW], hones[:], C2[:, gcol(g)])
                m.then_inc(sem("vr_done"), 1)
                give("vr_ev", 3, 4, 5)
                take(0, 1, 2)
                for g in range(G):
                    m = mm(pb[g][:, 0:GW], Lw[64:128, P * j:P * (j + 1)], Lx[64:128, gcol(g)])
                m.then_inc(sem("gl_done"), 1)
                give("gl_ev", 0, 1, 2)
            pe.wait_ge(sem("sho_ready"), RT)
            for b in range(4):
                take(b)
                for q in range(4 if b < 3 else 1):
                    m = turn(pb[b][0:NSEQ, P * q:P * (q + 1)], shO[:, 4 * b + q, :])
                m.then_inc(sem("sh_turned"), 1)
                give("sh_rows", b)
            turn_x(1)
            pair = 0
            for n in range(KT):
                i = index[("merge", n)]
                arrived(i)
                lifts = ((3072, 2, 0), (3328, 4, 2), (3840, 2, 6))
                for g in range(G):
                    for br in range(3):
                        b = 2 * (pair % 3)
                        pair += 1
                        take(b, b + 1)
                        w = wslot(i, 1024 * br, 8, P)
                        for k in range(KT):
                            mm(pb[b][:, 0:GW], w[:, k, :], hT[:, k, gcol(g)], k == 0, k == KT - 1)
                        off, nk, y0 = lifts[br]
                        w = wslot(i, off, nk, P)
                        for k in range(nk):
                            m = mm(pb[b + 1][:, 0:GW], w[:, k, :], Y[:, y0 + k, gcol(g)], k == 0, k == nk - 1)
                        m.then_inc(sem("gemm_done"), 1)
                        give("pair_ev", b, b + 1)
            pe.wait_ge(sem("mg_ready"), G * KT)
            for c in range(2):
                i = index[("out", c)]
                arrived(i)
                for q in range(4):
                    gemm(wslot(i, 0, 8, 512), P * q, 8, lambda k: MG[:, k, :], "res_ev")
            norm(1)
            pe.wait_ge(sem("h_ready"), 2)

            def last_rows(n):
                pe.wait_ge(sem("cob_ready"), n + 1)
                take(7)
                for q in range(4):
                    m = turn(pb[7][0:18, P * q:P * (q + 1)], cob[:, q, :])
                m.then_inc(sem("cob_turned"), 1)
                give("conv_rows", 7)

            for half, (m0, m1) in enumerate(HALVES):
                for mt_ in range(m0, m1, 2):
                    n = mt_ // 2
                    pe.wait_ge(sem("conv_in"), 32 * (n + 1))
                    take(6)
                    for q in range(4):
                        m = turn(pb[6][:, 16 * q:16 * q + 16], crw[0:16, P * q:P * (q + 1)])
                    m.then_inc(sem("conv_turned"), 1)
                    give("cst_ev", 6)
                    i = index[("up", mt_)]
                    arrived(i)
                    for q in range(2):
                        for s in range(2):
                            gemm(wslot(i, 2048 * s, 8, 256), P * q, 8, h, "u_in")
                    if n:
                        last_rows(n - 1)
                pe.wait_ge(sem("ff_ready"), m1)
                for c in range(4):
                    i = index[("down", (m0, c))]
                    arrived(i)
                    for q in range(2):
                        gemm(wslot(i, 0, m1 - m0, 256), P * q, m1 - m0, lambda k: FFh[:, k, :], "res_ev")
            last_rows(FT // 2 - 1)
            norm(2)
            pe.wait_ge(sem("h_ready"), 3)
            for i in range(XQ):
                n = xrows(i)
                for half in range(2):
                    b = 2 * (i % 3) + half
                    take(b)
                    for q in range(4):
                        k = 4 * half + q
                        m = turn(pb[b][0:n, P * q:P * (q + 1)], hT[:, k, P * i:P * i + n])
                    m.then_inc(sem("y_turned"), 1)
                    give("y_rows", b)

        @block.scalar
        def _(act):
            done = [0]

            def step(ins):
                done[0] += 1
                ins.then_inc(sem("act_step"), 1)
                act.wait_ge(sem("act_step"), done[0])

            def copy(out, in_):
                return nc.scalar.activation(out, in_, ACT.Copy)

            act.wait_ge(sem("c_turned"), 1)
            nc.scalar.activation(csT[:].rearrange("p a b -> p (a b)"), pb[7][:, 0:KT * NSEQ], ACT.Silu)\
                .then_inc(sem("cs_ready"), 1)

            def evac_x(base):
                for i in range(XQ):
                    n = xrows(i)
                    for half in range(2):
                        b = 2 * (i % 3) + half
                        act.wait_ge(sem("x_half" if half == 0 else "x_turned"), XQ * base + i + 1)
                        copy(xT[:, 4 * half:4 * half + 4, P * i:P * i + n],
                             pb[b][:, :].rearrange("p (q t) -> p q t", q=4)[:, :, 0:n]).then_inc(sem("x_ev"), 1)

            act.wait_ge(sem("par_ready"), 1)
            V = lambda k: s5v[:, k, :]
            step(nc.scalar.activation(V(0), par("s5_log_dt", 0, NJ), ACT.Exp))
            nc.scalar.copy(V(1), V(0)).then_inc(sem("dt_ready"), 1)
            act.wait_ge(sem("low_diff"), 1)
            nc.scalar.activation(low[:, 1], low[:, 0], ACT.Exp).then_inc(sem("low_exp"), 1)
            act.wait_ge(sem("angles_ready"), 1)
            nc.scalar.activation(V(5), V(2), ACT.Exp).then_inc(sem("s5_fn"), 1)
            nc.scalar.activation(V(6), V(3), ACT.Sin).then_inc(sem("s5_fn"), 1)
            nc.scalar.activation(V(7), V(4), ACT.Sin).then_inc(sem("s5_fn"), 1)
            evac_x(0)

            def root(buf, n, scale=1.0):
                act.wait_ge(sem("var_ready"), n)
                step(nc.scalar.activation(buf, buf, ACT.Ln, scale=scale))
                nc.scalar.activation(buf, buf, ACT.Exp, scale=-0.5).then_inc(sem("rs_ready"), 1)

            def norm(n):
                buf = sq if n == 0 else sq2
                for k in range(KT):
                    i = KT * n + k
                    if i >= 2:
                        act.wait_ge(sem("sq_used"), i - 1)
                    nc.scalar.activation(buf[:, k % 2, :], xT[:, k, :], ACT.Square).then_inc(sem("sq_ready"), 1)
                root(rstd if n == 0 else rstd2, (1, 12, 13)[n])

            act.wait_ge(sem("x_ev"), 2 * XQ)
            norm(0)
            ring = [0]
            z_n = [0]

            def z_evac(dst_of, fn, count):
                for g in range(G):
                    b = ring[0] % 6
                    ring[0] += 1
                    act.wait_ge(sem("gemm_done"), count + g + 1)
                    for ins in dst_of(g, pb[b], fn):
                        m = ins
                    m.then_inc(sem("z_ev"), 1)

            def compact(dst):
                def go(g, bank, fn):
                    yield nc.scalar.activation(dst[:, gcol(g)], bank[:, 0:GW], fn)
                return go

            def split(prompt, decode):
                def go(g, bank, fn):
                    n = min(GW, TP - g * GW)
                    yield nc.scalar.activation(prompt[:, g * GW:g * GW + n], bank[:, 0:n], fn)
                    if n < GW:
                        yield nc.scalar.activation(decode, bank[:, n:GW].rearrange("p (a b) -> p a b", b=LS), fn)
                return go

            base = signals[index[("s5", 0)]]
            act.wait_ge(sem("h_ready"), 1)
            for t in range(2):
                z_evac(compact(U5[:, t, :]), ACT.Copy, base + G * t)
            act.wait_ge(sem("zh_padded"), 1)
            base = signals[index[("hg", 0)]]
            for q, fn in enumerate((ACT.Silu, ACT.Sigmoid, ACT.Copy, ACT.Sigmoid)):
                for t in range(2):
                    z = ZH[:, q, t, :]
                    z_evac(split(z[:, 0:TP], z[:, TP:HT].rearrange("p (c t) -> p c t", t=HC)[:, :, 0:LS]), fn,
                           base + G * (2 * q + t))
            for j in range(NJ):
                for g in range(G):
                    for ri in range(2):
                        act.wait_ge(sem("e_done"), 6 * j + 2 * g + ri + 1)
                        if j == 0:
                            act.wait_ge(sem("bt_ev"), 4)
                        copy((e0, e1)[ri][:, gcol(g)], pb[6 + (9 * j + 2 * g + ri + 1) % 2][:, 0:GW])\
                            .then_inc(sem("e_ev"), 1)
            act.wait_ge(sem("y5_ev"), G * NJ)
            for a in range(2):
                nc.scalar.activation((t0, t1)[a], Y[:, a, :], ACT.Gelu_apprx_tanh).then_inc(sem("gelu_ready"), 1)
            for m_ in range(2):
                for g in range(G):
                    n = G * m_ + g
                    act.wait_ge(sem("glu_done"), n + 1)
                    nc.scalar.activation((e0, e1)[m_][:, gcol(g)], pb[6 + (9 * NJ + 4 + n + 1) % 2][:, 0:GW], ACT.Sigmoid,
                                         bias=par("s5_b_glu", m_)).then_inc(sem("glu_ev"), 1)
            for t in range(2):
                for b in range(9):
                    act.wait_ge(sem("tok_done"), 9 * t + b + 1)
                    if b >= 2:
                        act.wait_ge(sem("u_done"), 9 * t + b - 1)
                    copy(tok[:, b % 2, :, :].rearrange("p a b -> p (a b)"), pb[6 + b % 2][:, 0:2 * P])\
                        .then_inc(sem("tok_ev"), 1)
                act.wait_ge(sem("oi_ev"), t + 1)
                nc.scalar.activation(HK, Ho, ACT.Square).then_inc(sem("hsq_ready"), 1)
                root(Hn, 2 + t)
            act.wait_ge(sem("hg_done"), 2)
            act.wait_ge(sem("hg_stored"), 128)

            def zplace(z):
                return split(z[:, 1:1 + TP], z[:, 1 + TP:1065].rearrange("p (n t) -> p n t", t=LS + 1)[:, :, 1:])

            z_evac(zplace(Z[0]), ACT.Copy, signals[index[("lora", 0)]])
            act.wait_ge(sem("lora_mixed"), 1)
            nc.scalar.activation(Lx[0:32, :], Lx[0:32, :], ACT.Tanh).then_inc(sem("lora_ready"), 1)
            nc.scalar.activation(Lx[64:128, :], Lx[64:128, :], ACT.Sigmoid).then_inc(sem("lora_ready"), 1)
            bank3 = lambda b: ps[:, b:b + 3, 0:GW]
            three = lambda x: x[:, 0:T].rearrange("p (g t) -> p g t", g=G)
            T1, T2, T3 = (z[:, 0:T] for z in Z[1:])
            for j in range(4):
                if j:
                    act.wait_ge(sem("rw_done"), j)
                for q in range(3):
                    z_evac(zplace(Z[1 + q]), ACT.Copy, signals[index[("rkv", j)]] + G * q)
                act.wait_ge(sem("sin_done"), j + 1)
                copy(Sin[:].rearrange("p a b -> p (a b)"), pb[6][:, :]).then_inc(sem("sin_ev"), 1)
                act.wait_ge(sem("mixed"), 3 * (j + 1))
                act.wait_ge(sem("wl_done"), j + 1)
                nc.scalar.activation(three(T1), bank3(0), ACT.Sigmoid, bias=par("rw_w0", j)).then_inc(sem("wl_ev"), 1)
                act.wait_ge(sem("al_done"), j + 1)
                nc.scalar.activation(three(T2), bank3(3), ACT.Sigmoid, bias=par("rw_a0", j)).then_inc(sem("al_ev"), 1)
                act.wait_ge(sem("kraw_ready"), j + 1)
                nc.scalar.activation(Y[:, 2 + j, :], T3, ACT.Square).then_inc(sem("ksq_ready"), 1)
                act.wait_ge(sem("cums_ready"), j + 1)
                nc.scalar.activation(C2, C1, ACT.Exp, scale=-C_DECAY).then_inc(sem("decays"), 1)
                act.wait_ge(sem("decays"), 3 * j + 1)
                nc.scalar.activation(C1, C1, ACT.Exp, scale=C_DECAY).then_inc(sem("decays"), 1)
                nc.scalar.activation(T1, T1, ACT.Exp, scale=-C_DECAY).then_inc(sem("decays"), 1)
                root(Y[:, 2 + j, :], 4 + 2 * j, 2.0 ** 30)
                for bt in range(3):
                    for x, dst in enumerate((Vt, Bt, Kt_)):
                        act.wait_ge(sem("tk_done"), 3 * (3 * j + bt) + x + 1)
                        copy(dst[:].rearrange("p a b -> p (a b)"), pb[x][:, :]).then_inc(sem("tk_ev"), 1)
                    for l in range(1, (5 if bt < 2 else 1) + 1):
                        act.wait_ge(sem("yy_done"), lt_count(j, bt, l))
                        copy(Yb[:].rearrange("p a b -> p (a b)"), pb[0][:, :]).then_inc(sem("yy_ev"), 1)
                act.wait_ge(sem("centred"), j + 1)
                nc.scalar.activation(C2, C1, ACT.Square).then_inc(sem("ysq_ready"), 1)
                root(Kc, 5 + 2 * j)
                act.wait_ge(sem("rw_done"), j + 1)
                act.wait_ge(sem("so_done"), 2 * (j + 1))
                copy(SO[:, 0:8, :].rearrange("p a b -> p (a b)"), pb[6][:, :]).then_inc(sem("rw_rows"), 1)
                copy(SO[:, 8, :], pb[7][:, 0:64]).then_inc(sem("rw_rows"), 1)
            for b in range(4):
                act.wait_ge(sem("sh_turned"), b + 1)
                n = 512 if b < 3 else P
                copy(shrow2[0:NSEQ, 512 * b:512 * b + n], pb[b][0:NSEQ, 0:n]).then_inc(sem("sh_rows"), 1)
            evac_x(1)
            for p in range(3 * G * KT):
                act.wait_ge(sem("gemm_done"), signals[index[("merge", 0)]] + p + 1)
                if p >= 3:
                    act.wait_ge(sem("pair_ev"), p - 2)
                nc.scalar.activation(sig[:, p % 3, :], pb[2 * (p % 3)][:, 0:GW], ACT.Sigmoid).then_inc(sem("sig_ready"), 1)
            act.wait_ge(sem("res_ev"), 8 * G)
            norm(1)

            def rows_out(n):
                act.wait_ge(sem("cob_turned"), n + 1)
                if n >= 2:
                    act.wait_ge(sem(f"conv_stored{n % 2}"), 64 * (n // 2))
                copy(cvr[0:18, n % 2, :], pb[7][0:18, :]).then_inc(sem("conv_rows"), 1)

            act.wait_ge(sem("u_zeroed"), 1)
            ring[0] = RING_UP
            for mt_ in range(0, FT, 2):
                n = mt_ // 2
                half = 0 if mt_ < HALVES[0][1] else 1
                if mt_ == HALVES[1][0]:
                    ring[0] += 8 * G
                act.wait_ge(sem("conv_turned"), n + 1)
                for q in range(4):
                    src = (q % 2) * 2 + q // 2
                    if n:
                        act.wait_ge(sem("u_used"), 4 * n + q - 3)
                    u = Uab[q]
                    dec = u[:, 2 + TP:UL].rearrange("p (n t) -> p n t", t=LS + 2)
                    m = copy(dec[:, :, 0:2], pb[6][:, 16 * src:16 * src + 16].rearrange("p (n r) -> p n r", r=2))
                    if q == 3:
                        m.then_inc(sem("cst_ev"), 1)
                    z0 = signals[index[("up", mt_)]] + G * q
                    for g in range(G):
                        b = ring[0] % 6
                        ring[0] += 1
                        act.wait_ge(sem("gemm_done"), z0 + g + 1)
                        k = min(GW, TP - g * GW)
                        m = copy(u[:, 2 + g * GW:2 + g * GW + k], pb[b][:, 0:k])
                        if k < GW:
                            m = copy(dec[:, :, 2:], pb[b][:, k:GW].rearrange("p (n t) -> p n t", t=LS))
                        m.then_inc(sem("u_in"), 1)
                    if q % 2:
                        p = 2 * n + q // 2
                        if p == HALVES[1][0]:
                            act.wait_ge(sem("res_ev"), 16 * G)
                        act.wait_ge(sem("conv_a"), p + 1)
                        nc.scalar.activation(FFh[:, p - (0 if p < HALVES[0][1] else HALVES[1][0]), :], Cab[p % 2],
                                             ACT.Gelu_apprx_tanh).then_inc(sem("gelu_done"), 1)
                act.wait_ge(sem("u_in"), G * 4 * (n + 1))
                if n:
                    rows_out(n - 1)
                    act.wait_ge(sem("cob_turned"), n)
                for q in range(4):
                    src = (q % 2) * 2 + q // 2
                    u = Uab[q]
                    dec = u[:, 2 + TP:UL].rearrange("p (n t) -> p n t", t=LS + 2)
                    copy(cob[:, src, 0:2], u[:, TP:TP + 2])
                    m = copy(cob[:, src, 2:18].rearrange("p (n r) -> p n r", r=2), dec[:, :, 4:6])
                m.then_inc(sem("cob_ready"), 1)
                act.wait_ge(sem("cob_ready"), n + 1)
            rows_out(FT // 2 - 1)
            act.wait_ge(sem("res_ev"), 24 * G)
            norm(2)
            for i in range(XQ):
                n = xrows(i)
                if i >= 2:
                    act.wait_ge(sem(f"y_stored{i % 2}"), 16 * (i // 2))
                for half in range(2):
                    act.wait_ge(sem("y_turned"), 2 * i + half + 1)
                    copy(yrow[0:n, i % 2, 512 * half:512 * half + 512], pb[2 * (i % 3) + half][0:n, :])\
                        .then_inc(sem("y_rows"), 1)

        @block.vector
        def _(dve):
            counts = {}
            v = nc.vector

            def step(ins, name="dve_step"):
                counts[name] = counts.get(name, 0) + 1
                ins.then_inc(sem(name), 1)

                dve.wait_ge(sem(name), counts[name])

            bank3 = lambda b: ps[:, b:b + 3, 0:GW]
            three = lambda x: x[:, 0:T].rearrange("p (g t) -> p g t", g=G)
            dec4 = lambda x: x.rearrange("p (n t) -> p n t", t=LS)

            def tt(out, a, b, op):
                return v.tensor_tensor(out, a, b, op)

            def stt(out, a, s, b, op0, op1):
                return v.scalar_tensor_tensor(out=out, in0=a, scalar=s, in1=b, op0=op0, op1=op1)

            dve.wait_ge(sem("par_turned"), 1)
            step(v.tensor_copy(PAR[:].rearrange("p a b -> p (a b)"), pb[6][:, 0:384]), "par_ready")
            dve.wait_ge(sem("st_turned"), 1)
            step(v.tensor_copy(shT[:].rearrange("p a b -> p (a b)"), pb[6][:, 0:RT * NS]))
            step(v.tensor_copy(st5[:].rearrange("p a b c -> p (a b c)"), pb[6][:, 128:256]), "st_ready")
            V = lambda k: s5v[:, k, :]
            lr, li = par("s5_lambda_re", 0, NJ), par("s5_lambda_im", 0, NJ)
            dve.wait_ge(sem("dt_ready"), 1)
            step(tt(V(8), li, V(0), MUL))
            step(v.tensor_scalar(V(9), V(8), math.pi / 2, None, ADD))
            for src, dst, tmp in ((8, 3, 10), (9, 4, 11)):
                step(v.tensor_scalar(V(tmp), V(src), 1 / (2 * math.pi), ROUND, MUL, ADD))
                step(v.tensor_scalar(V(tmp), V(tmp), ROUND, None, SUB))
                step(stt(V(12), V(tmp), -TWO_PI_HI, V(src), MUL, ADD))
                step(stt(V(12), V(tmp), -TWO_PI_LO, V(12), MUL, ADD))
                step(v.tensor_scalar(V(dst), V(12), PI_SAFE, -PI_SAFE, ALU.min, MAX))
            step(tt(V(2), lr, V(0), MUL), "angles_ready")
            lb = par("hg_lb", 0, 2)
            step(tt(low[:, 0], lb, lb, SUB), "low_diff")
            dve.wait_ge(sem("low_exp"), 1)
            step(v.reciprocal(low[:, 2], low[:, 1]))
            step(tt(low[:, 2], low[:, 1], low[:, 2], MUL))
            step(tt(low[:, 0], low[:, 2], low[:, 2], SUB))
            step(v.tensor_scalar(low[:, 3], low[:, 0], -1.0, 1.0, MUL, ADD))
            dve.wait_ge(sem("gemm_done"), 12)
            b_ada = par("b_ada", 0, 48).unsqueeze(2).to_broadcast([P, 48, NSEQ])
            step(tt(MOD[:], pb[7][:, 0:48 * NSEQ].rearrange("p (a b) -> p a b", b=NSEQ), b_ada, ADD), "mod_ready")
            for n, g in ((0, "g_mix"), (1, "g_ffn")):
                gb = par(g, 0, KT).unsqueeze(2).to_broadcast([P, KT, NSEQ])
                step(stt(GSC[:, n], MOD[:, 24 * n + 8:24 * n + 16, :], 1.0, gb, ADD, MUL))

            def root(n):
                step(v.memset(flag[:], 0.0), "var_ready")
                dve.wait_ge(sem("rs_ready"), n)

            def norm(n):
                rs, hn_ = (rstd, hn) if n == 0 else (rstd2, hn2)
                dve.wait_ge(sem("sq_used"), KT * (n + 1))
                step(v.tensor_scalar(three(rs), bank3(0), 1.0 / D, RMS_EPS, MUL, ADD), "rstd_ready")
                root((1, 12, 13)[n])
                for k in range(KT):
                    if n == 2:
                        step(stt(hT[:, k, :], xT[:, k, :], par("final_g", k), rs, MUL, MUL))
                        continue
                    step(tt(hn_, xT[:, k, :], rs, MUL))
                    A, B = GSC[:, n, k, :], MOD[:, 24 * n + k, :]
                    step(v.tensor_scalar(hT[:, k, 0:TP], hn_[:, 0:TP], A[:, 0:1], B[:, 0:1], MUL, ADD))
                    d = dec4(hn_[:, TP:T])
                    step(tt(d, d, A[:, 1:].unsqueeze(2).to_broadcast([P, NS, LS]), MUL))
                    step(tt(dec4(hT[:, k, TP:T]), d, B[:, 1:].unsqueeze(2).to_broadcast([P, NS, LS]), ADD))
                step(v.tensor_copy(flag[:], m16[:, 0:1]), "h_ready")

            norm(0)
            dve.wait_ge(sem("h_ready"), 1)
            for q in range(4):
                for t in range(2):
                    z = ZH[:, q, t, TP:HT].rearrange("p (c t) -> p c t", t=HC)[:, :, LS:]
                    step(v.memset(z, 1.0 if q == 1 else 0.0))
            step(v.memset(flag[:], 1.0), "zh_padded")
            dve.wait_ge(sem("s5_fn"), 3)
            mag, sn, cs = V(5), V(6), V(7)
            step(tt(V(8), mag, cs, MUL))
            step(tt(V(9), mag, sn, MUL))
            step(tt(V(10), lr, lr, MUL))
            step(tt(V(11), li, li, MUL))
            step(tt(V(10), V(10), V(11), ADD))
            step(v.reciprocal(V(10), V(10)))
            step(v.tensor_scalar(V(11), V(8), 1.0, None, SUB))
            step(tt(V(12), V(11), lr, MUL))
            step(tt(V(13), V(9), li, MUL))
            step(tt(V(12), V(12), V(13), ADD))
            step(tt(V(12), V(12), V(10), MUL))
            step(tt(V(13), V(9), lr, MUL))
            step(tt(V(14), V(11), li, MUL))
            step(tt(V(13), V(13), V(14), SUB))
            step(tt(V(13), V(13), V(10), MUL))
            step(v.memset(BB[:].rearrange("p a b c -> p (a b c)"), 0.0))
            step(v.memset(CTl[:].rearrange("p a b c -> p (a b c)"), 0.0))
            dve.wait_ge(sem("s5_in"), 96)
            zr = V(12).unsqueeze(2).to_broadcast([P, NJ, 16])
            zi = V(13).unsqueeze(2).to_broadcast([P, NJ, 16])
            CB = K_tmp
            step(tt(BBt[:, 0], BRI[:, 0], zr, MUL))
            step(tt(BBt[:, 1], BRI[:, 1], zi, MUL))
            step(tt(CB[:, 0], BBt[:, 0], BBt[:, 1], SUB))
            step(tt(BBt[:, 0], BRI[:, 1], zr, MUL))
            step(tt(BBt[:, 1], BRI[:, 0], zi, MUL))
            step(tt(CB[:, 1], BBt[:, 0], BBt[:, 1], ADD))
            for b in range(4):
                for gi in range(2):
                    hp, cols = slice(64 * gi, 64 * gi + 64), slice(16 * (2 * b + gi), 16 * (2 * b + gi + 1))
                    for ri in range(2):
                        step(v.tensor_copy(BB[hp, ri, b::4, cols], CB[hp, ri, b::4, :]))
            step(v.memset(flag[:], 1.0), "s5_bb")
            step(v.tensor_copy(wpw[:, 0, 0], cs))
            step(v.tensor_copy(wpw[:, 0, 1], sn))
            for l in range(1, 10):
                c, s = wpw[:, l - 1, 0], wpw[:, l - 1, 1]
                step(tt(V(14), s, s, MUL))
                step(tt(V(15), c, c, MUL))
                step(tt(wpw[:, l, 0], V(15), V(14), SUB))
                step(stt(wpw[:, l, 1], c, 2.0, s, MUL, MUL))
            ar = V(8).unsqueeze(2).to_broadcast([P, NJ, NS])
            ai = V(9).unsqueeze(2).to_broadcast([P, NJ, NS])
            step(tt(inj[:, 0], st5[:, 0], ar, MUL))
            step(tt(inj_t[:], st5[:, 1], ai, MUL))
            step(tt(inj[:, 0], inj[:, 0], inj_t[:], SUB))
            step(tt(inj[:, 1], st5[:, 1], ar, MUL))
            step(tt(inj_t[:], st5[:, 0], ai, MUL))
            step(tt(inj[:, 1], inj[:, 1], inj_t[:], ADD))
            for q in range(4):
                dve.wait_ge(sem("bt_turned"), q + 1)
                step(v.tensor_copy(BTl[:, q // 2, 4 * (q % 2):4 * (q % 2) + 4, :].rearrange("p a b -> p (a b)"),
                                   pb[6 + q % 2][:, :]), "bt_ev")
            dve.wait_ge(sem("ct_turned"), 1)
            cps = pb[6].rearrange("p (r a c) -> p r a c", r=2, a=2)
            for b in range(4):
                for gi in range(2):
                    hp, cols = slice(64 * gi, 64 * gi + 64), slice(16 * (2 * b + gi), 16 * (2 * b + gi + 1))
                    step(v.tensor_copy(CTl[hp, 0, b::4, cols], cps[hp, 0, :, cols]))
                    step(v.tensor_scalar(CTl[hp, 1, b::4, cols], cps[hp, 1, :, cols], -1.0, None, MUL))
            step(v.memset(flag[:], 1.0), "ct_ev")
            dve.wait_ge(sem("z_ev"), 2 * G)
            for a in range(2):
                step(v.tensor_scalar(Y[:, a, :], U5[:, a, :], par("s5_d", a), None, MUL))
            for j in range(NJ):
                col = lambda x: x[:, j:j + 1]
                step(v.memset(tc[:, 0:1], 1.0))
                step(v.memset(ts[:, 0:1], 0.0))
                for l in range(10):
                    n = 1 << l
                    wr, wi = wpw[:, l, 0, j:j + 1], wpw[:, l, 1, j:j + 1]
                    step(v.tensor_scalar(tc[:, n:2 * n], ts[:, 0:n], wi, None, MUL))
                    step(v.tensor_scalar(ts[:, n:2 * n], tc[:, 0:n], wi, None, MUL))
                    step(stt(tc[:, n:2 * n], tc[:, 0:n], wr, tc[:, n:2 * n], MUL, SUB))
                    step(stt(ts[:, n:2 * n], ts[:, 0:n], wr, ts[:, n:2 * n], MUL, ADD))
                for x in (tc, ts):
                    step(v.tensor_copy(dec4(x[:, TP:T]), x[:, 0:LS].unsqueeze(1).to_broadcast([P, NS, LS])))
                step(v.memset(Mg, 0.0))
                step(v.tensor_scalar(Mg, Mg, col(mag), None, ADD))
                step(v.memset(dec4(Mg[:, TP:T])[:, :, 0], 0.0))
                dve.wait_ge(sem("e_ev"), 6 * (j + 1))
                for ri, e in enumerate((e0, e1)):
                    f = dec4(e[:, TP:T])[:, :, 0]
                    step(tt(f, f, inj[:, ri, j, :], ADD))
                step(tt(t0, e0, tc, MUL))
                step(tt(t1, e1, ts, MUL))
                step(tt(t0, t0, t1, ADD))
                step(tt(t1, e1, tc, MUL))
                step(tt(e0, e0, ts, MUL))
                step(tt(t1, t1, e0, SUB))
                step(v.tensor_tensor_scan(t0, Mg, t0, 0.0, MUL, ADD))
                step(v.tensor_tensor_scan(t1, Mg, t1, 0.0, MUL, ADD))
                step(tt(e0, t0, tc, MUL))
                step(tt(e1, t1, ts, MUL))
                step(tt(e0, e0, e1, SUB))
                step(tt(e1, t1, tc, MUL))
                step(tt(t0, t0, ts, MUL))
                step(tt(e1, e1, t0, ADD))
                for ri, e in enumerate((e0, e1)):
                    step(v.tensor_copy(ls5[:, ri, j, 0:1], e[:, TP - 1:TP]))
                    step(v.tensor_copy(ls5[:, ri, j, 1:], dec4(e[:, TP:T])[:, :, LS - 1]))
                step(v.memset(flag[:], 1.0), "s5_scanned")
                for g in range(G):
                    dve.wait_ge(sem("y5_done"), G * j + g + 1)
                    y = Y[:, j // 4, gcol(g)]
                    step(tt(y, pb[6 + (9 * j + 6 + g + 1) % 2][:, 0:GW], y, ADD), "y5_ev")
            for q in range(4):
                dve.wait_ge(sem("s5_lturned"), q + 1)
                src = pb[6 + (9 * NJ + q + 1) % 2][0:NSEQ, :].rearrange("p (j c) -> p j c", c=P)
                step(v.tensor_copy(s5out[0:NSEQ, 4 * (q % 2):4 * (q % 2) + 4, :, q // 2], src), "s5_rows")
            dve.wait_ge(sem("glu_ev"), 2 * G)
            step(tt(Y[:, 0, :], t0, e0, MUL))
            step(tt(Y[:, 1, :], t1, e1, MUL))
            dve.wait_ge(sem("s5_stored"), 32)
            dve.wait_ge(sem("z_ev"), 10 * G)
            cv = lambda x: x.rearrange("p (c t) -> p c t", t=HC)
            for t in range(2):
                if t:
                    dve.wait_ge(sem("hg_stored"), 64)
                q_, f_, v_, og = (ZH[:, i, t, :] for i in range(4))
                step(v.tensor_scalar(f_, f_, low[:, 3, t:t + 1], low[:, 0, t:t + 1], MUL, ADD))
                step(v.tensor_scalar(K0, f_, -1.0, 1.0, MUL, ADD))
                step(v.tensor_scalar(f_, f_, 1e-30, None, MAX))
                step(v.tensor_copy(Ht0, f_))
                step(v.memset(Ht1, 0.0))
                step(v.tensor_copy(cv(Ht1)[:, :, 0], cv(f_)[:, :, 0]))
                step(v.memset(cv(Ht0)[:, :, 0], 0.0))
                step(v.tensor_tensor_scan(HD, Ht0, Ht1, 0.0, MUL, ADD))
                for d in range(HC):
                    w = HC - d
                    kd = (K0, K1)[d % 2]
                    if d:
                        step(tt(cv(kd)[:, :, d:], cv((K1, K0)[d % 2])[:, :, d - 1:HC - 1], cv(f_)[:, :, d:], MUL))
                    step(v.tensor_copy(cv(HK)[:, :, HC - 1 - d], cv(kd)[:, :, HC - 1]))
                    if d >= 2:
                        dve.wait_ge(sem("att_done"), HC * t + d - 1)
                    step(tt(cv((Hp0, Hp1)[d % 2])[:, :, d:], cv(kd)[:, :, d:], cv(q_)[:, :, d:], MUL), "prod_ready")
                    if d:
                        lag_out(v, dve, step, tt, cv, t, d - 1, v_)
                lag_out(v, dve, step, tt, cv, t, HC - 1, v_)
                step(v.tensor_copy(chunk_decay[:], cv(HD)[:, :, HC - 1]))
                step(tt(HD, HD, q_, MUL))
                step(v.memset(Sx[:, 0, :], 0.0), "lags_done")
                step(v.memset(flag[:], 1.0), "hk_ready")
                dve.wait_ge(sem("hs_in"), 32 * (t + 1))
                mb = m16[:, :].unsqueeze(2).to_broadcast([P, 8, 64])
                for b in range(9):
                    dve.wait_ge(sem("tok_ev"), 9 * t + b + 1)
                    if 9 * t + b:
                        dve.wait_ge(sem("u_done"), 9 * t + b)
                    for hh in range(2):
                        vt = tok[:, b % 2, 1, 64 * hh:64 * hh + 64].unsqueeze(1).to_broadcast([P, 8, 64])
                        step(tt(Vblk[:, hh], vt, mb, MUL), "vb" if hh == 0 else "vblk_ready")
                    if b:
                        state_out(v, dve, step, stt, t, b - 1)
                state_out(v, dve, step, stt, t, 8)
                step(v.memset(flag[:], 1.0), "hg_states")
                dve.wait_ge(sem("oi_done"), t + 1)
                o3 = Ho.rearrange("p (g c) -> p g c", g=3)
                step(tt(o3, ps[:, 3:6, 0:384], o3, ADD), "oi_ev")
                dve.wait_ge(sem("hn_done"), t + 1)
                r3 = Hn.rearrange("p (g c) -> p g c", g=3)
                step(v.tensor_scalar(r3, ps[:, 0:3, 0:384], 1.0 / 64, RMS_EPS, MUL, ADD), "hn_ev")
                root(2 + t)
                step(stt(Ho, Ho, par("hg_norm", t), Hn, MUL, MUL))
                y = Y[:, 6 + t, :]
                step(tt(y[:, 0:TP], Ho[:, 0:TP], og[:, 0:TP], MUL))
                step(tt(dec4(y[:, TP:T]), cv(Ho)[:, 64:, 0:LS], cv(og)[:, 64:, 0:LS], MUL), "hg_done")
            dve.wait_ge(sem("hg_stored"), 128)
            zcur = lambda z: (z[:, 1:1 + TP], z[:, 1 + TP:1065].rearrange("p (n t) -> p n t", t=LS + 1)[:, :, 1:])
            zprev = lambda z: (z[:, 0:TP], z[:, 1 + TP:1065].rearrange("p (n t) -> p n t", t=LS + 1)[:, :, 0:LS])
            pads = lambda x: (x[:, 0:16, :], x[:, 16:RN, 0:LS])
            flat = lambda x: (x[:, 0:TP], dec4(x[:, TP:T]))
            chunked = lambda x: (x[:, 0:TP].rearrange("p (c t) -> p c t", t=RCH), dec4(x[:, TP:T]))

            def mix(z, tile, tmp, dst, name):
                step(v.memset(z[:, 0:1], 0.0))
                sc = z[:, 1 + TP:1065].rearrange("p (n t) -> p n t", t=LS + 1)
                step(v.tensor_copy(sc[:, :, 0], shT[:, tile, :]))
                for o, a, b in zip(flat(tmp), zprev(z), zcur(z)):
                    step(tt(o, a, b, SUB))
                step(v.tensor_copy(shO[:, tile, 0:1], z[:, TP:TP + 1]))
                step(v.tensor_copy(shO[:, tile, 1:], sc[:, :, LS]), "sho_ready")
                for i, (o, a, b) in enumerate(zip(dst, flat(tmp), zcur(z))):
                    if len(o.shape) == 3 and len(a.shape) == 2:
                        a, b = (x.rearrange("p (c t) -> p c t", t=RCH) for x in (a, b))
                    step(stt(o, a, par("rw_mu", tile), b, MUL, ADD), name if i else "dve_step")

            dve.wait_ge(sem("z_ev"), 11 * G)
            mix(Z[0], 12, Kc, flat(Lx), "lora_mixed")
            for x in (ARp, Bp, Kp, Vp):
                n = 0 if len(x.shape) == 3 else 1
                dst = x[:, 16:RN].rearrange("p a b c -> p (a b c)") if n else x[:, 16:RN].rearrange("p a b -> p (a b)")
                step(v.memset(dst, 0.0))
            T1, T2, T3 = (z[:, 0:T] for z in Z[1:])
            pc = lambda i: ARp[:, :, i, :]
            for j in range(4):
                if j:
                    dve.wait_ge(sem("rw_stored"), 64 * j)
                dve.wait_ge(sem("sin_ev"), j + 1)
                dve.wait_ge(sem("z_ev"), (11 + 3 * (j + 1)) * G)
                mix(Z[1], j, C1, flat(Rc), "mixed")
                mix(Z[2], 4 + j, C1, flat(Kc), "mixed")
                mix(Z[3], 8 + j, C1, pads(Vp), "mixed")
                step(v.tensor_scalar(T3, Kc, par("rw_k_k", j), None, MUL), "kraw_ready")
                dve.wait_ge(sem("wl_ev"), j + 1)
                step(v.tensor_tensor_scan(C1, resets[:], T1, 0.0, MUL, ADD))
                step(tt(T1, C1, T1, SUB), "cums_ready")
                dve.wait_ge(sem("al_ev"), j + 1)
                dve.wait_ge(sem("kn_done"), j + 1)
                kn = three(Y[:, 2 + j, :])
                step(v.tensor_scalar(kn, bank3(0), 1e-24, None, MAX), "kn_ev")
                root(4 + 2 * j)
                step(stt(T3, T3, 2.0 ** 15, Y[:, 2 + j, :], MUL, MUL))
                dve.wait_ge(sem("decays"), 3 * (j + 1))
                for o, a, b in zip(pads(pc(0)), chunked(T3), chunked(T1)):
                    step(stt(o, a, -1.0, b, MUL, MUL))
                step(tt(T1, T3, T2, MUL))
                for o, a, b in zip(pads(Bp), chunked(T1), chunked(C1)):
                    step(tt(o, a, b, MUL))
                step(v.tensor_scalar(T2, T2, 1.0, par("rw_k_a", j), SUB, MUL))
                step(stt(Kc, T2, 1.0, Kc, ADD, MUL))
                for o, a, b in zip(pads(Kp), chunked(Kc), chunked(C1)):
                    step(tt(o, a, b, MUL))
                for o, a, b in zip(pads(pc(1)), chunked(Rc), chunked(C2)):
                    step(tt(o, a, b, MUL))
                step(v.tensor_copy(PC[:, 0:16], chunked(C2)[0][:, :, RCH - 1]))
                step(v.tensor_copy(PC[:, 16:RN], chunked(C2)[1][:, :, LS - 1]))
                step(stt(Rc, Rc, par("rw_r_k", j), Kc, MUL, MUL), "rk_ready")
                step(v.memset(S2[:, 0, :], 0.0), "pads_ready")
                dve.wait_ge(sem("bn_done"), j + 1)
                step(v.tensor_copy(three(T2), bank3(3)), "bn_ev")
                for a, b in zip(chunked(T2), pads(Vp)):
                    step(tt(a, a, b, MUL))
                for bt in range(3):
                    for half in range(2):
                        dve.wait_ge(sem("la_done"), 2 * (3 * j + bt) + half + 1)
                        step(tt(LA[:, 4 * half:4 * half + 4], pb[3 + half].rearrange("p (c a t) -> p c a t", c=4, a=2),
                                m_ar[:].unsqueeze(1).to_broadcast([P, 4, 2, RCH]), MUL), "la_ev")
                    for half in range(2):
                        dve.wait_ge(sem("ka_done"), 2 * (3 * j + bt) + half + 1)
                        step(tt(KA[:, 4 * half:4 * half + 4], pb[5 + half].rearrange("p (c a t) -> p c a t", c=4, a=2),
                                m_ar[:].unsqueeze(1).to_broadcast([P, 4, 2, RCH]), MUL), "ka_ev")
                    dve.wait_ge(sem("l_done"), 3 * j + bt + 1)
                    m8 = lambda m: m.unsqueeze(1).to_broadcast([P, 8, RCH])
                    step(tt(X[:], pb[7].rearrange("p (c t) -> p c t", c=8), m8(m_l0[:]), MUL), "l_ev")
                    step(tt(X[:], X[:], m8(idS[:]), ADD))
                    step(tt(XT[:], LA[:, :, 0, :], m8(m_lt[:, 0, :]), MUL))
                    step(tt(XT[:], XT[:], m8(idS[:]), ADD))
                    last = 5 if bt < 2 else 1
                    for l in range(1, last + 1):
                        step(tt(LTm[:], LA[:, :, 0, :], m8(m_lt[:, l, :]), MUL), "lt_ready")
                        n = lt_count(j, bt, l)
                        dve.wait_ge(sem("zx_done"), n)
                        step(tt(X[:], pb[1].rearrange("p (c t) -> p c t", c=8), X[:], ADD), "zx_ev")
                        dve.wait_ge(sem("zt_done"), n)
                        step(tt(XT[:], pb[2].rearrange("p (c t) -> p c t", c=8), XT[:], ADD), "zt_ev")
                    for c in range(8):
                        ci = 8 * bt + c
                        n = RN * j + ci
                        S0 = S2[:, ci % 2, :] if bt < 2 else Sin[:, c, :]
                        S1 = S2[:, (ci + 1) % 2, :] if bt < 2 else Sout[:, c, :]
                        step(v.tensor_scalar(SPc, S0, PC[:, ci:ci + 1], None, MUL), "s_ready")
                        dve.wait_ge(sem("g_done"), n + 1)
                        step(v.tensor_copy(Gb, pb[3][:, 0:64]), "g_ev")
                        dve.wait_ge(sem("ub_done"), n + 1)
                        step(v.tensor_copy(Ub, pb[4][:, 0:64]), "ub_ev")
                        dve.wait_ge(sem("ds_done"), n + 1)
                        step(stt(S1, pb[5][:, 0:64], PC[:, ci:ci + 1], SPc, MUL, ADD), "ds_ev")
                    dve.wait_ge(sem("ry_done"), 3 * j + bt + 1)
                    y = Y[:, 2 + j, :]
                    src = pb[7].rearrange("p (c t) -> p c t", c=8)
                    if bt < 2:
                        step(v.tensor_copy(y[:, 512 * bt:512 * bt + 512], pb[7]), "ry_ev")
                    else:
                        step(v.tensor_copy(dec4(y[:, TP:T]), src[:, :, 0:LS]), "ry_ev")
                y = Y[:, 2 + j, :]
                dve.wait_ge(sem("mn_done"), j + 1)
                step(stt(three(C1), bank3(0), -1.0 / 64, three(y), MUL, ADD), "mn_ev")
                step(v.memset(SPc, 0.0), "centred")
                dve.wait_ge(sem("vr_done"), j + 1)
                step(v.tensor_scalar(three(Kc), bank3(3), 1.0 / 64, GN_EPS, MUL, ADD), "vr_ev")
                root(5 + 2 * j)
                step(tt(C1, C1, Kc, MUL))
                step(v.tensor_scalar(C1, C1, par("rw_ln_w", j), par("rw_ln_b", j), MUL, ADD))
                step(tt(C1, C1, T2, ADD))
                dve.wait_ge(sem("gl_done"), j + 1)
                step(tt(three(y), bank3(0), three(C1), MUL), "gl_ev")
                step(v.memset(SPc, 0.0), "rw_done")
            dve.wait_ge(sem("rw_stored"), 256)
            for n in range(KT):
                for g in range(G):
                    o = MG[:, n, gcol(g)]
                    for br in range(3):
                        p = 3 * (G * n + g) + br
                        dve.wait_ge(sem("sig_ready"), p + 1)
                        lift = pb[2 * (p % 3) + 1][:, 0:GW]
                        if br == 0:
                            step(tt(o, lift, sig[:, p % 3, :], MUL), "pair_ev")
                        else:
                            step(tt(mt[:, p % 3, :], lift, sig[:, p % 3, :], MUL), "pair_ev")
                            step(tt(o, o, mt[:, p % 3, :], ADD), "mg_ready" if br == 2 else "dve_step")

            res = [RING_OUT]

            def residual(base, gate):
                for m_ in range(KT):
                    for g in range(G):
                        b = res[0] % 6
                        res[0] += 1
                        dve.wait_ge(sem("gemm_done"), base + G * m_ + g + 1)
                        n = min(GW, TP - g * GW)
                        x = xT[:, m_, g * GW:g * GW + n]
                        gt = MOD[:, gate + m_, :]
                        ins = stt(x, pb[b][:, 0:n], gt[:, 0:1], x, MUL, ADD)
                        if n == GW:
                            step(ins, "res_ev")
                            continue
                        step(ins)
                        d = dec4(res_t[:])
                        step(tt(d, dec4(pb[b][:, n:GW]), gt[:, 1:].unsqueeze(2).to_broadcast([P, NS, LS]), MUL))
                        x = xT[:, m_, TP:T]
                        step(tt(x, x, res_t[:], ADD), "res_ev")

            dve.wait_ge(sem("x_ev"), 4 * XQ)
            residual(signals[index[("out", 0)]], 16)
            dve.wait_ge(sem("sh_stored"), 32)
            norm(1)
            for i in range(4):
                step(v.memset(Uab[i][:, 0:2], 0.0))
            step(v.memset(res_t[:, 0:1], 0.0), "u_zeroed")
            for half, (m0, m1) in enumerate(HALVES):
                for p in range(m0, m1):
                    for s in range(2):
                        q = 4 * (p // 2) + 2 * (p % 2) + s
                        dve.wait_ge(sem("u_in"), G * (q + 1))
                        if s == 0 and p >= 2:
                            dve.wait_ge(sem("gelu_done"), p - 1)
                        u = Uab[q % 4]
                        c = Cab[p % 2] if s == 0 else Cab[2]
                        dec = u[:, 2 + TP:UL].rearrange("p (n t) -> p n t", t=LS + 2)
                        ch = FT * s + p
                        for k in range(3):
                            wk = par(f"conv_w{k}", ch)
                            for o, src in ((c[:, 0:TP], u[:, k:k + TP]), (dec4(c[:, TP:T]), dec[:, :, k:k + LS])):
                                final = k == 2 and len(o.shape) == 3
                                if k == 0:
                                    ins = v.tensor_scalar(o, src, wk, par("conv_b", ch), MUL, ADD)
                                else:
                                    ins = stt(o, src, wk, o, MUL, ADD)
                                step(ins, "u_used" if final else "dve_step")
                        if s == 0:
                            step(v.memset(res_t[:, 0:1], 0.0), "conv_a")
                    dve.wait_ge(sem("gelu_done"), p + 1)
                    f = FFh[:, p - m0, :]
                    step(tt(f, f, Cab[2], MUL), "ff_ready")
                res[0] += 2 * (m1 - m0) * G
                residual(signals[index[("down", (m0, 0))]], 40)
            norm(2)


def build(nc, args):
    I = dict(zip(_INS, args[:len(_INS)]))
    O = dict(zip(("y_p", "y_s", "s5_p", "sh_p", "rw_p", "hg_p", "cv_p", "s5_s", "sh_s", "rw_s", "hg_s", "cv_s"),
                 args[len(_INS):]))
    trunk(nc, I, O)


_INS = ['x_prompt', 'x_sample', 'c_prompt', 'c_sample', 'state_s5', 'state_rwkv_shift', 'state_rwkv', 'state_hgrn',
        'state_ffn_conv', 'w_ada', 'b_ada', 'g_mix', 'g_ffn', 'w_in', 's5_lambda_re', 's5_lambda_im', 's5_log_dt',
        's5_b_re', 's5_b_im', 's5_c_re', 's5_c_im', 's5_d', 's5_w_glu', 's5_b_glu', 'rw_mu', 'rw_w0', 'rw_w2',
        'rw_a0', 'rw_a2', 'rw_g2', 'rw_k_k', 'rw_k_a', 'rw_r_k', 'rw_ln_w', 'rw_ln_b', 'hg_lb', 'hg_norm',
        'w_lift_a', 'w_lift_b', 'w_lift_c', 'w_out', 'w_up', 'conv_w', 'conv_b', 'w_down', 'final_g']
_OUTS = [((1, 1024, 1024), 'float32'), ((8, 4, 1024), 'float32'),
         ((1, 1, 16, 64, 2), 'float32'), ((1, 1, 1664), 'float32'), ((1, 1, 8, 64, 64), 'float32'),
         ((1, 1, 4, 64, 64), 'float32'), ((1, 1, 2, 5632), 'float32'),
         ((1, 8, 16, 64, 2), 'float32'), ((1, 8, 1664), 'float32'), ((1, 8, 8, 64, 64), 'float32'),
         ((1, 8, 4, 64, 64), 'float32'), ((1, 8, 2, 5632), 'float32')]


def kernel(**inputs):
    import numpy as _np
    import concourse.bacc as _bacc
    from concourse import mybir as _mybir
    from concourse.bass_utils import run_bass_kernel_spmd as _run

    nc = _bacc.Bacc("TRN2", target_bir_lowering=False, num_devices=1)
    arrays, args = {}, []
    for name in _INS:
        a = _np.ascontiguousarray(inputs[name])
        arrays[f"in_{name}_dram"] = a
        args.append(nc.dram_tensor(f"in_{name}_dram", a.shape, _mybir.dt.from_np(a.dtype), kind="ExternalInput").ap())
    for i, (shape, dtype) in enumerate(_OUTS):
        dt = _mybir.dt.from_np(_np.dtype(dtype))
        args.append(nc.dram_tensor(f"out_{i}_dram", shape, dt, kind="ExternalOutput").ap())
    build(nc, args)
    r = _run(nc, [arrays], core_ids=[0])
    return tuple(r.results[0][f"out_{i}_dram"] for i in range(len(_OUTS)))
```

```python
import math
from contextlib import ExitStack

import concourse.bass as bass
from concourse import mybir

F32 = mybir.dt.float32
BF16 = mybir.dt.bfloat16
ALU = mybir.AluOpType
ACT = mybir.ActivationFunctionType
MUL, ADD, SUB, MAX = ALU.mult, ALU.add, ALU.subtract, ALU.max

P = 128
D = 1024
KT = D // P
TP = 1024
NS, LS = 8, 4
TS = NS * LS
T = TP + TS
G, GW = 3, T // 3
NSEQ = 1 + NS
SW = 256
NJ = 8
RC = 1664
RT = RC // P
HW = 256
FF = 2816
FT = FF // P
HC = 16
HN = TP // HC + NS
HT = HN * HC
RCH = 64
RN = TP // RCH + NS
STEPS = TP // RCH + 1
LEVELS = 6
C_DECAY = math.exp(-0.5)
TWO_PI_HI = 6.28125
TWO_PI_LO = 2 * math.pi - 6.28125
ROUND = 12582912.0
PI_SAFE = 3.1415925
RMS_EPS = 1e-6
GN_EPS = 1e-5 * 64
RING_GATES = 10 * G
RING_OUT = RING_GATES + 4 * 14 + 13 * G
RING_UP = RING_OUT + 8 * G
N_SMALL = 26
HALVES = ((0, 12), (12, 22))

ROWS = (
    (("b_ada", 48), ("g_mix", 8), ("g_ffn", 8), ("final_g", 8), ("rw_mu", 13), ("rw_w0", 4), ("rw_a0", 4),
     ("rw_k_k", 4), ("rw_k_a", 4), ("rw_r_k", 4), ("rw_ln_w", 4), ("rw_ln_b", 4), ("hg_lb", 2), ("hg_norm", 2),
     ("s5_d", 2), ("s5_b_glu", 2)),
    (("s5_log_dt", 8), ("s5_lambda_re", 8), ("s5_lambda_im", 8), ("conv_b", 44), ("conv_w2", 44)),
    (("conv_w0", 44), ("conv_w1", 44)),
)


def weight_chunks():
    out = [("ada", c, 1) for c in range(4)]
    out += [("s5", 0, 2 * G), ("hg", 0, 4 * G), ("hg", 1, 4 * G)]
    for q in range(4):
        out += [("ada", 4 + 2 * q, 1), ("ada", 5 + 2 * q, 1), ("gate", q, 4 * G)]
    out += [("gate", 4, 4 * G), ("gate", 5, 4 * G), ("lora", 0, G)]
    out += [("rkv", j, 3 * G) for j in range(4)]
    out += [("lift", c, 12) for c in range(2)]
    out += [("out", c, 4 * G) for c in range(2)]
    for m0, m1 in HALVES:
        out += [("up", m, 4 * G) for m in range(m0, m1, 2)]
        out += [("down", (m0, c), 2 * G) for c in range(4)]
    return out


def trunk(nc, I, O):
    ctx = ExitStack()

    def sb(name, shape, dt=F32):
        return ctx.enter_context(nc.sbuf_tensor(name, shape, dt))

    with ctx:
        hT = sb("hT", [P, KT, T])
        Y = sb("Y", [P, KT, T])
        W = sb("W", [P, 2, 4096])
        PAR = sb("PAR", [P, 3, P])
        MOD = sb("MOD", [P, 48, NSEQ])
        GSC = sb("GSC", [P, 2, KT, NSEQ])
        csT = sb("csT", [P, KT, NSEQ])
        ident = sb("ident", [P, P])
        ones = sb("ones", [P, P])
        hones = sb("hones", [P, P])
        m_ar = sb("m_ar", [P, 2, RCH])
        m_lt = sb("m_lt", [P, LEVELS, RCH])
        m_l0 = sb("m_l0", [P, RCH])
        idS = sb("idS", [P, RCH])
        m16 = sb("m16", [P, 8])
        resets = sb("resets", [P, T], BF16)
        shT = sb("shT", [P, RT, NS])
        shO = sb("shO", [P, RT, NSEQ])
        st5 = sb("st5", [P, 2, NJ, NS])
        ls5 = sb("ls5", [P, 2, NJ, NSEQ])
        s5v = sb("s5v", [P, 24, NJ])
        wpw = sb("wpw", [P, 10, 2, NJ])
        inj = sb("inj", [P, 2, NJ, NS])
        inj_t = sb("inj_t", [P, NJ, NS])
        low = sb("low", [P, 4, 2])
        AR = 24220
        arena = sb("arena", [P, AR])

        def carve(off, *shape):
            n = math.prod(shape)
            assert off + n <= AR, (off, shape)
            a = arena[:, off:off + n]
            if len(shape) == 1:
                return a
            names = "abcd"[:len(shape)]
            return a.rearrange(f"p ({' '.join(names)}) -> p {' '.join(names)}", **dict(zip(names, shape)))

        ps = ctx.enter_context(nc.psum_tensor("ps", [P, 8, 512], F32))
        pb = [ps[:, i, :] for i in range(8)]

        sems = {}

        def sem(name):
            if name not in sems:
                sems[name] = ctx.enter_context(nc.semaphore(name))
            return sems[name]

        def par(name, j=0, n=1, lo=0, hi=P):
            for t, rows in enumerate(ROWS):
                at = 0
                for nm, k in rows:
                    if nm == name:
                        return PAR[lo:hi, t, at + j:at + j + n]
                    at += k
            raise KeyError(name)

        xT = carve(0, KT, T)
        xr = carve(8448, 2, D)
        sq = carve(10496, 2, T)
        rstd = carve(12608, T)
        hn = carve(13664, T)
        rows = carve(14720, 3, P)
        crow = carve(15104, D)
        shrow = carve(16128, RC)
        s5row = carve(17792, 2048)
        U5 = carve(0, 2, T)
        ZH = carve(2112, 4, 2, HT)
        tc, ts = carve(11328, T), carve(12384, T)
        e0, e1, t0, t1 = (carve(13440 + T * i, T) for i in range(4))
        Mg = carve(17664, T)
        BTl = carve(18720, 2, NJ, P)
        CTl = carve(20768, 2, NJ, P)
        BB = carve(13440, 2, NJ, P)
        BRI = carve(22816, 2, NJ, 16)
        CRI = carve(23072, 2, 2, 2, 64)
        BBt = carve(23584, 2, NJ, 16)
        wglu = carve(17664, 2, SW)
        s5out = carve(18720, NJ, P, 2)
        K0, K1, Hp0, Hp1, Ht0, Ht1, Ho, HD, HK = (carve(11328 + HT * i, HT) for i in range(9))
        tok = carve(11328, 2, 2, P)
        Vblk = carve(11840, 2, 8, 64)
        Sx = carve(12864, 81, 64)
        assert 12864 + 81 * 64 <= 11328 + 6 * HT
        Z = [carve(1065 * i, 1065) for i in range(4)]
        ARp = carve(4260, RN, 2, RCH)
        Bp = carve(7332, RN, RCH)
        Kp = carve(8868, RN, RCH)
        Vp = carve(10404, RN, RCH)
        Rc, Kc, C1, C2 = (carve(11940 + T * i, T) for i in range(4))
        Vt, Bt, Kt_ = (carve(16164 + 512 * i, 8, RCH) for i in range(3))
        LA = carve(17700, 8, 2, RCH)
        KA = carve(18724, 8, 2, RCH)
        X, XT, Yb, LTm = (carve(19748 + 512 * i, 8, RCH) for i in range(4))
        Gb = carve(21796, RCH)
        Ub = carve(21860, RCH)
        S2 = carve(21924, 2, RCH)
        SPc = carve(22052, RCH)
        Sin = carve(22116, 8, RCH)
        Sout = carve(11940, 8, RCH)
        PC = carve(22628, RN)
        Lw = carve(22652, 512)
        Lx = carve(23164, T)
        SR = C1[:, 0:512].rearrange("p (a b) -> p a b", a=8)
        SO = C1[:, 0:576].rearrange("p (a b) -> p a b", a=9)
        MG = carve(10496, KT, T)
        sg = carve(18944, 3, T)
        shrow2 = carve(22464, RC)
        FFh = carve(10496, 12, T)
        Yf = Y[:, :, :].rearrange("p a b -> p (a b)")
        UL = 2 + TP + 6 * NS
        Uab = [Yf[:, UL * i:UL * (i + 1)] for i in range(4)]
        Cab = [Yf[:, 4 * UL + T * i:4 * UL + T * (i + 1)] for i in range(3)]
        crw = Yf[:, 7464:7976]
        cob = Yf[:, 7976:8048].rearrange("p (a b) -> p a b", a=4)
        cvr = carve(23168, 2, 512)
        yrow = carve(10496, 2, D)
        sq2, rstd2, hn2 = carve(18944, 2, T), carve(21056, T), carve(22112, T)

        chunks = weight_chunks()
        index = {(k, c): i for i, (k, c, _) in enumerate(chunks)}
        signals = [0]
        for _, _, n in chunks:
            signals.append(signals[-1] + n)

        w_in, w_up, w_down = I["w_in"][0], I["w_up"][0], I["w_down"][0]

        def wsrc(kind, c):
            if kind == "ada":
                return [(0, 8, 512, I["w_ada"][0][:, c * 512:(c + 1) * 512])]
            if kind == "s5":
                return [(0, 8, 256, w_in[:, 0:256])]
            if kind == "hg":
                return [(0, 8, 512, w_in[:, SW + RC + 512 * c:SW + RC + 512 * (c + 1)])]
            if kind == "lora":
                return [(0, 8, 128, w_in[:, SW + 1536:SW + RC])]
            if kind == "rkv":
                return [(1024 * b, 8, 128, w_in[:, SW + 512 * b + 128 * c:SW + 512 * b + 128 * (c + 1)])
                        for b in range(3)]
            if kind == "gate":
                g0 = SW + RC + 4 * HW + 512 * c
                return [(0, 8, 512, w_in[:, g0:g0 + 512])]
            if kind == "lift":
                cs = slice(512 * c, 512 * (c + 1))
                return [(0, 2, 512, I["w_lift_a"][0][:, cs]), (1024, 4, 512, I["w_lift_b"][0][:, cs]),
                        (3072, 2, 512, I["w_lift_c"][0][:, cs])]
            if kind == "out":
                return [(0, 8, 512, I["w_out"][0][:, c * 512:(c + 1) * 512])]
            if kind == "up":
                return [(0, 8, 256, w_up[:, P * c:P * (c + 2)]), (2048, 8, 256, w_up[:, FF + P * c:FF + P * (c + 2)])]
            m0, q = c
            m1 = dict(HALVES)[m0]
            return [(0, m1 - m0, 256, w_down[P * m0:P * m1, 256 * q:256 * (q + 1)])]

        loads = []
        total = [0, 0]
        for i, (k, c, _) in enumerate(chunks):
            total[i % 2] += 16 * len(wsrc(k, c))
            loads.append(total[i % 2])

        def wslot(i, off, n, cols):
            return W[:, i % 2, off:off + n * cols].rearrange("p (k c) -> p k c", k=n)

        def gcol(g):
            return slice(g * GW, (g + 1) * GW)

        XQ = 9

        def xrows(i):
            return P if i < 8 else TS


        Hn = K0
        gst = Y[:, 7, :].rearrange("p (b t) -> p b t", b=3)
        gates = nc.dram_tensor("gates", [24, P, T], F32, kind="Internal").ap()
        K_tmp = carve(17664, 2, NJ, 16)
        chunk_decay = sb("chunk_decay", [P, HN])
        res_t = sb("res_t", [P, TS])
        ldt = sb("ldt", [NJ, 2])
        flag = sb("flag", [P, 1])

        def lt_count(j, bt, l):
            return 11 * j + 5 * bt + l

        def lag_out(v, dve, step, tt, cv, t, d, v_):
            w, bs = HC - d, 3 * (d % 2)
            dve.wait_ge(sem("att_done"), HC * t + d + 1)
            att = ps[:, bs:bs + 3, 0:24 * w].rearrange("p g (c t) -> p g c t", t=w)
            vs = cv(v_)[:, :, 0:w].rearrange("p (g c) t -> p g c t", g=3)
            if d == 0:
                step(tt(cv(Ho).rearrange("p (g c) t -> p g c t", g=3), att, vs, MUL), "att_ev")
            else:
                tmp = cv(Ht0)[:, :, 0:w]
                step(tt(tmp.rearrange("p (g c) t -> p g c t", g=3), att, vs, MUL), "att_ev")
                step(tt(cv(Ho)[:, :, d:], cv(Ho)[:, :, d:], tmp, ADD))

        def state_out(v, dve, step, stt, t, b):
            dve.wait_ge(sem("u_done"), 9 * t + b + 1)
            for c in range(8):
                ci = 8 * b + c
                s, o = (Sx[:, ci], Sx[:, ci + 1]) if b < 8 else (Sx[:, 65 + c], Sx[:, 73 + c])
                step(stt(o, s, chunk_decay[:, ci:ci + 1], pb[b % 2][:, 64 * c:64 * c + 64], MUL, ADD),
                     "u_ev" if c == 7 else "dve_step")

        block = ctx.enter_context(nc.Block())

        @block.sync
        def _(sp):
            n_small = [0]

            def small(dst, src):
                n_small[0] += 1
                sp.dma_start(dst, src).then_inc(sem("small_in"), 16)

            def vec(a):
                while len(a.shape) > 1:
                    a = a[0] if a.shape[0] == 1 else a.rearrange("a b -> (a b)")
                return a.rearrange("(r c) -> r c", c=P)

            sp.wait_ge(sem("rows_zeroed"), 1)
            for t, rws in enumerate(ROWS):
                at = 0
                for nm, k in rws:
                    dst = rows[at:at + k, t, :]
                    if nm == "s5_log_dt":
                        sp.dma_start(ldt[:], I[nm][0].rearrange("(j g) -> j g", g=2)).then_inc(sem("ldt_in"), 16)
                    elif nm.startswith("conv_w"):
                        small(dst, I["conv_w"][0][int(nm[-1])].rearrange("(r c) -> r c", c=P))
                    else:
                        small(dst, vec(I[nm]))
                    at += k
            small(crow[0:1, :], I["c_prompt"])
            small(crow[1:NSEQ, :], I["c_sample"])
            small(shrow[0:NS, :], I["state_rwkv_shift"][0])
            small(s5row[0:NS, :], I["state_s5"][0].rearrange("n g p c -> n (g p c)"))
            assert n_small[0] == N_SMALL, n_small

            def load_x(base, i):
                src = I["x_prompt"][0][P * i:P * (i + 1), :] if i < 8 else I["x_sample"].rearrange("n t d -> (n t) d")
                sp.dma_start(xr[0:xrows(i), i % 2, :], src).then_inc(sem(f"x_in{i % 2}"), 16)

            def weights(i):
                k, c, _ = chunks[i]
                if i >= 2:
                    sp.wait_ge(sem("gemm_done"), signals[i - 1])
                for off, n, cols, src in wsrc(k, c):
                    sp.dma_start(wslot(i, off, n, cols), src.rearrange("(k p) c -> p k c", p=P))\
                        .then_inc(sem(f"w_in{i % 2}"), 16)

            for i in range(2):
                load_x(0, i)
            for i in range(2):
                weights(i)
            for i in range(2, XQ):
                sp.wait_ge(sem("x_turned"), i - 1)
                load_x(0, i)
            for i in range(2, index[("s5", 0)] + 1):
                weights(i)
            sp.wait_ge(sem("h_ready"), 1)
            for ri, nm in enumerate(("s5_b_re", "s5_b_im")):
                sp.dma_start(BRI[:, ri], I[nm][0].rearrange("(j g) p c -> (g p) j c", g=2)).then_inc(sem("s5_in"), 16)
            for ri, nm in enumerate(("s5_c_re", "s5_c_im")):
                src = I[nm][0].rearrange("(a g) c p -> (g c) a p", a=2)
                for dup in range(2):
                    sp.dma_start(CRI[:, ri, :, dup, :], src).then_inc(sem("s5_in"), 16)
            for i in range(index[("hg", 0)], index[("gate", 3)] + 1):
                weights(i)
            sp.wait_ge(sem("s5_scanned"), NJ)
            sp.dma_start(wglu, I["s5_w_glu"][0].rearrange("(k p) c -> p k c", p=P)).then_inc(sem("glu_in"), 16)
            for t in range(2):
                weights(index[("gate", 4 + t)])
                sp.wait_ge(sem("lags_done"), t + 1)
                for h in range(2):
                    sp.dma_start(Sx[64 * h:64 * h + 64, 65:73, :],
                                 I["state_hgrn"][0][:, 2 * t + h].rearrange("n k v -> k n v")).then_inc(sem("hs_in"), 16)
            weights(index[("lora", 0)])
            sp.wait_ge(sem("hg_done"), 2)
            sp.wait_ge(sem("hg_stored"), 128)
            for lo, hi, nm in ((0, 32, "rw_w2"), (32, 64, "rw_a2"), (64, 128, "rw_g2")):
                sp.dma_start(Lw[lo:hi, :], I[nm][0]).then_inc(sem("lw_in"), 16)
            for j in range(4):
                weights(index[("rkv", j)])
                if j:
                    sp.wait_ge(sem("rw_stored"), 64 * j)
                for h in range(2):
                    sp.dma_start(SR[64 * h:64 * h + 64, :, :],
                                 I["state_rwkv"][0][:, 2 * j + h].rearrange("n v k -> v n k")).then_inc(sem("sr_in"), 16)
            for c in range(2):
                weights(index[("lift", c)])
            sp.wait_ge(sem("rw_done"), 4)
            for i in range(2):
                load_x(1, i)
            for i in range(2, XQ):
                sp.wait_ge(sem("x_turned"), XQ + i - 1)
                load_x(1, i)
            for k in range(3):
                sp.wait_ge(sem(f"gate_saved{k}"), 16 * 24)
            for u in range(3 * KT):
                if u >= 3:
                    sp.wait_ge(sem("sg_used"), u - 2)
                sp.dma_start(sg[:, u % 3, :], gates[KT * (u % 3) + u // 3]).then_inc(sem(f"sg_in{u % 3}"), 16)
            for i in range(index[("out", 0)], len(chunks)):
                k, c, _ = chunks[i]
                weights(i)
                if k == "up":
                    n = c // 2
                    if n:
                        sp.wait_ge(sem("conv_turned"), n)
                    for b in range(2):
                        sp.dma_start(crw[0:16, 256 * b:256 * b + 256],
                                     I["state_ffn_conv"][0][:, :, FF * b + P * c:FF * b + P * (c + 2)]
                                     .rearrange("n r c -> (n r) c")).then_inc(sem("conv_in"), 16)

        @block.gpsimd
        def _(pool):
            done = [0]

            def step(ins):
                done[0] += 1
                ins.then_inc(sem("pool_step"), 1)
                pool.wait_ge(sem("pool_step"), done[0])

            pool.memset(rows[:, :, :], 0.0).then_inc(sem("rows_zeroed"), 1)
            step(pool.memset(ones[:], 1.0))
            for m in (ident, hones, m_lt, m_l0, idS):
                step(pool.memset(m[:], 0.0))
            step(pool.memset(m_ar[:], 1.0))
            step(pool.memset(m16[:], 1.0))
            step(pool.memset(hones[0:64, 0:64], 1.0))
            step(pool.memset(hones[64:128, 64:128], 1.0))
            step(pool.affine_select(out=ident[:], in_=ident[:], compare_op=ALU.not_equal, fill=1.0, base=0,
                                    pattern=[[-1, P]], channel_multiplier=1))
            step(pool.affine_select(out=m16[:], in_=m16[:], compare_op=ALU.is_ge, fill=0.0, base=0,
                                    pattern=[[-16, 8]], channel_multiplier=1))
            step(pool.affine_select(out=m16[:], in_=m16[:], compare_op=ALU.is_ge, fill=0.0, base=15,
                                    pattern=[[16, 8]], channel_multiplier=-1))
            for h in range(2):
                hp = slice(64 * h, 64 * h + 64)
                step(pool.affine_select(out=idS[hp], in_=idS[hp], compare_op=ALU.not_equal, fill=1.0, base=0,
                                        pattern=[[-1, RCH]], channel_multiplier=1))
                step(pool.affine_select(out=m_ar[hp, 0], in_=m_ar[hp, 0], compare_op=ALU.is_gt, fill=0.0, base=0,
                                        pattern=[[1, RCH]], channel_multiplier=-1))
                step(pool.affine_select(out=m_ar[hp, 1], in_=m_ar[hp, 1], compare_op=ALU.is_ge, fill=0.0, base=0,
                                        pattern=[[1, RCH]], channel_multiplier=-1))
                v = m_l0[hp, :].rearrange("p (b i) -> p b i", i=2)[:, :, 0]
                step(pool.affine_select(out=v, in_=v, compare_op=ALU.not_equal, fill=1.0, base=-1,
                                        pattern=[[-2, RCH // 2]], channel_multiplier=1))
                for l in range(LEVELS):
                    B = 1 << l
                    v = m_lt[hp, l, :].rearrange("p (b i r) -> p b i r", i=2, r=B)[:, :, 1, :]
                    step(pool.memset(v, 1.0))
                    step(pool.affine_select(out=v, in_=v, compare_op=ALU.is_ge, fill=0.0, base=0,
                                            pattern=[[-2 * B, RCH // (2 * B)], [0, B]], channel_multiplier=1))
                    step(pool.affine_select(out=v, in_=v, compare_op=ALU.is_ge, fill=0.0, base=B - 1,
                                            pattern=[[2 * B, RCH // (2 * B)], [0, B]], channel_multiplier=-1))
            step(pool.memset(resets[:], 1.0))
            step(pool.memset(resets[:, 0:TP].rearrange("p (c t) -> p c t", t=RCH)[:, :, 0], 0.0))
            pool.memset(resets[:, TP:T].rearrange("p (c t) -> p c t", t=LS)[:, :, 0], 0.0)\
                .then_inc(sem("consts_ready"), 1)
            pool.wait_ge(sem("ldt_in"), 16)
            pool.tensor_copy(rows[0:NJ, 1, :].rearrange("p (g c) -> p g c", g=2),
                             ldt[:].unsqueeze(2).to_broadcast([NJ, 2, 64])).then_inc(sem("ldt_spread"), 1)
            stored = {}

            def out(name, dst, src):
                stored[name] = stored.get(name, 0) + 16
                pool.dma_start(dst, src).then_inc(sem(name), 16)

            pool.wait_ge(sem("s5_rows"), 4)
            flat = s5out.rearrange("p a b c -> p (a b c)")
            out("s5_stored", O["s5_p"].rearrange("l n g p c -> (l n) (g p c)"), flat[0:1, :])
            out("s5_stored", O["s5_s"].rearrange("l n g p c -> (l n) (g p c)"), flat[1:NSEQ, :])
            for t in range(2):
                pool.wait_ge(sem("hg_states"), t + 1)
                for h in range(2):
                    hp = slice(64 * h, 64 * h + 64)
                    out("hg_stored", O["hg_p"][0, 0, 2 * t + h], Sx[hp, 64, :])
                    out("hg_stored", O["hg_s"][0][:, 2 * t + h].rearrange("n k v -> k n v"), Sx[hp, 73:81, :])
            for j in range(4):
                pool.wait_ge(sem("rw_rows"), 2 * (j + 1))
                for h in range(2):
                    hp = slice(64 * h, 64 * h + 64)
                    out("rw_stored", O["rw_p"][0, 0, 2 * j + h], SO[hp, 8, :])
                    out("rw_stored", O["rw_s"][0][:, 2 * j + h].rearrange("n v k -> v n k"), SO[hp, 0:8, :])
            pool.wait_ge(sem("sh_rows"), 4)
            out("sh_stored", O["sh_p"].rearrange("l n c -> (l n) c"), shrow2[0:1, :])
            out("sh_stored", O["sh_s"].rearrange("l n c -> (l n) c"), shrow2[1:NSEQ, :])
            for n in range(FT // 2):
                pool.wait_ge(sem("conv_rows"), n + 1)
                for b in range(2):
                    cs = slice(FF * b + 2 * P * n, FF * b + 2 * P * (n + 1))
                    src = cvr[:, n % 2, 256 * b:256 * b + 256]
                    out(f"conv_stored{n % 2}", O["cv_p"][0, 0][:, cs], src[0:2, :])
                    out(f"conv_stored{n % 2}", O["cv_s"][0][:, :, cs].rearrange("n r c -> (n r) c"), src[2:18, :])
            for i in range(XQ):
                pool.wait_ge(sem("y_rows"), 2 * (i + 1))
                dst = O["y_p"][0][P * i:P * (i + 1), :] if i < 8 else O["y_s"].rearrange("n t d -> (n t) d")
                out(f"y_stored{i % 2}", dst, yrow[0:xrows(i), i % 2, :])
            for name, n in stored.items():
                pool.wait_ge(sem(name), n)


        @block.tensor
        def _(pe):
            readers = {}
            last_read = {}

            def take(*banks):
                for b in banks:
                    if b in last_read:
                        pe.wait_ge(sem(last_read[b][0]), last_read[b][1])

            def give(name, *banks):
                readers[name] = readers.get(name, 0) + 1
                for b in banks:
                    last_read[b] = (name, readers[name])

            def mm(out, lhsT, rhs, start=True, stop=True):
                return nc.tensor.matmul(out, lhsT, rhs, start=start, stop=stop, skip_group_check=True)

            def turn(out, in_):
                n = in_.shape[0]
                return nc.tensor.transpose(out, in_, ident[0:n, 0:n])

            ring = [0]

            def gemm(w, c0, nk, rhs, reader):
                for g in range(G):
                    b = ring[0] % 6
                    ring[0] += 1
                    take(b)
                    for k in range(nk):
                        m = mm(pb[b][:, 0:GW], w[:, k, c0:c0 + P], rhs(k)[:, gcol(g)], k == 0, k == nk - 1)
                    m.then_inc(sem("gemm_done"), 1)
                    give(reader, b)

            def arrived(i):
                pe.wait_ge(sem(f"w_in{i % 2}"), loads[i])

            pe.wait_ge(sem("consts_ready"), 1)
            pe.wait_ge(sem("ldt_spread"), 1)
            pe.wait_ge(sem("small_in"), 16 * N_SMALL)
            for t in range(3):
                m = turn(pb[6][:, P * t:P * (t + 1)], rows[:, t, :])
            m.then_inc(sem("par_turned"), 1)
            give("par_ready", 6)
            for k in range(KT):
                m = turn(pb[7][:, NSEQ * k:NSEQ * (k + 1)], crow[0:NSEQ, P * k:P * (k + 1)])
            m.then_inc(sem("c_turned"), 1)
            give("cs_ready", 7)
            take(6)
            for k in range(RT):
                turn(pb[6][:, NS * k:NS * (k + 1)], shrow[0:NS, P * k:P * (k + 1)])
            for ri in range(2):
                for j in range(NJ):
                    m = turn(pb[6][:, 128 + NS * (NJ * ri + j):128 + NS * (NJ * ri + j + 1)],
                             s5row[0:NS, 256 * j + ri:256 * (j + 1):2])
            m.then_inc(sem("st_turned"), 1)
            give("st_ready", 6)

            def turn_x(base):
                for i in range(XQ):
                    n = xrows(i)
                    pe.wait_ge(sem(f"x_in{i % 2}"), 16 * (i // 2 + 1 + base * (5 - i % 2)))
                    for half in range(2):
                        b = 2 * (i % 3) + half
                        take(b)
                        for q in range(4):
                            k = 4 * half + q
                            m = turn(pb[b][:, P * q:P * q + n], xr[0:n, i % 2, P * k:P * (k + 1)])
                        if half == 0:
                            m.then_inc(sem("x_half"), 1)
                        else:
                            m.then_inc(sem("x_turned"), 1)
                        give("x_ev", b)

            turn_x(0)
            take(7)
            def ada(c, bank, t0):
                i = index[("ada", c)]
                arrived(i)
                w = wslot(i, 0, 8, 512)
                for q in range(4):
                    t = t0 + q
                    for k in range(KT):
                        m = mm(bank[:, NSEQ * t:NSEQ * (t + 1)], w[:, k, P * q:P * (q + 1)], csT[:, k, :],
                               k == 0, k == KT - 1)
                m.then_inc(sem("gemm_done"), 1)

            for c in range(4):
                ada(c, pb[7], 4 * c)
            give("mod_ready", 7)

            def norm(n):
                take(0, 1, 2)
                for k in range(KT):
                    pe.wait_ge(sem("sq_ready"), KT * n + k + 1)
                    for g in range(G):
                        m = mm(pb[g][:, 0:GW], ones[:], (sq if n == 0 else sq2)[:, k % 2, gcol(g)], k == 0, k == KT - 1)
                    m.then_inc(sem("sq_used"), 1)
                give("rstd_ready", 0, 1, 2)

            norm(0)
            pe.wait_ge(sem("h_ready"), 1)
            h = lambda k: hT[:, k, :]
            i = index[("s5", 0)]
            arrived(i)
            for t in range(2):
                gemm(wslot(i, 0, 8, 256), P * t, 8, h, "z_ev")
            pe.wait_ge(sem("s5_bb"), 1)
            for q in range(4):
                b = 6 + q % 2
                take(b)
                for r in range(4):
                    m = turn(pb[b][:, P * r:P * (r + 1)], BB[:, q // 2, 4 * (q % 2) + r, :])
                m.then_inc(sem("bt_turned"), 1)
                give("bt_ev", b)
            take(6)
            pe.wait_ge(sem("s5_in"), 16 * 6)
            for ri in range(2):
                for a in range(2):
                    m = turn(pb[6][:, P * (2 * ri + a):P * (2 * ri + a + 1)],
                             CRI[:, ri, a, :, :].rearrange("p a b -> p (a b)"))
            m.then_inc(sem("ct_turned"), 1)
            give("ct_ev", 6)
            for c in range(2):
                i = index[("hg", c)]
                arrived(i)
                for q in range(4):
                    gemm(wslot(i, 0, 8, 512), P * q, 8, h, "z_ev")
            pe.wait_ge(sem("bt_ev"), 4)
            pe.wait_ge(sem("z_ev"), 2 * G)
            misc = [0]

            def misc_bank():
                misc[0] += 1
                take(6 + misc[0] % 2)
                return 6 + misc[0] % 2

            for j in range(NJ):
                for g in range(G):
                    for ri in range(2):
                        b = misc_bank()
                        mm(pb[b][:, 0:GW], BTl[:, ri, j, :], U5[:, j // 4, gcol(g)]).then_inc(sem("e_done"), 1)
                        give("e_ev", b)
                if j % 2 == 0:
                    for c in (4 + j, 5 + j):
                        b = ring[0] % 6
                        ring[0] += 1
                        take(b)
                        ada(c, pb[b], 0)
                        give("mod_rest", b)
                    arrived(index[("gate", j // 2)])
                for q in range(2):
                    gemm(wslot(index[("gate", j // 2)], 0, 8, 512), P * (2 * (j % 2) + q), 8, h, "gate_ev")
                pe.wait_ge(sem("s5_scanned"), j + 1)
                for g in range(G):
                    b = misc_bank()
                    mm(pb[b][:, 0:GW], CTl[:, 0, j, :], e0[:, gcol(g)], True, False)
                    mm(pb[b][:, 0:GW], CTl[:, 1, j, :], e1[:, gcol(g)], False, True).then_inc(sem("y5_done"), 1)
                    give("y5_ev", b)
            for q in range(4):
                b = misc_bank()
                for r in range(4):
                    m = turn(pb[b][0:NSEQ, P * r:P * (r + 1)], ls5[:, q // 2, 4 * (q % 2) + r, :])
                m.then_inc(sem("s5_lturned"), 1)
                give("s5_rows", b)
            pe.wait_ge(sem("glu_in"), 16)
            pe.wait_ge(sem("gelu_ready"), 2)
            for m_ in range(2):
                for g in range(G):
                    b = misc_bank()
                    for k, x in enumerate((t0, t1)):
                        m = mm(pb[b][:, 0:GW], wglu[:, k, P * m_:P * (m_ + 1)], x[:, gcol(g)], k == 0, k == 1)
                    m.then_inc(sem("glu_done"), 1)
                    give("glu_ev", b)
            for t in range(2):
                for d in range(HC):
                    w, bs = HC - d, 3 * (d % 2)
                    pe.wait_ge(sem("prod_ready"), HC * t + d + 1)
                    take(bs, bs + 1, bs + 2)
                    src = (Hp0, Hp1)[d % 2].rearrange("p (c t) -> p c t", t=HC)
                    for q in range(3):
                        m = mm(pb[bs + q][:, 0:24 * w].rearrange("p (c t) -> p c t", t=w), hones[:],
                               src[:, 24 * q:24 * (q + 1), d:HC])
                    m.then_inc(sem("att_done"), 1)
                    give("att_ev", bs, bs + 1, bs + 2)
                    if d == 0:
                        gi = index[("gate", 4 + t)]
                        arrived(gi)
                    if d % 4 != 3:
                        u = 3 * (d // 4) + d % 4
                        b = 6 + u % 2
                        take(b)
                        w8 = wslot(gi, 0, 8, 512)
                        for k in range(KT):
                            m = mm(pb[b][:, 0:GW], w8[:, k, P * (u // G):P * (u // G + 1)], hT[:, k, gcol(u % G)],
                                   k == 0, k == KT - 1)
                        m.then_inc(sem("gemm_done"), 1)
                        give("gate_ev", b)
                pe.wait_ge(sem("hk_ready"), t + 1)

                def tokens(b):
                    k = 6 + b % 2
                    take(k)
                    turn(pb[k][:, 0:P], HK[:, P * b:P * (b + 1)])
                    turn(pb[k][:, P:2 * P], ZH[:, 2, t, P * b:P * (b + 1)]).then_inc(sem("tok_done"), 1)
                    give("tok_ev", k)

                tokens(0)
                for b in range(9):
                    if b < 8:
                        tokens(b + 1)
                    pe.wait_ge(sem("vblk_ready"), 9 * t + b + 1)
                    take(b % 2)
                    for hh in range(2):
                        m = mm(pb[b % 2][64 * hh:64 * hh + 64, :], tok[:, b % 2, 0, 64 * hh:64 * hh + 64],
                               Vblk[:, hh, :, :].rearrange("p a b -> p (a b)"))
                    m.then_inc(sem("u_done"), 1)
                    give("u_ev", b % 2)
                pe.wait_ge(sem("hg_states"), t + 1)
                take(3, 4, 5)
                qd = HD.rearrange("p (c t) -> p c t", t=HC)
                for c in range(HN):
                    s = c if c < 64 else c + 1
                    for hh in range(2):
                        hp = slice(64 * hh, 64 * hh + 64)
                        m = mm(pb[3 + c // 24][hp, HC * (c % 24):HC * (c % 24 + 1)], Sx[hp, s, :], qd[hp, c, :])
                m.then_inc(sem("oi_done"), 1)
                give("oi_ev", 3, 4, 5)
                pe.wait_ge(sem("hsq_ready"), t + 1)
                take(0, 1, 2)
                for q in range(3):
                    m = mm(pb[q][:, 0:384], hones[:], HK[:, 384 * q:384 * (q + 1)])
                m.then_inc(sem("hn_done"), 1)
                give("hn_ev", 0, 1, 2)
            i = index[("lora", 0)]
            arrived(i)
            gemm(wslot(i, 0, 8, 128), 0, 8, h, "z_ev")

            def heads(fn):
                for hh in range(2):
                    m = fn(slice(64 * hh, 64 * hh + 64))
                return m

            for j in range(4):
                i = index[("rkv", j)]
                arrived(i)
                for q in range(3):
                    gemm(wslot(i, 1024 * q, 8, 128), 0, 8, h, "z_ev")
                pe.wait_ge(sem("sr_in"), 32 * (j + 1))
                take(6)
                for n in range(NS):
                    m = heads(lambda hp: mm(pb[6][hp, 64 * n:64 * n + 64], SR[hp, n, :], idS[hp, :]))
                m.then_inc(sem("sin_done"), 1)
                give("sin_ev", 6)
                pe.wait_ge(sem("lora_ready"), 2)
                pe.wait_ge(sem("lw_in"), 48)
                take(0, 1, 2, 3, 4, 5)
                for g in range(G):
                    m = mm(pb[g][:, 0:GW], Lw[0:32, P * j:P * (j + 1)], Lx[0:32, gcol(g)])
                m.then_inc(sem("sum_done"), 1)
                give("wl_ev", 0, 1, 2)
                for g in range(G):
                    m = mm(pb[3 + g][:, 0:GW], Lw[32:64, P * j:P * (j + 1)], Lx[32:64, gcol(g)])
                m.then_inc(sem("sum_done"), 1)
                give("al_ev", 3, 4, 5)
                pe.wait_ge(sem("ksq_ready"), j + 1)
                take(0, 1, 2)
                for g in range(G):
                    m = mm(pb[g][:, 0:GW], hones[:], Y[:, 2 + j, gcol(g)])
                m.then_inc(sem("sum_done"), 1)
                give("sum_ev", 0, 1, 2)
                pe.wait_ge(sem("rk_ready"), j + 1)
                take(3, 4, 5)
                for g in range(G):
                    m = mm(pb[3 + g][:, 0:GW], hones[:], Rc[:, gcol(g)])
                m.then_inc(sem("sum_done"), 1)
                give("sum_ev", 3, 4, 5)
                pe.wait_ge(sem("pads_ready"), j + 1)
                for bt in range(3):
                    for x, (b, src) in enumerate(((0, Vp), (1, Bp), (2, Kp))):
                        take(b)
                        for c in range(8):
                            m = heads(lambda hp: mm(pb[b][hp, 64 * c:64 * c + 64], src[hp, 8 * bt + c, :], idS[hp, :]))
                        m.then_inc(sem("tk_done"), 1)
                        give("tk_ev", b)
                    for half in range(2):
                        take(3 + half)
                        for q in range(4):
                            c = 8 * bt + 4 * half + q
                            m = heads(lambda hp: mm(pb[3 + half][hp, P * q:P * (q + 1)], Bp[hp, c, :],
                                                    ARp[hp, c, :, :].rearrange("p a b -> p (a b)")))
                        m.then_inc(sem("la_done"), 1)
                        give("la_ev", 3 + half)
                    for half in range(2):
                        take(5 + half)
                        for q in range(4):
                            c = 8 * bt + 4 * half + q
                            m = heads(lambda hp: mm(pb[5 + half][hp, P * q:P * (q + 1)], Kp[hp, c, :],
                                                    ARp[hp, c, :, :].rearrange("p a b -> p (a b)")))
                        m.then_inc(sem("ka_done"), 1)
                        give("ka_ev", 5 + half)
                    take(7)
                    for c in range(8):
                        m = heads(lambda hp: mm(pb[7][hp, 64 * c:64 * c + 64], ARp[hp, 8 * bt + c, 0, :],
                                                Bp[hp, 8 * bt + c, :]))
                    m.then_inc(sem("l_done"), 1)
                    give("l_ev", 7)
                    last = 5 if bt < 2 else 1
                    for l in range(1, last + 1):
                        n = lt_count(j, bt, l)
                        pe.wait_ge(sem("lt_ready"), n)

                        def half_mm(b, lhsT, rhs, half):
                            for c in range(4 * half, 4 * half + 4):
                                m = heads(lambda hp: mm(pb[b][hp, 64 * (c % 4):64 * (c % 4) + 64], lhsT[hp, c, :],
                                                        rhs[hp, c, :]))
                            return m

                        for half in range(2):
                            if l > 1:
                                pe.wait_ge(sem("zx_ev"), 2 * (n - 2) + half + 1)
                            take(half)
                            half_mm(half, LTm, X, half).then_inc(sem("yy_done"), 1)
                            give("yy_ev", half)
                        for half in range(2):
                            pe.wait_ge(sem("yy_ev"), 2 * (n - 1) + half + 1)
                            if l > 1:
                                pe.wait_ge(sem("zt_ev"), 2 * (n - 2) + half + 1)
                            take(2 + half)
                            half_mm(2 + half, XT, Yb, half).then_inc(sem("zx_done"), 1)
                            give("zx_ev", 2 + half)
                            take(4 + half)
                            half_mm(4 + half, Yb, XT, half).then_inc(sem("zt_done"), 1)
                            give("zt_ev", 4 + half)
                    pe.wait_ge(sem("zt_ev"), 2 * lt_count(j, bt, last))
                    pe.wait_ge(sem("tk_ev"), 3 * (3 * j + bt + 1))
                    pe.wait_ge(sem("ka_ev"), 2 * (3 * j + bt + 1))
                    pe.wait_ge(sem("la_ev"), 2 * (3 * j + bt + 1))
                    take(3, 4, 5, 7)
                    if bt == 2:
                        n = STEPS * j + 16
                        pe.wait_ge(sem("s_ready"), n + 1)
                        for c in range(8):
                            def g8(hp):
                                o = pb[3][hp, 64 * c:64 * c + 64]
                                mm(o, ARp[hp, 16 + c, 0, :], Sin[hp, c, :], True, False)
                                return mm(o, KA[hp, c, 0, :], Vt[hp, c, :], False, True)
                            m = heads(g8)
                        m.then_inc(sem("g_done"), 1)
                        give("g_ev", 3)
                        pe.wait_ge(sem("g_ev"), n + 1)
                        for c in range(8):
                            m = heads(lambda hp: mm(pb[4][hp, 64 * c:64 * c + 64], XT[hp, c, :], LTm[hp, c, :]))
                        m.then_inc(sem("ub_done"), 1)
                        give("ub_ev", 4)
                        pe.wait_ge(sem("ub_ev"), n + 1)
                        for c in range(8):
                            def d8(hp):
                                o = pb[5][hp, 64 * c:64 * c + 64]
                                mm(o, Bt[hp, c, :], Yb[hp, c, :], True, False)
                                return mm(o, Kt_[hp, c, :], Vt[hp, c, :], False, True)
                            m = heads(d8)
                        m.then_inc(sem("ds_done"), 1)
                        give("ds_ev", 5)
                        for c in range(8):
                            def y8(hp):
                                o = pb[7][hp, 64 * c:64 * c + 64]
                                mm(o, Sin[hp, c, :], ARp[hp, 16 + c, 1, :], True, False)
                                mm(o, Yb[hp, c, :], LA[hp, c, 1, :], False, False)
                                return mm(o, Vt[hp, c, :], KA[hp, c, 1, :], False, True)
                            m = heads(y8)
                    for c in range(8 if bt < 2 else 0):
                        n = STEPS * j + 8 * bt + c
                        ci = 8 * bt + c
                        S0 = S2[:, ci % 2, :]
                        pe.wait_ge(sem("s_ready"), n + 1)
                        take(3)

                        def g_(hp):
                            mm(pb[3][hp, 0:64], ARp[hp, ci, 0, :], S0[hp, :], True, False)
                            return mm(pb[3][hp, 0:64], KA[hp, c, 0, :], Vt[hp, c, :], False, True)
                        heads(g_).then_inc(sem("g_done"), 1)
                        give("g_ev", 3)
                        pe.wait_ge(sem("g_ev"), n + 1)
                        take(4)
                        heads(lambda hp: mm(pb[4][hp, 0:64], XT[hp, c, :], Gb[hp, :])).then_inc(sem("ub_done"), 1)
                        give("ub_ev", 4)
                        pe.wait_ge(sem("ub_ev"), n + 1)
                        take(5)

                        def ds_(hp):
                            mm(pb[5][hp, 0:64], Bt[hp, c, :], Ub[hp, :], True, False)
                            return mm(pb[5][hp, 0:64], Kt_[hp, c, :], Vt[hp, c, :], False, True)
                        heads(ds_).then_inc(sem("ds_done"), 1)
                        give("ds_ev", 5)

                        def y_(hp):
                            o = pb[7][hp, 64 * c:64 * c + 64]
                            mm(o, S0[hp, :], ARp[hp, ci, 1, :], True, False)
                            mm(o, Ub[hp, :], LA[hp, c, 1, :], False, False)
                            return mm(o, Vt[hp, c, :], KA[hp, c, 1, :], False, True)
                        m = heads(y_)
                    m.then_inc(sem("ry_done"), 1)
                    give("ry_ev", 7)
                pe.wait_ge(sem("ry_ev"), 3 * (j + 1))
                take(0, 1, 2)
                for g in range(G):
                    m = mm(pb[g][:, 0:GW], hones[:], Y[:, 2 + j, gcol(g)])
                m.then_inc(sem("sum_done"), 1)
                give("sum_ev", 0, 1, 2)
                pe.wait_ge(sem("ds_ev"), STEPS * (j + 1))
                take(6, 7)
                for n in range(NS):
                    m = heads(lambda hp: mm(pb[6][hp, 64 * n:64 * n + 64], Sout[hp, n, :], idS[hp, :]))
                m.then_inc(sem("so_done"), 1)
                give("rw_rows", 6)
                heads(lambda hp: mm(pb[7][hp, 0:64], S2[hp, 0, :], idS[hp, :])).then_inc(sem("so_done"), 1)
                give("rw_rows", 7)
                pe.wait_ge(sem("ysq_ready"), j + 1)
                take(3, 4, 5)
                for g in range(G):
                    m = mm(pb[3 + g][:, 0:GW], hones[:], C2[:, gcol(g)])
                m.then_inc(sem("sum_done"), 1)
                give("sum_ev", 3, 4, 5)
                take(0, 1, 2)
                for g in range(G):
                    m = mm(pb[g][:, 0:GW], Lw[64:128, P * j:P * (j + 1)], Lx[64:128, gcol(g)])
                m.then_inc(sem("sum_done"), 1)
                give("sum_ev", 0, 1, 2)
            pe.wait_ge(sem("sho_ready"), RT)
            for b in range(4):
                take(b)
                for q in range(4 if b < 3 else 1):
                    m = turn(pb[b][0:NSEQ, P * q:P * (q + 1)], shO[:, 4 * b + q, :])
                m.then_inc(sem("sh_turned"), 1)
                give("sh_rows", b)
            turn_x(1)
            for n in range(KT):
                i = index[("lift", n // 4)]
                if n % 4 == 0:
                    arrived(i)
                for br, (off, nk, y0) in enumerate(((0, 2, 0), (1024, 4, 2), (3072, 2, 6))):
                    b = 3 * ((3 * n + br) % 2)
                    take(b, b + 1, b + 2)
                    w = wslot(i, off, nk, 512)
                    for g in range(G):
                        for k in range(nk):
                            m = mm(pb[b + g][:, 0:GW], w[:, k, P * (n % 4):P * (n % 4 + 1)], Y[:, y0 + k, gcol(g)],
                                   k == 0, k == nk - 1)
                    m.then_inc(sem("gemm_done"), 1)
                    give("lift_ev", b, b + 1, b + 2)
            pe.wait_ge(sem("mg_ready"), KT)
            for c in range(2):
                i = index[("out", c)]
                arrived(i)
                for q in range(4):
                    gemm(wslot(i, 0, 8, 512), P * q, 8, lambda k: MG[:, k, :], "res_ev")
            norm(1)
            pe.wait_ge(sem("h_ready"), 2)

            def last_rows(n):
                pe.wait_ge(sem("cob_ready"), n + 1)
                take(7)
                for q in range(4):
                    m = turn(pb[7][0:18, P * q:P * (q + 1)], cob[:, q, :])
                m.then_inc(sem("cob_turned"), 1)
                give("conv_rows", 7)

            for half, (m0, m1) in enumerate(HALVES):
                for mt_ in range(m0, m1, 2):
                    n = mt_ // 2
                    pe.wait_ge(sem("conv_in"), 32 * (n + 1))
                    take(6)
                    for q in range(4):
                        m = turn(pb[6][:, 16 * q:16 * q + 16], crw[0:16, P * q:P * (q + 1)])
                    m.then_inc(sem("conv_turned"), 1)
                    give("cst_ev", 6)
                    i = index[("up", mt_)]
                    arrived(i)
                    for q in range(2):
                        for s in range(2):
                            gemm(wslot(i, 2048 * s, 8, 256), P * q, 8, h, "u_in")
                    if n:
                        last_rows(n - 1)
                pe.wait_ge(sem("ff_ready"), m1)
                for c in range(4):
                    i = index[("down", (m0, c))]
                    arrived(i)
                    for q in range(2):
                        gemm(wslot(i, 0, m1 - m0, 256), P * q, m1 - m0, lambda k: FFh[:, k, :], "res_ev")
            last_rows(FT // 2 - 1)
            norm(2)
            pe.wait_ge(sem("h_ready"), 3)
            for i in range(XQ):
                n = xrows(i)
                for half in range(2):
                    b = 2 * (i % 3) + half
                    take(b)
                    for q in range(4):
                        k = 4 * half + q
                        m = turn(pb[b][0:n, P * q:P * (q + 1)], hT[:, k, P * i:P * i + n])
                    m.then_inc(sem("y_turned"), 1)
                    give("y_rows", b)

        @block.scalar
        def _(act):
            done = [0]

            def step(ins):
                done[0] += 1
                ins.then_inc(sem("act_step"), 1)
                act.wait_ge(sem("act_step"), done[0])

            def copy(out, in_):
                return nc.scalar.activation(out, in_, ACT.Copy)

            act.wait_ge(sem("c_turned"), 1)
            nc.scalar.activation(csT[:].rearrange("p a b -> p (a b)"), pb[7][:, 0:KT * NSEQ], ACT.Silu)\
                .then_inc(sem("cs_ready"), 1)

            def evac_x(base):
                for i in range(XQ):
                    n = xrows(i)
                    for half in range(2):
                        b = 2 * (i % 3) + half
                        act.wait_ge(sem("x_half" if half == 0 else "x_turned"), XQ * base + i + 1)
                        copy(xT[:, 4 * half:4 * half + 4, P * i:P * i + n],
                             pb[b][:, :].rearrange("p (q t) -> p q t", q=4)[:, :, 0:n]).then_inc(sem("x_ev"), 1)

            act.wait_ge(sem("par_ready"), 1)
            V = lambda k: s5v[:, k, :]
            step(nc.scalar.activation(V(0), par("s5_log_dt", 0, NJ), ACT.Exp))
            nc.scalar.copy(V(1), V(0)).then_inc(sem("dt_ready"), 1)
            act.wait_ge(sem("low_diff"), 1)
            nc.scalar.activation(low[:, 1], low[:, 0], ACT.Exp).then_inc(sem("low_exp"), 1)
            act.wait_ge(sem("angles_ready"), 1)
            nc.scalar.activation(V(5), V(2), ACT.Exp).then_inc(sem("s5_fn"), 1)
            nc.scalar.activation(V(6), V(3), ACT.Sin).then_inc(sem("s5_fn"), 1)
            nc.scalar.activation(V(7), V(4), ACT.Sin).then_inc(sem("s5_fn"), 1)
            evac_x(0)

            def root(buf, n, scale=1.0):
                act.wait_ge(sem("var_ready"), n)
                step(nc.scalar.activation(buf, buf, ACT.Ln, scale=scale))
                nc.scalar.activation(buf, buf, ACT.Exp, scale=-0.5).then_inc(sem("rs_ready"), 1)

            def norm(n):
                buf = sq if n == 0 else sq2
                for k in range(KT):
                    i = KT * n + k
                    if i >= 2:
                        act.wait_ge(sem("sq_used"), i - 1)
                    nc.scalar.activation(buf[:, k % 2, :], xT[:, k, :], ACT.Square).then_inc(sem("sq_ready"), 1)
                root(rstd if n == 0 else rstd2, (1, 12, 13)[n])

            act.wait_ge(sem("x_ev"), 2 * XQ)
            norm(0)
            ring = [0]
            z_n = [0]

            def z_evac(dst_of, fn, count):
                for g in range(G):
                    b = ring[0] % 6
                    ring[0] += 1
                    act.wait_ge(sem("gemm_done"), count + g + 1)
                    for ins in dst_of(g, pb[b], fn):
                        m = ins
                    m.then_inc(sem("z_ev"), 1)

            def compact(dst):
                def go(g, bank, fn):
                    yield nc.scalar.activation(dst[:, gcol(g)], bank[:, 0:GW], fn)
                return go

            def split(prompt, decode):
                def go(g, bank, fn):
                    n = min(GW, TP - g * GW)
                    yield nc.scalar.activation(prompt[:, g * GW:g * GW + n], bank[:, 0:n], fn)
                    if n < GW:
                        yield nc.scalar.activation(decode, bank[:, n:GW].rearrange("p (a b) -> p a b", b=LS), fn)
                return go

            base = signals[index[("s5", 0)]]
            act.wait_ge(sem("h_ready"), 1)
            for t in range(2):
                z_evac(compact(U5[:, t, :]), ACT.Copy, base + G * t)
            act.wait_ge(sem("zh_padded"), 1)
            base = signals[index[("hg", 0)]]
            for q, fn in enumerate((ACT.Silu, ACT.Sigmoid, ACT.Copy, ACT.Sigmoid)):
                for t in range(2):
                    z = ZH[:, q, t, :]
                    z_evac(split(z[:, 0:TP], z[:, TP:HT].rearrange("p (c t) -> p c t", t=HC)[:, :, 0:LS]), fn,
                           base + G * (2 * q + t))
            gate_n = [0]

            def beside_s5(j):
                if j % 2 == 0:
                    for c in (4 + j, 5 + j):
                        act.wait_ge(sem("gemm_done"), signals[index[("ada", c)] + 1])
                        bank = pb[ring[0] % 6]
                        ring[0] += 1
                        for q in range(4):
                            t = 4 * c + q
                            m = nc.scalar.activation(MOD[:, t, :], bank[:, NSEQ * q:NSEQ * (q + 1)], ACT.Identity,
                                                     bias=par("b_ada", t))
                        m.then_inc(sem("mod_rest"), 1)
                for u in range(2 * G):
                    n = 2 * G * (j % 2) + u
                    bank = pb[ring[0] % 6]
                    ring[0] += 1
                    save_gate(signals[index[("gate", j // 2)]] + n + 1, bank, 4 * (j // 2) + n // G, n % G)

            def save_gate(done, bank, tile, g):
                u = gate_n[0]
                gate_n[0] += 1
                act.wait_ge(sem("gemm_done"), done)
                if u >= 3:
                    act.wait_ge(sem(f"gate_saved{u % 3}"), 16 * (u // 3))
                nc.scalar.activation(gst[:, u % 3, :], bank[:, 0:GW], ACT.Sigmoid).then_inc(sem("gate_ev"), 1)
                act.wait_ge(sem("gate_ev"), u + 1)
                act.dma_start(gates[tile, :, gcol(g)], gst[:, u % 3, :]).then_inc(sem(f"gate_saved{u % 3}"), 16)

            for j in range(NJ):
                if j:
                    beside_s5(j - 1)
                for g in range(G):
                    for ri in range(2):
                        act.wait_ge(sem("e_done"), 6 * j + 2 * g + ri + 1)
                        if j == 0:
                            act.wait_ge(sem("bt_ev"), 4)
                        copy((e0, e1)[ri][:, gcol(g)], pb[6 + (9 * j + 2 * g + ri + 1) % 2][:, 0:GW])\
                            .then_inc(sem("e_ev"), 1)
            beside_s5(NJ - 1)
            act.wait_ge(sem("y5_ev"), G * NJ)
            for a in range(2):
                nc.scalar.activation((t0, t1)[a], Y[:, a, :], ACT.Gelu_apprx_tanh).then_inc(sem("gelu_ready"), 1)
            for m_ in range(2):
                for g in range(G):
                    n = G * m_ + g
                    act.wait_ge(sem("glu_done"), n + 1)
                    nc.scalar.activation((e0, e1)[m_][:, gcol(g)], pb[6 + (9 * NJ + 4 + n + 1) % 2][:, 0:GW], ACT.Sigmoid,
                                         bias=par("s5_b_glu", m_)).then_inc(sem("glu_ev"), 1)
            for t in range(2):
                for u in range(4 * G):
                    save_gate(signals[index[("gate", 4 + t)]] + u + 1, pb[6 + u % 2], 4 * (4 + t) + u // G, u % G)
                for b in range(9):
                    act.wait_ge(sem("tok_done"), 9 * t + b + 1)
                    if b >= 2:
                        act.wait_ge(sem("u_done"), 9 * t + b - 1)
                    copy(tok[:, b % 2, :, :].rearrange("p a b -> p (a b)"), pb[6 + b % 2][:, 0:2 * P])\
                        .then_inc(sem("tok_ev"), 1)
                act.wait_ge(sem("oi_ev"), t + 1)
                nc.scalar.activation(HK, Ho, ACT.Square).then_inc(sem("hsq_ready"), 1)
                root(Hn, 2 + t)
            act.wait_ge(sem("hg_done"), 2)
            act.wait_ge(sem("hg_stored"), 128)

            def zplace(z):
                return split(z[:, 1:1 + TP], z[:, 1 + TP:1065].rearrange("p (n t) -> p n t", t=LS + 1)[:, :, 1:])

            z_evac(zplace(Z[0]), ACT.Copy, signals[index[("lora", 0)]])
            act.wait_ge(sem("lora_mixed"), 1)
            nc.scalar.activation(Lx[0:32, :], Lx[0:32, :], ACT.Tanh).then_inc(sem("lora_ready"), 1)
            nc.scalar.activation(Lx[64:128, :], Lx[64:128, :], ACT.Sigmoid).then_inc(sem("lora_ready"), 1)
            bank3 = lambda b: ps[:, b:b + 3, 0:GW]
            three = lambda x: x[:, 0:T].rearrange("p (g t) -> p g t", g=G)
            T1, T2, T3 = (z[:, 0:T] for z in Z[1:])
            for j in range(4):
                if j:
                    act.wait_ge(sem("rw_done"), j)
                for q in range(3):
                    z_evac(zplace(Z[1 + q]), ACT.Copy, signals[index[("rkv", j)]] + G * q)
                act.wait_ge(sem("sin_done"), j + 1)
                copy(Sin[:].rearrange("p a b -> p (a b)"), pb[6][:, :]).then_inc(sem("sin_ev"), 1)
                act.wait_ge(sem("mixed"), 3 * (j + 1))
                act.wait_ge(sem("sum_done"), 7 * j + 1)
                nc.scalar.activation(three(T1), bank3(0), ACT.Sigmoid, bias=par("rw_w0", j)).then_inc(sem("wl_ev"), 1)
                act.wait_ge(sem("sum_done"), 7 * j + 2)
                nc.scalar.activation(three(T2), bank3(3), ACT.Sigmoid, bias=par("rw_a0", j)).then_inc(sem("al_ev"), 1)
                act.wait_ge(sem("kraw_ready"), j + 1)
                nc.scalar.activation(Y[:, 2 + j, :], T3, ACT.Square).then_inc(sem("ksq_ready"), 1)
                act.wait_ge(sem("cums_ready"), j + 1)
                nc.scalar.activation(C2, C1, ACT.Exp, scale=-C_DECAY).then_inc(sem("decays"), 1)
                act.wait_ge(sem("decays"), 3 * j + 1)
                nc.scalar.activation(C1, C1, ACT.Exp, scale=C_DECAY).then_inc(sem("decays"), 1)
                nc.scalar.activation(T1, T1, ACT.Exp, scale=-C_DECAY).then_inc(sem("decays"), 1)
                root(Y[:, 2 + j, :], 4 + 2 * j, 2.0 ** 30)
                for bt in range(3):
                    for x, dst in enumerate((Vt, Bt, Kt_)):
                        act.wait_ge(sem("tk_done"), 3 * (3 * j + bt) + x + 1)
                        copy(dst[:].rearrange("p a b -> p (a b)"), pb[x][:, :]).then_inc(sem("tk_ev"), 1)
                    for l in range(1, (5 if bt < 2 else 1) + 1):
                        for half in range(2):
                            act.wait_ge(sem("yy_done"), 2 * (lt_count(j, bt, l) - 1) + half + 1)
                            copy(Yb[:, 4 * half:4 * half + 4].rearrange("p a b -> p (a b)"), pb[half][:, 0:256])\
                                .then_inc(sem("yy_ev"), 1)
                act.wait_ge(sem("centred"), j + 1)
                nc.scalar.activation(C2, C1, ACT.Square).then_inc(sem("ysq_ready"), 1)
                root(Kc, 5 + 2 * j)
                act.wait_ge(sem("rw_done"), j + 1)
                act.wait_ge(sem("so_done"), 2 * (j + 1))
                copy(SO[:, 0:8, :].rearrange("p a b -> p (a b)"), pb[6][:, :]).then_inc(sem("rw_rows"), 1)
                copy(SO[:, 8, :], pb[7][:, 0:64]).then_inc(sem("rw_rows"), 1)
            for b in range(4):
                act.wait_ge(sem("sh_turned"), b + 1)
                n = 512 if b < 3 else P
                copy(shrow2[0:NSEQ, 512 * b:512 * b + n], pb[b][0:NSEQ, 0:n]).then_inc(sem("sh_rows"), 1)
            evac_x(1)
            act.wait_ge(sem("res_ev"), 8 * G)
            norm(1)

            def rows_out(n):
                act.wait_ge(sem("cob_turned"), n + 1)
                if n >= 2:
                    act.wait_ge(sem(f"conv_stored{n % 2}"), 64 * (n // 2))
                copy(cvr[0:18, n % 2, :], pb[7][0:18, :]).then_inc(sem("conv_rows"), 1)

            act.wait_ge(sem("u_zeroed"), 1)
            ring[0] = RING_UP
            for mt_ in range(0, FT, 2):
                n = mt_ // 2
                half = 0 if mt_ < HALVES[0][1] else 1
                if mt_ == HALVES[1][0]:
                    ring[0] += 8 * G
                act.wait_ge(sem("conv_turned"), n + 1)
                for q in range(4):
                    src = (q % 2) * 2 + q // 2
                    if n:
                        act.wait_ge(sem("u_used"), 4 * n + q - 3)
                    u = Uab[q]
                    dec = u[:, 2 + TP:UL].rearrange("p (n t) -> p n t", t=LS + 2)
                    m = copy(dec[:, :, 0:2], pb[6][:, 16 * src:16 * src + 16].rearrange("p (n r) -> p n r", r=2))
                    if q == 3:
                        m.then_inc(sem("cst_ev"), 1)
                    z0 = signals[index[("up", mt_)]] + G * q
                    for g in range(G):
                        b = ring[0] % 6
                        ring[0] += 1
                        act.wait_ge(sem("gemm_done"), z0 + g + 1)
                        k = min(GW, TP - g * GW)
                        m = copy(u[:, 2 + g * GW:2 + g * GW + k], pb[b][:, 0:k])
                        if k < GW:
                            m = copy(dec[:, :, 2:], pb[b][:, k:GW].rearrange("p (n t) -> p n t", t=LS))
                        m.then_inc(sem("u_in"), 1)
                    if q % 2:
                        p = 2 * n + q // 2
                        if p == HALVES[1][0]:
                            act.wait_ge(sem("res_ev"), 16 * G)
                        act.wait_ge(sem("conv_a"), p + 1)
                        nc.scalar.activation(FFh[:, p - (0 if p < HALVES[0][1] else HALVES[1][0]), :], Cab[p % 2],
                                             ACT.Gelu_apprx_tanh).then_inc(sem("gelu_done"), 1)
                act.wait_ge(sem("u_in"), G * 4 * (n + 1))
                if n:
                    rows_out(n - 1)
                    act.wait_ge(sem("cob_turned"), n)
                for q in range(4):
                    src = (q % 2) * 2 + q // 2
                    u = Uab[q]
                    dec = u[:, 2 + TP:UL].rearrange("p (n t) -> p n t", t=LS + 2)
                    copy(cob[:, src, 0:2], u[:, TP:TP + 2])
                    m = copy(cob[:, src, 2:18].rearrange("p (n r) -> p n r", r=2), dec[:, :, 4:6])
                m.then_inc(sem("cob_ready"), 1)
                act.wait_ge(sem("cob_ready"), n + 1)
            rows_out(FT // 2 - 1)
            act.wait_ge(sem("res_ev"), 24 * G)
            norm(2)
            for i in range(XQ):
                n = xrows(i)
                if i >= 2:
                    act.wait_ge(sem(f"y_stored{i % 2}"), 16 * (i // 2))
                for half in range(2):
                    act.wait_ge(sem("y_turned"), 2 * i + half + 1)
                    copy(yrow[0:n, i % 2, 512 * half:512 * half + 512], pb[2 * (i % 3) + half][0:n, :])\
                        .then_inc(sem("y_rows"), 1)

        @block.vector
        def _(dve):
            counts = {}
            v = nc.vector

            def step(ins, name="dve_step"):
                counts[name] = counts.get(name, 0) + 1
                ins.then_inc(sem(name), 1)

                dve.wait_ge(sem(name), counts[name])

            bank3 = lambda b: ps[:, b:b + 3, 0:GW]
            three = lambda x: x[:, 0:T].rearrange("p (g t) -> p g t", g=G)
            dec4 = lambda x: x.rearrange("p (n t) -> p n t", t=LS)

            def tt(out, a, b, op):
                return v.tensor_tensor(out, a, b, op)

            def stt(out, a, s, b, op0, op1):
                return v.scalar_tensor_tensor(out=out, in0=a, scalar=s, in1=b, op0=op0, op1=op1)

            dve.wait_ge(sem("par_turned"), 1)
            step(v.tensor_copy(PAR[:].rearrange("p a b -> p (a b)"), pb[6][:, 0:384]), "par_ready")
            dve.wait_ge(sem("st_turned"), 1)
            step(v.tensor_copy(shT[:].rearrange("p a b -> p (a b)"), pb[6][:, 0:RT * NS]))
            step(v.tensor_copy(st5[:].rearrange("p a b c -> p (a b c)"), pb[6][:, 128:256]), "st_ready")
            V = lambda k: s5v[:, k, :]
            lr, li = par("s5_lambda_re", 0, NJ), par("s5_lambda_im", 0, NJ)
            dve.wait_ge(sem("dt_ready"), 1)
            step(tt(V(8), li, V(0), MUL))
            step(v.tensor_scalar(V(9), V(8), math.pi / 2, None, ADD))
            for src, dst, tmp in ((8, 3, 10), (9, 4, 11)):
                step(v.tensor_scalar(V(tmp), V(src), 1 / (2 * math.pi), ROUND, MUL, ADD))
                step(v.tensor_scalar(V(tmp), V(tmp), ROUND, None, SUB))
                step(stt(V(12), V(tmp), -TWO_PI_HI, V(src), MUL, ADD))
                step(stt(V(12), V(tmp), -TWO_PI_LO, V(12), MUL, ADD))
                step(v.tensor_scalar(V(dst), V(12), PI_SAFE, -PI_SAFE, ALU.min, MAX))
            step(tt(V(2), lr, V(0), MUL), "angles_ready")
            lb = par("hg_lb", 0, 2)
            step(tt(low[:, 0], lb, lb, SUB), "low_diff")
            dve.wait_ge(sem("low_exp"), 1)
            step(v.reciprocal(low[:, 2], low[:, 1]))
            step(tt(low[:, 2], low[:, 1], low[:, 2], MUL))
            step(tt(low[:, 0], low[:, 2], low[:, 2], SUB))
            step(v.tensor_scalar(low[:, 3], low[:, 0], -1.0, 1.0, MUL, ADD))
            dve.wait_ge(sem("gemm_done"), 4)
            b_ada = par("b_ada", 0, 16).unsqueeze(2).to_broadcast([P, 16, NSEQ])
            step(tt(MOD[:, 0:16], pb[7][:, 0:16 * NSEQ].rearrange("p (a b) -> p a b", b=NSEQ), b_ada, ADD), "mod_ready")

            def scales(n):
                gb = par(("g_mix", "g_ffn")[n], 0, KT).unsqueeze(2).to_broadcast([P, KT, NSEQ])
                step(stt(GSC[:, n], MOD[:, 24 * n + 8:24 * n + 16, :], 1.0, gb, ADD, MUL))

            scales(0)

            def root(n):
                step(v.memset(flag[:], 0.0), "var_ready")
                dve.wait_ge(sem("rs_ready"), n)

            def norm(n):
                rs, hn_ = (rstd, hn) if n == 0 else (rstd2, hn2)
                dve.wait_ge(sem("sq_used"), KT * (n + 1))
                step(v.tensor_scalar(three(rs), bank3(0), 1.0 / D, RMS_EPS, MUL, ADD), "rstd_ready")
                root((1, 12, 13)[n])
                for k in range(KT):
                    if n == 2:
                        step(stt(hT[:, k, :], xT[:, k, :], par("final_g", k), rs, MUL, MUL))
                        continue
                    step(tt(hn_, xT[:, k, :], rs, MUL))
                    A, B = GSC[:, n, k, :], MOD[:, 24 * n + k, :]
                    step(v.tensor_scalar(hT[:, k, 0:TP], hn_[:, 0:TP], A[:, 0:1], B[:, 0:1], MUL, ADD))
                    d = dec4(hn_[:, TP:T])
                    step(tt(d, d, A[:, 1:].unsqueeze(2).to_broadcast([P, NS, LS]), MUL))
                    step(tt(dec4(hT[:, k, TP:T]), d, B[:, 1:].unsqueeze(2).to_broadcast([P, NS, LS]), ADD))
                step(v.tensor_copy(flag[:], m16[:, 0:1]), "h_ready")

            norm(0)
            dve.wait_ge(sem("h_ready"), 1)
            for q in range(4):
                for t in range(2):
                    z = ZH[:, q, t, TP:HT].rearrange("p (c t) -> p c t", t=HC)[:, :, LS:]
                    step(v.memset(z, 1.0 if q == 1 else 0.0))
            step(v.memset(flag[:], 1.0), "zh_padded")
            dve.wait_ge(sem("s5_fn"), 3)
            mag, sn, cs = V(5), V(6), V(7)
            step(tt(V(8), mag, cs, MUL))
            step(tt(V(9), mag, sn, MUL))
            step(tt(V(10), lr, lr, MUL))
            step(tt(V(11), li, li, MUL))
            step(tt(V(10), V(10), V(11), ADD))
            step(v.reciprocal(V(10), V(10)))
            step(v.tensor_scalar(V(11), V(8), 1.0, None, SUB))
            step(tt(V(12), V(11), lr, MUL))
            step(tt(V(13), V(9), li, MUL))
            step(tt(V(12), V(12), V(13), ADD))
            step(tt(V(12), V(12), V(10), MUL))
            step(tt(V(13), V(9), lr, MUL))
            step(tt(V(14), V(11), li, MUL))
            step(tt(V(13), V(13), V(14), SUB))
            step(tt(V(13), V(13), V(10), MUL))
            step(v.memset(BB[:].rearrange("p a b c -> p (a b c)"), 0.0))
            step(v.memset(CTl[:].rearrange("p a b c -> p (a b c)"), 0.0))
            dve.wait_ge(sem("s5_in"), 96)
            zr = V(12).unsqueeze(2).to_broadcast([P, NJ, 16])
            zi = V(13).unsqueeze(2).to_broadcast([P, NJ, 16])
            CB = K_tmp
            step(tt(BBt[:, 0], BRI[:, 0], zr, MUL))
            step(tt(BBt[:, 1], BRI[:, 1], zi, MUL))
            step(tt(CB[:, 0], BBt[:, 0], BBt[:, 1], SUB))
            step(tt(BBt[:, 0], BRI[:, 1], zr, MUL))
            step(tt(BBt[:, 1], BRI[:, 0], zi, MUL))
            step(tt(CB[:, 1], BBt[:, 0], BBt[:, 1], ADD))
            for b in range(4):
                for gi in range(2):
                    hp, cols = slice(64 * gi, 64 * gi + 64), slice(16 * (2 * b + gi), 16 * (2 * b + gi + 1))
                    for ri in range(2):
                        step(v.tensor_copy(BB[hp, ri, b::4, cols], CB[hp, ri, b::4, :]))
            step(v.memset(flag[:], 1.0), "s5_bb")
            step(v.tensor_copy(wpw[:, 0, 0], cs))
            step(v.tensor_copy(wpw[:, 0, 1], sn))
            for l in range(1, 10):
                c, s = wpw[:, l - 1, 0], wpw[:, l - 1, 1]
                step(tt(V(14), s, s, MUL))
                step(tt(V(15), c, c, MUL))
                step(tt(wpw[:, l, 0], V(15), V(14), SUB))
                step(stt(wpw[:, l, 1], c, 2.0, s, MUL, MUL))
            ar = V(8).unsqueeze(2).to_broadcast([P, NJ, NS])
            ai = V(9).unsqueeze(2).to_broadcast([P, NJ, NS])
            step(tt(inj[:, 0], st5[:, 0], ar, MUL))
            step(tt(inj_t[:], st5[:, 1], ai, MUL))
            step(tt(inj[:, 0], inj[:, 0], inj_t[:], SUB))
            step(tt(inj[:, 1], st5[:, 1], ar, MUL))
            step(tt(inj_t[:], st5[:, 0], ai, MUL))
            step(tt(inj[:, 1], inj[:, 1], inj_t[:], ADD))
            for q in range(4):
                dve.wait_ge(sem("bt_turned"), q + 1)
                step(v.tensor_copy(BTl[:, q // 2, 4 * (q % 2):4 * (q % 2) + 4, :].rearrange("p a b -> p (a b)"),
                                   pb[6 + q % 2][:, :]), "bt_ev")
            dve.wait_ge(sem("ct_turned"), 1)
            cps = pb[6].rearrange("p (r a c) -> p r a c", r=2, a=2)
            for b in range(4):
                for gi in range(2):
                    hp, cols = slice(64 * gi, 64 * gi + 64), slice(16 * (2 * b + gi), 16 * (2 * b + gi + 1))
                    step(v.tensor_copy(CTl[hp, 0, b::4, cols], cps[hp, 0, :, cols]))
                    step(v.tensor_scalar(CTl[hp, 1, b::4, cols], cps[hp, 1, :, cols], -1.0, None, MUL))
            step(v.memset(flag[:], 1.0), "ct_ev")
            dve.wait_ge(sem("z_ev"), 2 * G)
            for a in range(2):
                step(v.tensor_scalar(Y[:, a, :], U5[:, a, :], par("s5_d", a), None, MUL))
            for j in range(NJ):
                col = lambda x: x[:, j:j + 1]
                step(v.memset(tc[:, 0:1], 1.0))
                step(v.memset(ts[:, 0:1], 0.0))
                for l in range(10):
                    n = 1 << l
                    wr, wi = wpw[:, l, 0, j:j + 1], wpw[:, l, 1, j:j + 1]
                    step(v.tensor_scalar(tc[:, n:2 * n], ts[:, 0:n], wi, None, MUL))
                    step(v.tensor_scalar(ts[:, n:2 * n], tc[:, 0:n], wi, None, MUL))
                    step(stt(tc[:, n:2 * n], tc[:, 0:n], wr, tc[:, n:2 * n], MUL, SUB))
                    step(stt(ts[:, n:2 * n], ts[:, 0:n], wr, ts[:, n:2 * n], MUL, ADD))
                for x in (tc, ts):
                    step(v.tensor_copy(dec4(x[:, TP:T]), x[:, 0:LS].unsqueeze(1).to_broadcast([P, NS, LS])))
                step(v.memset(Mg, 0.0))
                step(v.tensor_scalar(Mg, Mg, col(mag), None, ADD))
                step(v.memset(dec4(Mg[:, TP:T])[:, :, 0], 0.0))
                dve.wait_ge(sem("e_ev"), 6 * (j + 1))
                for ri, e in enumerate((e0, e1)):
                    f = dec4(e[:, TP:T])[:, :, 0]
                    step(tt(f, f, inj[:, ri, j, :], ADD))
                step(tt(t0, e0, tc, MUL))
                step(tt(t1, e1, ts, MUL))
                step(tt(t0, t0, t1, ADD))
                step(tt(t1, e1, tc, MUL))
                step(tt(e0, e0, ts, MUL))
                step(tt(t1, t1, e0, SUB))
                step(v.tensor_tensor_scan(t0, Mg, t0, 0.0, MUL, ADD))
                step(v.tensor_tensor_scan(t1, Mg, t1, 0.0, MUL, ADD))
                step(tt(e0, t0, tc, MUL))
                step(tt(e1, t1, ts, MUL))
                step(tt(e0, e0, e1, SUB))
                step(tt(e1, t1, tc, MUL))
                step(tt(t0, t0, ts, MUL))
                step(tt(e1, e1, t0, ADD))
                for ri, e in enumerate((e0, e1)):
                    step(v.tensor_copy(ls5[:, ri, j, 0:1], e[:, TP - 1:TP]))
                    step(v.tensor_copy(ls5[:, ri, j, 1:], dec4(e[:, TP:T])[:, :, LS - 1]))
                step(v.memset(flag[:], 1.0), "s5_scanned")
                for g in range(G):
                    dve.wait_ge(sem("y5_done"), G * j + g + 1)
                    y = Y[:, j // 4, gcol(g)]
                    step(tt(y, pb[6 + (9 * j + 6 + g + 1) % 2][:, 0:GW], y, ADD), "y5_ev")
            for q in range(4):
                dve.wait_ge(sem("s5_lturned"), q + 1)
                src = pb[6 + (9 * NJ + q + 1) % 2][0:NSEQ, :].rearrange("p (j c) -> p j c", c=P)
                step(v.tensor_copy(s5out[0:NSEQ, 4 * (q % 2):4 * (q % 2) + 4, :, q // 2], src), "s5_rows")
            dve.wait_ge(sem("glu_ev"), 2 * G)
            step(tt(Y[:, 0, :], t0, e0, MUL))
            step(tt(Y[:, 1, :], t1, e1, MUL))
            dve.wait_ge(sem("s5_stored"), 32)
            dve.wait_ge(sem("z_ev"), 10 * G)
            cv = lambda x: x.rearrange("p (c t) -> p c t", t=HC)
            for t in range(2):
                if t:
                    dve.wait_ge(sem("hg_stored"), 64)
                q_, f_, v_, og = (ZH[:, i, t, :] for i in range(4))
                step(v.tensor_scalar(f_, f_, low[:, 3, t:t + 1], low[:, 0, t:t + 1], MUL, ADD))
                step(v.tensor_scalar(K0, f_, -1.0, 1.0, MUL, ADD))
                step(v.tensor_scalar(f_, f_, 1e-30, None, MAX))
                step(v.tensor_copy(Ht0, f_))
                step(v.memset(Ht1, 0.0))
                step(v.tensor_copy(cv(Ht1)[:, :, 0], cv(f_)[:, :, 0]))
                step(v.memset(cv(Ht0)[:, :, 0], 0.0))
                step(v.tensor_tensor_scan(HD, Ht0, Ht1, 0.0, MUL, ADD))
                for d in range(HC):
                    w = HC - d
                    kd = (K0, K1)[d % 2]
                    if d:
                        step(tt(cv(kd)[:, :, d:], cv((K1, K0)[d % 2])[:, :, d - 1:HC - 1], cv(f_)[:, :, d:], MUL))
                    step(v.tensor_copy(cv(HK)[:, :, HC - 1 - d], cv(kd)[:, :, HC - 1]))
                    if d >= 2:
                        dve.wait_ge(sem("att_done"), HC * t + d - 1)
                    step(tt(cv((Hp0, Hp1)[d % 2])[:, :, d:], cv(kd)[:, :, d:], cv(q_)[:, :, d:], MUL), "prod_ready")
                    if d:
                        lag_out(v, dve, step, tt, cv, t, d - 1, v_)
                lag_out(v, dve, step, tt, cv, t, HC - 1, v_)
                step(v.tensor_copy(chunk_decay[:], cv(HD)[:, :, HC - 1]))
                step(tt(HD, HD, q_, MUL))
                step(v.memset(Sx[:, 0, :], 0.0), "lags_done")
                step(v.memset(flag[:], 1.0), "hk_ready")
                dve.wait_ge(sem("hs_in"), 32 * (t + 1))
                mb = m16[:, :].unsqueeze(2).to_broadcast([P, 8, 64])
                for b in range(9):
                    dve.wait_ge(sem("tok_ev"), 9 * t + b + 1)
                    if 9 * t + b:
                        dve.wait_ge(sem("u_done"), 9 * t + b)
                    for hh in range(2):
                        vt = tok[:, b % 2, 1, 64 * hh:64 * hh + 64].unsqueeze(1).to_broadcast([P, 8, 64])
                        step(tt(Vblk[:, hh], vt, mb, MUL), "dve_step" if hh == 0 else "vblk_ready")
                    if b:
                        state_out(v, dve, step, stt, t, b - 1)
                state_out(v, dve, step, stt, t, 8)
                step(v.memset(flag[:], 1.0), "hg_states")
                dve.wait_ge(sem("oi_done"), t + 1)
                o3 = Ho.rearrange("p (g c) -> p g c", g=3)
                step(tt(o3, ps[:, 3:6, 0:384], o3, ADD), "oi_ev")
                dve.wait_ge(sem("hn_done"), t + 1)
                r3 = Hn.rearrange("p (g c) -> p g c", g=3)
                step(v.tensor_scalar(r3, ps[:, 0:3, 0:384], 1.0 / 64, RMS_EPS, MUL, ADD), "hn_ev")
                root(2 + t)
                step(stt(Ho, Ho, par("hg_norm", t), Hn, MUL, MUL))
                if t:
                    for k in range(3):
                        dve.wait_ge(sem(f"gate_saved{k}"), 16 * 24)
                y = Y[:, 6 + t, :]
                step(tt(y[:, 0:TP], Ho[:, 0:TP], og[:, 0:TP], MUL))
                step(tt(dec4(y[:, TP:T]), cv(Ho)[:, 64:, 0:LS], cv(og)[:, 64:, 0:LS], MUL), "hg_done")
            dve.wait_ge(sem("hg_stored"), 128)
            zcur = lambda z: (z[:, 1:1 + TP], z[:, 1 + TP:1065].rearrange("p (n t) -> p n t", t=LS + 1)[:, :, 1:])
            zprev = lambda z: (z[:, 0:TP], z[:, 1 + TP:1065].rearrange("p (n t) -> p n t", t=LS + 1)[:, :, 0:LS])
            pads = lambda x: (x[:, 0:16, :], x[:, 16:RN, 0:LS])
            flat = lambda x: (x[:, 0:TP], dec4(x[:, TP:T]))
            chunked = lambda x: (x[:, 0:TP].rearrange("p (c t) -> p c t", t=RCH), dec4(x[:, TP:T]))

            def mix(z, tile, tmp, dst, name):
                step(v.memset(z[:, 0:1], 0.0))
                sc = z[:, 1 + TP:1065].rearrange("p (n t) -> p n t", t=LS + 1)
                step(v.tensor_copy(sc[:, :, 0], shT[:, tile, :]))
                for o, a, b in zip(flat(tmp), zprev(z), zcur(z)):
                    step(tt(o, a, b, SUB))
                step(v.tensor_copy(shO[:, tile, 0:1], z[:, TP:TP + 1]))
                step(v.tensor_copy(shO[:, tile, 1:], sc[:, :, LS]), "sho_ready")
                for i, (o, a, b) in enumerate(zip(dst, flat(tmp), zcur(z))):
                    if len(o.shape) == 3 and len(a.shape) == 2:
                        a, b = (x.rearrange("p (c t) -> p c t", t=RCH) for x in (a, b))
                    step(stt(o, a, par("rw_mu", tile), b, MUL, ADD), name if i else "dve_step")

            dve.wait_ge(sem("z_ev"), 11 * G)
            mix(Z[0], 12, Kc, flat(Lx), "lora_mixed")
            for x in (ARp, Bp, Kp, Vp):
                n = 0 if len(x.shape) == 3 else 1
                dst = x[:, 16:RN].rearrange("p a b c -> p (a b c)") if n else x[:, 16:RN].rearrange("p a b -> p (a b)")
                step(v.memset(dst, 0.0))
            T1, T2, T3 = (z[:, 0:T] for z in Z[1:])
            pc = lambda i: ARp[:, :, i, :]
            for j in range(4):
                if j:
                    dve.wait_ge(sem("rw_stored"), 64 * j)
                dve.wait_ge(sem("sin_ev"), j + 1)
                dve.wait_ge(sem("z_ev"), (11 + 3 * (j + 1)) * G)
                mix(Z[1], j, C1, flat(Rc), "mixed")
                mix(Z[2], 4 + j, C1, flat(Kc), "mixed")
                mix(Z[3], 8 + j, C1, pads(Vp), "mixed")
                step(v.tensor_scalar(T3, Kc, par("rw_k_k", j), None, MUL), "kraw_ready")
                dve.wait_ge(sem("wl_ev"), j + 1)
                step(v.tensor_tensor_scan(C1, resets[:], T1, 0.0, MUL, ADD))
                step(tt(T1, C1, T1, SUB), "cums_ready")
                dve.wait_ge(sem("al_ev"), j + 1)
                dve.wait_ge(sem("sum_done"), 7 * j + 3)
                kn = three(Y[:, 2 + j, :])
                step(v.tensor_scalar(kn, bank3(0), 1e-24, None, MAX), "sum_ev")
                root(4 + 2 * j)
                step(stt(T3, T3, 2.0 ** 15, Y[:, 2 + j, :], MUL, MUL))
                dve.wait_ge(sem("decays"), 3 * (j + 1))
                for o, a, b in zip(pads(pc(0)), chunked(T3), chunked(T1)):
                    step(stt(o, a, -1.0, b, MUL, MUL))
                step(tt(T1, T3, T2, MUL))
                for o, a, b in zip(pads(Bp), chunked(T1), chunked(C1)):
                    step(tt(o, a, b, MUL))
                step(v.tensor_scalar(T2, T2, 1.0, par("rw_k_a", j), SUB, MUL))
                step(stt(Kc, T2, 1.0, Kc, ADD, MUL))
                for o, a, b in zip(pads(Kp), chunked(Kc), chunked(C1)):
                    step(tt(o, a, b, MUL))
                for o, a, b in zip(pads(pc(1)), chunked(Rc), chunked(C2)):
                    step(tt(o, a, b, MUL))
                step(v.tensor_copy(PC[:, 0:16], chunked(C2)[0][:, :, RCH - 1]))
                step(v.tensor_copy(PC[:, 16:RN], chunked(C2)[1][:, :, LS - 1]))
                step(stt(Rc, Rc, par("rw_r_k", j), Kc, MUL, MUL), "rk_ready")
                step(v.memset(S2[:, 0, :], 0.0), "pads_ready")
                dve.wait_ge(sem("sum_done"), 7 * j + 4)
                step(v.tensor_copy(three(T2), bank3(3)), "sum_ev")
                for a, b in zip(chunked(T2), pads(Vp)):
                    step(tt(a, a, b, MUL))
                for bt in range(3):
                    for half in range(2):
                        dve.wait_ge(sem("la_done"), 2 * (3 * j + bt) + half + 1)
                        step(tt(LA[:, 4 * half:4 * half + 4], pb[3 + half].rearrange("p (c a t) -> p c a t", c=4, a=2),
                                m_ar[:].unsqueeze(1).to_broadcast([P, 4, 2, RCH]), MUL), "la_ev")
                    for half in range(2):
                        dve.wait_ge(sem("ka_done"), 2 * (3 * j + bt) + half + 1)
                        step(tt(KA[:, 4 * half:4 * half + 4], pb[5 + half].rearrange("p (c a t) -> p c a t", c=4, a=2),
                                m_ar[:].unsqueeze(1).to_broadcast([P, 4, 2, RCH]), MUL), "ka_ev")
                    dve.wait_ge(sem("l_done"), 3 * j + bt + 1)
                    m8 = lambda m: m.unsqueeze(1).to_broadcast([P, 8, RCH])
                    step(tt(X[:], pb[7].rearrange("p (c t) -> p c t", c=8), m8(m_l0[:]), MUL), "l_ev")
                    step(tt(X[:], X[:], m8(idS[:]), ADD))
                    step(tt(XT[:], LA[:, :, 0, :], m8(m_lt[:, 0, :]), MUL))
                    step(tt(XT[:], XT[:], m8(idS[:]), ADD))
                    last = 5 if bt < 2 else 1
                    step(tt(LTm[:], LA[:, :, 0, :], m8(m_lt[:, 1, :]), MUL), "lt_ready")
                    for l in range(1, last + 1):
                        n = lt_count(j, bt, l)
                        if l < last:
                            dve.wait_ge(sem("yy_done"), 2 * n)
                            step(tt(LTm[:], LA[:, :, 0, :], m8(m_lt[:, l + 1, :]), MUL), "lt_ready")
                        for half in range(2):
                            hc = slice(4 * half, 4 * half + 4)
                            dve.wait_ge(sem("zt_done"), 2 * (n - 1) + half + 1)
                            zx = pb[2 + half][:, 0:256].rearrange("p (c t) -> p c t", c=4)
                            zt = pb[4 + half][:, 0:256].rearrange("p (c t) -> p c t", c=4)
                            step(tt(X[:, hc], zx, X[:, hc], ADD), "zx_ev")
                            step(tt(XT[:, hc], zt, XT[:, hc], ADD), "zt_ev")
                    if bt == 2:
                        n = STEPS * j + 16
                        f8 = lambda x: x.rearrange("p c t -> p (c t)")
                        step(v.memset(flag[:], 0.0), "s_ready")
                        dve.wait_ge(sem("g_done"), n + 1)
                        step(v.tensor_copy(f8(LTm[:]), pb[3]), "g_ev")
                        dve.wait_ge(sem("ub_done"), n + 1)
                        step(v.tensor_copy(f8(Yb[:]), pb[4]), "ub_ev")
                        dve.wait_ge(sem("ds_done"), n + 1)
                        step(tt(f8(Sout[:]), pb[5], f8(Sin[:]), ADD))
                        step(tt(Sout[:], Sout[:], PC[:, 16:RN].unsqueeze(2).to_broadcast([P, 8, RCH]), MUL), "ds_ev")
                    for c in range(8 if bt < 2 else 0):
                        ci = 8 * bt + c
                        n = STEPS * j + ci
                        S0 = S2[:, ci % 2, :]
                        S1 = S2[:, (ci + 1) % 2, :]
                        step(v.tensor_scalar(SPc, S0, PC[:, ci:ci + 1], None, MUL), "s_ready")
                        dve.wait_ge(sem("g_done"), n + 1)
                        step(v.tensor_copy(Gb, pb[3][:, 0:64]), "g_ev")
                        dve.wait_ge(sem("ub_done"), n + 1)
                        step(v.tensor_copy(Ub, pb[4][:, 0:64]), "ub_ev")
                        dve.wait_ge(sem("ds_done"), n + 1)
                        step(stt(S1, pb[5][:, 0:64], PC[:, ci:ci + 1], SPc, MUL, ADD), "ds_ev")
                    dve.wait_ge(sem("ry_done"), 3 * j + bt + 1)
                    y = Y[:, 2 + j, :]
                    src = pb[7].rearrange("p (c t) -> p c t", c=8)
                    if bt < 2:
                        step(v.tensor_copy(y[:, 512 * bt:512 * bt + 512], pb[7]), "ry_ev")
                    else:
                        step(v.tensor_copy(dec4(y[:, TP:T]), src[:, :, 0:LS]), "ry_ev")
                y = Y[:, 2 + j, :]
                dve.wait_ge(sem("sum_done"), 7 * j + 5)
                step(stt(three(C1), bank3(0), -1.0 / 64, three(y), MUL, ADD), "sum_ev")
                step(v.memset(SPc, 0.0), "centred")
                dve.wait_ge(sem("sum_done"), 7 * j + 6)
                step(v.tensor_scalar(three(Kc), bank3(3), 1.0 / 64, GN_EPS, MUL, ADD), "sum_ev")
                root(5 + 2 * j)
                step(tt(C1, C1, Kc, MUL))
                step(v.tensor_scalar(C1, C1, par("rw_ln_w", j), par("rw_ln_b", j), MUL, ADD))
                step(tt(C1, C1, T2, ADD))
                dve.wait_ge(sem("sum_done"), 7 * j + 7)
                step(tt(three(y), bank3(0), three(C1), MUL), "sum_ev")
                step(v.memset(SPc, 0.0), "rw_done")
            dve.wait_ge(sem("rw_stored"), 256)
            for n in range(KT):
                for br in range(3):
                    u = 3 * n + br
                    dve.wait_ge(sem("gemm_done"), signals[index[("lift", 0)]] + u + 1)
                    dve.wait_ge(sem(f"sg_in{br}"), 16 * (n + 1))
                    gt, lift = sg[:, br, :], bank3(3 * (u % 2))
                    if br == 0:
                        step(tt(three(MG[:, n, :]), lift, three(gt), MUL), "lift_ev")
                        step(v.memset(flag[:], 0.0), "sg_used")
                    else:
                        step(tt(three(gt), lift, three(gt), MUL), "lift_ev")
                        step(tt(MG[:, n, :], MG[:, n, :], gt, ADD), "sg_used")
                step(v.memset(flag[:], 0.0), "mg_ready")
            dve.wait_ge(sem("mod_rest"), 8)
            scales(1)

            res = [RING_OUT]

            def residual(base, gate):
                for m_ in range(KT):
                    for g in range(G):
                        b = res[0] % 6
                        res[0] += 1
                        dve.wait_ge(sem("gemm_done"), base + G * m_ + g + 1)
                        n = min(GW, TP - g * GW)
                        x = xT[:, m_, g * GW:g * GW + n]
                        gt = MOD[:, gate + m_, :]
                        ins = stt(x, pb[b][:, 0:n], gt[:, 0:1], x, MUL, ADD)
                        if n == GW:
                            step(ins, "res_ev")
                            continue
                        step(ins)
                        d = dec4(res_t[:])
                        step(tt(d, dec4(pb[b][:, n:GW]), gt[:, 1:].unsqueeze(2).to_broadcast([P, NS, LS]), MUL))
                        x = xT[:, m_, TP:T]
                        step(tt(x, x, res_t[:], ADD), "res_ev")

            dve.wait_ge(sem("x_ev"), 4 * XQ)
            residual(signals[index[("out", 0)]], 16)
            dve.wait_ge(sem("sh_stored"), 32)
            norm(1)
            for i in range(4):
                step(v.memset(Uab[i][:, 0:2], 0.0))
            step(v.memset(res_t[:, 0:1], 0.0), "u_zeroed")
            for half, (m0, m1) in enumerate(HALVES):
                for p in range(m0, m1):
                    for s in range(2):
                        q = 4 * (p // 2) + 2 * (p % 2) + s
                        dve.wait_ge(sem("u_in"), G * (q + 1))
                        if s == 0 and p >= 2:
                            dve.wait_ge(sem("gelu_done"), p - 1)
                        u = Uab[q % 4]
                        c = Cab[p % 2] if s == 0 else Cab[2]
                        dec = u[:, 2 + TP:UL].rearrange("p (n t) -> p n t", t=LS + 2)
                        ch = FT * s + p
                        for k in range(3):
                            wk = par(f"conv_w{k}", ch)
                            for o, src in ((c[:, 0:TP], u[:, k:k + TP]), (dec4(c[:, TP:T]), dec[:, :, k:k + LS])):
                                final = k == 2 and len(o.shape) == 3
                                if k == 0:
                                    ins = v.tensor_scalar(o, src, wk, par("conv_b", ch), MUL, ADD)
                                else:
                                    ins = stt(o, src, wk, o, MUL, ADD)
                                step(ins, "u_used" if final else "dve_step")
                        if s == 0:
                            step(v.memset(res_t[:, 0:1], 0.0), "conv_a")
                    dve.wait_ge(sem("gelu_done"), p + 1)
                    f = FFh[:, p - m0, :]
                    step(tt(f, f, Cab[2], MUL), "ff_ready")
                res[0] += 2 * (m1 - m0) * G
                residual(signals[index[("down", (m0, 0))]], 40)
            norm(2)


def build(nc, args):
    I = dict(zip(_INS, args[:len(_INS)]))
    O = dict(zip(("y_p", "y_s", "s5_p", "sh_p", "rw_p", "hg_p", "cv_p", "s5_s", "sh_s", "rw_s", "hg_s", "cv_s"),
                 args[len(_INS):]))
    trunk(nc, I, O)


_INS = ['x_prompt', 'x_sample', 'c_prompt', 'c_sample', 'state_s5', 'state_rwkv_shift', 'state_rwkv', 'state_hgrn',
        'state_ffn_conv', 'w_ada', 'b_ada', 'g_mix', 'g_ffn', 'w_in', 's5_lambda_re', 's5_lambda_im', 's5_log_dt',
        's5_b_re', 's5_b_im', 's5_c_re', 's5_c_im', 's5_d', 's5_w_glu', 's5_b_glu', 'rw_mu', 'rw_w0', 'rw_w2',
        'rw_a0', 'rw_a2', 'rw_g2', 'rw_k_k', 'rw_k_a', 'rw_r_k', 'rw_ln_w', 'rw_ln_b', 'hg_lb', 'hg_norm',
        'w_lift_a', 'w_lift_b', 'w_lift_c', 'w_out', 'w_up', 'conv_w', 'conv_b', 'w_down', 'final_g']
_OUTS = [((1, 1024, 1024), 'float32'), ((8, 4, 1024), 'float32'),
         ((1, 1, 16, 64, 2), 'float32'), ((1, 1, 1664), 'float32'), ((1, 1, 8, 64, 64), 'float32'),
         ((1, 1, 4, 64, 64), 'float32'), ((1, 1, 2, 5632), 'float32'),
         ((1, 8, 16, 64, 2), 'float32'), ((1, 8, 1664), 'float32'), ((1, 8, 8, 64, 64), 'float32'),
         ((1, 8, 4, 64, 64), 'float32'), ((1, 8, 2, 5632), 'float32')]


def kernel(**inputs):
    import numpy as _np
    import concourse.bacc as _bacc
    from concourse import mybir as _mybir
    from concourse.bass_utils import run_bass_kernel_spmd as _run

    nc = _bacc.Bacc("TRN2", target_bir_lowering=False, num_devices=1)
    arrays, args = {}, []
    for name in _INS:
        a = _np.ascontiguousarray(inputs[name])
        arrays[f"in_{name}_dram"] = a
        args.append(nc.dram_tensor(f"in_{name}_dram", a.shape, _mybir.dt.from_np(a.dtype), kind="ExternalInput").ap())
    for i, (shape, dtype) in enumerate(_OUTS):
        dt = _mybir.dt.from_np(_np.dtype(dtype))
        args.append(nc.dram_tensor(f"out_{i}_dram", shape, dt, kind="ExternalOutput").ap())
    build(nc, args)
    r = _run(nc, [arrays], core_ids=[0])
    return tuple(r.results[0][f"out_{i}_dram"] for i in range(len(_OUTS)))
```

```python
import math
from contextlib import ExitStack

import concourse.bass as bass
from concourse import mybir

F32 = mybir.dt.float32
BF16 = mybir.dt.bfloat16
ALU = mybir.AluOpType
ACT = mybir.ActivationFunctionType
MUL, ADD, SUB, MAX = ALU.mult, ALU.add, ALU.subtract, ALU.max

P = 128
D = 1024
KT = D // P
TP = 1024
NS, LS = 8, 4
TS = NS * LS
T = TP + TS
G, GW = 3, T // 3
NSEQ = 1 + NS
SW = 256
NJ = 8
RC = 1664
RT = RC // P
HW = 256
FF = 2816
FT = FF // P
HC = 16
HN = TP // HC + NS
HT = HN * HC
RCH = 64
RN = TP // RCH + NS
STEPS = TP // RCH + 1
LEVELS = 6
C_DECAY = math.exp(-0.5)
TWO_PI_HI = 6.28125
TWO_PI_LO = 2 * math.pi - 6.28125
ROUND = 12582912.0
PI_SAFE = 3.1415925
RMS_EPS = 1e-6
GN_EPS = 1e-5 * 64
RING_OUT = 10 * G + 8 + 4 * G + 13 * G
RING_UP = RING_OUT + 8 * G
N_SMALL = 26
HALVES = ((0, 12), (12, 22))

ROWS = (
    (("b_ada", 48), ("g_mix", 8), ("g_ffn", 8), ("final_g", 8), ("rw_mu", 13), ("rw_w0", 4), ("rw_a0", 4),
     ("rw_k_k", 4), ("rw_k_a", 4), ("rw_r_k", 4), ("rw_ln_w", 4), ("rw_ln_b", 4), ("hg_lb", 2), ("hg_norm", 2),
     ("s5_d", 2), ("s5_b_glu", 2)),
    (("s5_log_dt", 8), ("s5_lambda_re", 8), ("s5_lambda_im", 8), ("conv_b", 44), ("conv_w2", 44)),
    (("conv_w0", 44), ("conv_w1", 44)),
)


def gate_tiles(c):
    return (4 * c, 4) if c < 3 else (12 + 3 * (c - 3), 3)


def fill_parts(q):
    return [(m // KT, m % KT) for m in range(2 * KT * q // 10, 2 * KT * (q + 1) // 10)]


def weight_chunks():
    out = [("ada", c, 1) for c in range(4)]
    out += [("s5", 0, 2 * G), ("hg", 0, 4 * G), ("hg", 1, 4 * G)]
    out += [("ada", c, 1) for c in range(4, 12)]
    out += [("gate", 0, 4 * G)]
    out += [("gate", 1, 4 * G), ("gate", 2, 4 * G), ("lora", 0, G)]
    for j in range(4):
        out += [("rkv", j, 3 * G), ("gate", 3 + j, 3 * G)]
    out += [("lift", c, 12) for c in range(2)]
    out += [("out", c, 4 * G) for c in range(2)]
    for m0, m1 in HALVES:
        out += [("up", m, 4 * G) for m in range(m0, m1, 2)]
        out += [("down", (m0, c), 2 * G) for c in range(4)]
    return out


def trunk(nc, I, O):
    ctx = ExitStack()

    def sb(name, shape, dt=F32):
        return ctx.enter_context(nc.sbuf_tensor(name, shape, dt))

    with ctx:
        hT = sb("hT", [P, KT, T])
        Y = sb("Y", [P, KT, T])
        W = sb("W", [P, 2, 4096])
        PAR = sb("PAR", [P, 3, P])
        MOD = sb("MOD", [P, 48, NSEQ])
        GSC = sb("GSC", [P, 2, KT, NSEQ])
        csT = sb("csT", [P, KT, NSEQ])
        ident = sb("ident", [P, P])
        ones = sb("ones", [P, P])
        hones = sb("hones", [P, P])
        m_ar = sb("m_ar", [P, 2, RCH])
        m_lt = sb("m_lt", [P, LEVELS, RCH])
        m_l0 = sb("m_l0", [P, RCH])
        idS = sb("idS", [P, RCH])
        m16 = sb("m16", [P, 8])
        resets = sb("resets", [P, T], BF16)
        shT = sb("shT", [P, RT, NS])
        shO = sb("shO", [P, RT, NSEQ])
        st5 = sb("st5", [P, 2, NJ, NS])
        ls5 = sb("ls5", [P, 2, NJ, NSEQ])
        s5v = sb("s5v", [P, 24, NJ])
        wpw = sb("wpw", [P, 10, 2, NJ])
        inj = sb("inj", [P, 2, NJ, NS])
        inj_t = sb("inj_t", [P, NJ, NS])
        low = sb("low", [P, 4, 2])
        AR = 24220
        arena = sb("arena", [P, AR])

        def carve(off, *shape):
            n = math.prod(shape)
            assert off + n <= AR, (off, shape)
            a = arena[:, off:off + n]
            if len(shape) == 1:
                return a
            names = "abcd"[:len(shape)]
            return a.rearrange(f"p ({' '.join(names)}) -> p {' '.join(names)}", **dict(zip(names, shape)))

        ps = ctx.enter_context(nc.psum_tensor("ps", [P, 8, 512], F32))
        pb = [ps[:, i, :] for i in range(8)]

        sems = {}

        def sem(name):
            if name not in sems:
                sems[name] = ctx.enter_context(nc.semaphore(name))
            return sems[name]

        def par(name, j=0, n=1, lo=0, hi=P):
            for t, rows in enumerate(ROWS):
                at = 0
                for nm, k in rows:
                    if nm == name:
                        return PAR[lo:hi, t, at + j:at + j + n]
                    at += k
            raise KeyError(name)

        xT = carve(0, KT, T)
        xr = carve(8448, 2, D)
        sq = carve(10496, 2, T)
        rstd = carve(12608, T)
        rows = carve(14720, 3, P)
        crow = carve(15104, D)
        shrow = carve(16128, RC)
        s5row = carve(17792, 2048)
        U5 = carve(0, 2, T)
        ZH = carve(2112, 4, 2, HT)
        tc, ts = carve(11328, T), carve(12384, T)
        e0, e1, t0, t1 = (carve(13440 + T * i, T) for i in range(4))
        Mg = carve(17664, T)
        BTl = carve(18720, 2, NJ, P)
        CTl = carve(20768, 2, NJ, P)
        BB = carve(13440, 2, NJ, P)
        BRI = carve(22816, 2, NJ, 16)
        CRI = carve(23072, 2, 2, 2, 64)
        BBt = carve(23584, 2, NJ, 16)
        wglu = carve(17664, 2, SW)
        s5out = carve(18720, NJ, P, 2)
        K0, K1, Hp0, Hp1, Ht0, Ht1, Ho, HD, HK = (carve(11328 + HT * i, HT) for i in range(9))
        tok = carve(11328, 2, 2, P)
        Vblk = carve(11840, 2, 8, 64)
        Sx = carve(12864, 81, 64)
        assert 12864 + 81 * 64 <= 11328 + 6 * HT
        Z = [carve(1065 * i, 1065) for i in range(4)]
        ARp = carve(4260, RN, 2, RCH)
        Bp = carve(7332, RN, RCH)
        Kp = carve(8868, RN, RCH)
        Vp = carve(10404, RN, RCH)
        Rc, Kc, C1, C2 = (carve(11940 + T * i, T) for i in range(4))
        Vt, Bt, Kt_ = (carve(16164 + 512 * i, 8, RCH) for i in range(3))
        LA = carve(17700, 8, 2, RCH)
        KA = carve(18724, 8, 2, RCH)
        X, XT, Yb, LTm = (carve(19748 + 512 * i, 8, RCH) for i in range(4))
        Ub = carve(21860, RCH)
        S2 = carve(21924, 2, RCH)
        SPc = carve(22052, RCH)
        Sin = carve(22116, 8, RCH)
        Sout = carve(11940, 8, RCH)
        PC = carve(22628, RN)
        Lw = carve(22652, 512)
        Lx = carve(23164, T)
        SR = C1[:, 0:512].rearrange("p (a b) -> p a b", a=8)
        SO = C1[:, 0:576].rearrange("p (a b) -> p a b", a=9)
        MG = carve(10496, KT, T)
        sg = carve(18944, 3, T)
        shrow2 = carve(22464, RC)
        FFh = carve(10496, 12, T)
        Yf = Y[:, :, :].rearrange("p a b -> p (a b)")
        UL = 2 + TP + 6 * NS
        Uab = [Yf[:, UL * i:UL * (i + 1)] for i in range(4)]
        Cab = [Yf[:, 4 * UL + T * i:4 * UL + T * (i + 1)] for i in range(3)]
        crw = Yf[:, 7464:7976]
        cob = Yf[:, 7976:8048].rearrange("p (a b) -> p a b", a=4)
        cvr = carve(23168, 2, 512)
        yrow = carve(10496, 2, D)
        sq2, rstd2 = carve(18944, 2, T), carve(21056, T)
        sq3 = carve(21056, 2, T)

        chunks = weight_chunks()
        index = {(k, c): i for i, (k, c, _) in enumerate(chunks)}
        signals = [0]
        for _, _, n in chunks:
            signals.append(signals[-1] + n)

        w_in, w_up, w_down = I["w_in"][0], I["w_up"][0], I["w_down"][0]

        def wsrc(kind, c):
            if kind == "ada":
                return [(0, 8, 512, I["w_ada"][0][:, c * 512:(c + 1) * 512])]
            if kind == "s5":
                return [(0, 8, 256, w_in[:, 0:256])]
            if kind == "hg":
                return [(0, 8, 512, w_in[:, SW + RC + 512 * c:SW + RC + 512 * (c + 1)])]
            if kind == "lora":
                return [(0, 8, 128, w_in[:, SW + 1536:SW + RC])]
            if kind == "rkv":
                return [(1024 * b, 8, 128, w_in[:, SW + 512 * b + 128 * c:SW + 512 * b + 128 * (c + 1)])
                        for b in range(3)]
            if kind == "gate":
                t0, n = gate_tiles(c)
                g0 = SW + RC + 4 * HW + P * t0
                return [(0, 8, P * n, w_in[:, g0:g0 + P * n])]
            if kind == "lift":
                cs = slice(512 * c, 512 * (c + 1))
                return [(0, 2, 512, I["w_lift_a"][0][:, cs]), (1024, 4, 512, I["w_lift_b"][0][:, cs]),
                        (3072, 2, 512, I["w_lift_c"][0][:, cs])]
            if kind == "out":
                return [(0, 8, 512, I["w_out"][0][:, c * 512:(c + 1) * 512])]
            if kind == "up":
                return [(0, 8, 256, w_up[:, P * c:P * (c + 2)]), (2048, 8, 256, w_up[:, FF + P * c:FF + P * (c + 2)])]
            m0, q = c
            m1 = dict(HALVES)[m0]
            return [(0, m1 - m0, 256, w_down[P * m0:P * m1, 256 * q:256 * (q + 1)])]

        loads = []
        total = [0, 0]
        for i, (k, c, _) in enumerate(chunks):
            total[i % 2] += 16 * len(wsrc(k, c))
            loads.append(total[i % 2])

        def wslot(i, off, n, cols):
            return W[:, i % 2, off:off + n * cols].rearrange("p (k c) -> p k c", k=n)

        def gcol(g):
            return slice(g * GW, (g + 1) * GW)

        XQ = 9

        def xrows(i):
            return P if i < 8 else TS


        Hn = K0
        gst = [x[:, 0:T].rearrange("p (b t) -> p b t", b=3) for x in (Y[:, 7, :], Z[0])]
        gates = nc.dram_tensor("gates", [24, P, T], F32, kind="Internal").ap()
        fine, coarse = carve(22816, 2, NJ, 64), carve(23840, 2, NJ, 16)
        K_tmp = carve(17664, 2, NJ, 16)
        chunk_decay = sb("chunk_decay", [P, HN])
        res_t = sb("res_t", [P, TS])
        ldt = sb("ldt", [NJ, 2])
        pflag = sb("pflag", [P, 1])
        tables = ((tc, ts, Mg), (Y[:, 2, :], Y[:, 3, :], Y[:, 4, :]))
        LTbd, Ybd, XTbd = (x[:, 0:1024].rearrange("p (c a t) -> p c a t", c=8, a=2) for x in (C1, Z[1], Z[3]))
        flag = sb("flag", [P, 1])

        def lt_count(j, bt, l):
            return 11 * j + 5 * bt + l

        def hg_group(n):
            return 1 + n // 12, n % 12

        def tk_count(j, bt):
            return 11 * j + 4 * bt

        def lag_out(v, dve, step, tt, cv, t, d, v_):
            w, bs = HC - d, 3 * (d % 2)
            dve.wait_ge(sem("att_done"), HC * t + d + 1)
            att = ps[:, bs:bs + 3, 0:24 * w].rearrange("p g (c t) -> p g c t", t=w)
            vs = cv(v_)[:, :, 0:w].rearrange("p (g c) t -> p g c t", g=3)
            if d == 0:
                step(tt(cv(Ho).rearrange("p (g c) t -> p g c t", g=3), att, vs, MUL), "att_ev")
            else:
                tmp = cv(Ht0)[:, :, 0:w]
                step(tt(tmp.rearrange("p (g c) t -> p g c t", g=3), att, vs, MUL), "att_ev")
                step(tt(cv(Ho)[:, :, d:], cv(Ho)[:, :, d:], tmp, ADD))

        def state_out(v, dve, step, stt, t, b):
            dve.wait_ge(sem("u_done"), 9 * t + b + 1)
            for c in range(8):
                ci = 8 * b + c
                s, o = (Sx[:, ci], Sx[:, ci + 1]) if b < 8 else (Sx[:, 65 + c], Sx[:, 73 + c])
                step(stt(o, s, chunk_decay[:, ci:ci + 1], pb[b % 2][:, 64 * c:64 * c + 64], MUL, ADD),
                     "u_ev" if c == 7 else "dve_step")

        block = ctx.enter_context(nc.Block())

        @block.sync
        def _(sp):
            n_small = [0]

            def small(dst, src):
                n_small[0] += 1
                sp.dma_start(dst, src).then_inc(sem("small_in"), 16)

            def vec(a):
                while len(a.shape) > 1:
                    a = a[0] if a.shape[0] == 1 else a.rearrange("a b -> (a b)")
                return a.rearrange("(r c) -> r c", c=P)

            sp.wait_ge(sem("rows_zeroed"), 1)
            for t, rws in enumerate(ROWS):
                at = 0
                for nm, k in rws:
                    dst = rows[at:at + k, t, :]
                    if nm == "s5_log_dt":
                        sp.dma_start(ldt[:], I[nm][0].rearrange("(j g) -> j g", g=2)).then_inc(sem("ldt_in"), 16)
                    elif nm.startswith("conv_w"):
                        small(dst, I["conv_w"][0][int(nm[-1])].rearrange("(r c) -> r c", c=P))
                    else:
                        small(dst, vec(I[nm]))
                    at += k
            small(crow[0:1, :], I["c_prompt"])
            small(crow[1:NSEQ, :], I["c_sample"])
            small(shrow[0:NS, :], I["state_rwkv_shift"][0])
            small(s5row[0:NS, :], I["state_s5"][0].rearrange("n g p c -> n (g p c)"))
            assert n_small[0] == N_SMALL, n_small

            def load_x(base, i):
                src = I["x_prompt"][0][P * i:P * (i + 1), :] if i < 8 else I["x_sample"].rearrange("n t d -> (n t) d")
                sp.dma_start(xr[0:xrows(i), i % 2, :], src).then_inc(sem(f"x_in{i % 2}"), 16)

            def weights(i):
                k, c, _ = chunks[i]
                if i >= 2:
                    sp.wait_ge(sem("gemm_done"), signals[i - 1])
                for off, n, cols, src in wsrc(k, c):
                    sp.dma_start(wslot(i, off, n, cols), src.rearrange("(k p) c -> p k c", p=P))\
                        .then_inc(sem(f"w_in{i % 2}"), 16)

            for i in range(2):
                load_x(0, i)
            for i in range(2):
                weights(i)
            for i in range(2, XQ):
                sp.wait_ge(sem("x_turned"), i - 1)
                load_x(0, i)
            for i in range(2, index[("s5", 0)] + 1):
                weights(i)
            sp.wait_ge(sem("h_ready"), 1)
            for ri, nm in enumerate(("s5_b_re", "s5_b_im")):
                sp.dma_start(BRI[:, ri], I[nm][0].rearrange("(j g) p c -> (g p) j c", g=2)).then_inc(sem("s5_in"), 16)
            for ri, nm in enumerate(("s5_c_re", "s5_c_im")):
                src = I[nm][0].rearrange("(a g) c p -> (g c) a p", a=2)
                for dup in range(2):
                    sp.dma_start(CRI[:, ri, :, dup, :], src).then_inc(sem("s5_in"), 16)
            for i in range(index[("hg", 0)], index[("gate", 1)] + 1):
                weights(i)
            sp.wait_ge(sem("s5_scanned"), NJ)
            sp.dma_start(wglu, I["s5_w_glu"][0].rearrange("(k p) c -> p k c", p=P)).then_inc(sem("s5_in"), 16)
            weights(index[("gate", 2)])
            for t in range(2):
                sp.wait_ge(sem("lags_done"), t + 1)
                for h in range(2):
                    sp.dma_start(Sx[64 * h:64 * h + 64, 65:73, :],
                                 I["state_hgrn"][0][:, 2 * t + h].rearrange("n k v -> k n v")).then_inc(sem("hs_in"), 16)
                weights(index[(("lora", 0), ("rkv", 0))[t]])
            sp.wait_ge(sem("hg_done"), 2)
            sp.wait_ge(sem("hg_stored"), 128)
            for lo, hi, nm in ((0, 32, "rw_w2"), (32, 64, "rw_a2"), (64, 128, "rw_g2")):
                sp.dma_start(Lw[lo:hi, :], I[nm][0]).then_inc(sem("lw_in"), 16)
            for j in range(4):
                if j:
                    weights(index[("rkv", j)])
                    sp.wait_ge(sem("rw_stored"), 64 * j)
                for h in range(2):
                    sp.dma_start(SR[64 * h:64 * h + 64, :, :],
                                 I["state_rwkv"][0][:, 2 * j + h].rearrange("n v k -> v n k")).then_inc(sem("sr_in"), 16)
                weights(index[("gate", 3 + j)])
            for c in range(2):
                weights(index[("lift", c)])
            sp.wait_ge(sem("rw_done"), 4)
            for i in range(2):
                load_x(1, i)
            for i in range(2, XQ):
                sp.wait_ge(sem("x_turned"), XQ + i - 1)
                load_x(1, i)
            for k in range(3):
                sp.wait_ge(sem(f"gate_saved{k}"), 16 * 24)
            for u in range(3 * KT):
                if u >= 3:
                    sp.wait_ge(sem("sg_used"), u - 2)
                sp.dma_start(sg[:, u % 3, :], gates[KT * (u % 3) + u // 3]).then_inc(sem(f"sg_in{u % 3}"), 16)
            for i in range(index[("out", 0)], len(chunks)):
                k, c, _ = chunks[i]
                weights(i)
                if k == "up":
                    n = c // 2
                    if n:
                        sp.wait_ge(sem("conv_turned"), n)
                    for b in range(2):
                        sp.dma_start(crw[0:16, 256 * b:256 * b + 256],
                                     I["state_ffn_conv"][0][:, :, FF * b + P * c:FF * b + P * (c + 2)]
                                     .rearrange("n r c -> (n r) c")).then_inc(sem("conv_in"), 16)

        @block.gpsimd
        def _(pool):
            done = [0]

            def step(ins):
                done[0] += 1
                ins.then_inc(sem("pool_step"), 1)
                pool.wait_ge(sem("pool_step"), done[0])

            pool.memset(rows[:, :, :], 0.0).then_inc(sem("rows_zeroed"), 1)
            step(pool.memset(ones[:], 1.0))
            for m in (ident, hones, m_lt, m_l0, idS):
                step(pool.memset(m[:], 0.0))
            step(pool.memset(m_ar[:], 1.0))
            step(pool.memset(m16[:], 1.0))
            step(pool.memset(hones[0:64, 0:64], 1.0))
            step(pool.memset(hones[64:128, 64:128], 1.0))
            step(pool.affine_select(out=ident[:], in_=ident[:], compare_op=ALU.not_equal, fill=1.0, base=0,
                                    pattern=[[-1, P]], channel_multiplier=1))
            step(pool.affine_select(out=m16[:], in_=m16[:], compare_op=ALU.is_ge, fill=0.0, base=0,
                                    pattern=[[-16, 8]], channel_multiplier=1))
            step(pool.affine_select(out=m16[:], in_=m16[:], compare_op=ALU.is_ge, fill=0.0, base=15,
                                    pattern=[[16, 8]], channel_multiplier=-1))
            for h in range(2):
                hp = slice(64 * h, 64 * h + 64)
                step(pool.affine_select(out=idS[hp], in_=idS[hp], compare_op=ALU.not_equal, fill=1.0, base=0,
                                        pattern=[[-1, RCH]], channel_multiplier=1))
                step(pool.affine_select(out=m_ar[hp, 0], in_=m_ar[hp, 0], compare_op=ALU.is_gt, fill=0.0, base=0,
                                        pattern=[[1, RCH]], channel_multiplier=-1))
                step(pool.affine_select(out=m_ar[hp, 1], in_=m_ar[hp, 1], compare_op=ALU.is_ge, fill=0.0, base=0,
                                        pattern=[[1, RCH]], channel_multiplier=-1))
                v = m_l0[hp, :].rearrange("p (b i) -> p b i", i=2)[:, :, 0]
                step(pool.affine_select(out=v, in_=v, compare_op=ALU.not_equal, fill=1.0, base=-1,
                                        pattern=[[-2, RCH // 2]], channel_multiplier=1))
                for l in range(LEVELS):
                    B = 1 << l
                    v = m_lt[hp, l, :].rearrange("p (b i r) -> p b i r", i=2, r=B)[:, :, 1, :]
                    step(pool.memset(v, 1.0))
                    step(pool.affine_select(out=v, in_=v, compare_op=ALU.is_ge, fill=0.0, base=0,
                                            pattern=[[-2 * B, RCH // (2 * B)], [0, B]], channel_multiplier=1))
                    step(pool.affine_select(out=v, in_=v, compare_op=ALU.is_ge, fill=0.0, base=B - 1,
                                            pattern=[[2 * B, RCH // (2 * B)], [0, B]], channel_multiplier=-1))
            step(pool.memset(resets[:], 1.0))
            step(pool.memset(resets[:, 0:TP].rearrange("p (c t) -> p c t", t=RCH)[:, :, 0], 0.0))
            pool.memset(resets[:, TP:T].rearrange("p (c t) -> p c t", t=LS)[:, :, 0], 0.0)\
                .then_inc(sem("consts_ready"), 1)
            pool.wait_ge(sem("ldt_in"), 16)
            pool.tensor_copy(rows[0:NJ, 1, :].rearrange("p (g c) -> p g c", g=2),
                             ldt[:].unsqueeze(2).to_broadcast([NJ, 2, 64])).then_inc(sem("ldt_spread"), 1)
            pool.wait_ge(sem("wpw_ready"), 1)
            pool.wait_ge(sem("s5_bb"), 1)
            pool.wait_ge(sem("ct_turned"), 1)
            for tab, l0, levels in ((fine, 0, 6), (coarse, 6, 4)):
                c, s_ = tab[:, 0], tab[:, 1]
                pool.memset(c[:, :, 0], 1.0)
                step(pool.memset(s_[:, :, 0], 0.0))
                for l in range(levels):
                    n = 1 << l
                    wr, wi = (wpw[:, l0 + l, r, :].unsqueeze(2).to_broadcast([P, NJ, n]) for r in range(2))
                    pr = [Y[:, 5, 256 * q:256 * q + NJ * n].rearrange("p (j t) -> p j t", j=NJ) for q in range(4)]
                    for q, (x, w) in enumerate(((c, wr), (s_, wi), (s_, wr), (c, wi))):
                        m = pool.tensor_tensor(pr[q], x[:, :, 0:n], w, MUL)
                    step(m)
                    pool.tensor_tensor(c[:, :, n:2 * n], pr[0], pr[1], SUB)
                    step(pool.tensor_tensor(s_[:, :, n:2 * n], pr[2], pr[3], ADD))
            for j in range(NJ):
                ct, st, mg = tables[j % 2]
                if j >= 2:
                    pool.wait_ge(sem("s5_scanned"), j - 1)
                rows16 = lambda x: x.rearrange("p (a b) -> p a b", a=16)
                A = [coarse[:, r, j, :].unsqueeze(2).to_broadcast([P, 16, 64]) for r in range(2)]
                B = [fine[:, r, j, :].unsqueeze(1).to_broadcast([P, 16, 64]) for r in range(2)]
                sasb, casb = rows16(Y[:, 5, 0:TP]), rows16(Y[:, 6, 0:TP])
                pool.tensor_tensor(rows16(ct[:, 0:TP]), A[0], B[0], MUL)
                pool.tensor_tensor(sasb, A[1], B[1], MUL)
                pool.tensor_tensor(rows16(st[:, 0:TP]), A[1], B[0], MUL)
                step(pool.tensor_tensor(casb, A[0], B[1], MUL))
                pool.tensor_tensor(rows16(ct[:, 0:TP]), rows16(ct[:, 0:TP]), sasb, SUB)
                step(pool.tensor_tensor(rows16(st[:, 0:TP]), rows16(st[:, 0:TP]), casb, ADD))
                for x in (ct, st):
                    step(pool.tensor_copy(x[:, TP:T].rearrange("p (n t) -> p n t", t=LS),
                                          x[:, 0:LS].unsqueeze(1).to_broadcast([P, NS, LS])))
                step(pool.tensor_copy(mg, s5v[:, 5, j:j + 1].to_broadcast([P, T])))
                step(pool.memset(mg[:, TP:T].rearrange("p (n t) -> p n t", t=LS)[:, :, 0], 0.0))
                pool.memset(pflag[:], 0.0).then_inc(sem("tab_ready"), 1)
            stored = {}

            def out(name, dst, src):
                stored[name] = stored.get(name, 0) + 16
                pool.dma_start(dst, src).then_inc(sem(name), 16)

            pool.wait_ge(sem("s5_rows"), 4)
            flat = s5out.rearrange("p a b c -> p (a b c)")
            out("s5_stored", O["s5_p"].rearrange("l n g p c -> (l n) (g p c)"), flat[0:1, :])
            out("s5_stored", O["s5_s"].rearrange("l n g p c -> (l n) (g p c)"), flat[1:NSEQ, :])
            for t in range(2):
                pool.wait_ge(sem("hg_states"), t + 1)
                for h in range(2):
                    hp = slice(64 * h, 64 * h + 64)
                    out("hg_stored", O["hg_p"][0, 0, 2 * t + h], Sx[hp, 64, :])
                    out("hg_stored", O["hg_s"][0][:, 2 * t + h].rearrange("n k v -> k n v"), Sx[hp, 73:81, :])
            for j in range(4):
                pool.wait_ge(sem("pads_ready"), j + 1)
                for x in (LTbd, Ybd, XTbd):
                    m = pool.memset(x.rearrange("p c a t -> p (c a t)"), 0.0)
                m.then_inc(sem("bd_zeroed"), 1)
                pool.wait_ge(sem("bd_zeroed"), j + 1)
                for bt in range(3):
                    pool.wait_ge(sem("la_ev"), 5 * (3 * j + bt) + 2)
                    for l in range(1, (5 if bt < 2 else 1) + 1):
                        n = lt_count(j, bt, l)
                        if n > 1:
                            pool.wait_ge(sem("yy_done"), 2 * (n - 1))
                        for h in range(2):
                            hp = slice(64 * h, 64 * h + 64)
                            m = pool.tensor_tensor(LTbd[hp, :, h, :], LA[hp, :, 0, :],
                                                   m_lt[hp, l, :].unsqueeze(1).to_broadcast([64, 8, RCH]), MUL)
                        m.then_inc(sem("lt_ready"), 1)
                pool.wait_ge(sem("rw_rows"), 2 * (j + 1))
                for h in range(2):
                    hp = slice(64 * h, 64 * h + 64)
                    out("rw_stored", O["rw_p"][0, 0, 2 * j + h], SO[hp, 8, :])
                    out("rw_stored", O["rw_s"][0][:, 2 * j + h].rearrange("n v k -> v n k"), SO[hp, 0:8, :])
            pool.wait_ge(sem("sh_rows"), 4)
            out("sh_stored", O["sh_p"].rearrange("l n c -> (l n) c"), shrow2[0:1, :])
            out("sh_stored", O["sh_s"].rearrange("l n c -> (l n) c"), shrow2[1:NSEQ, :])
            for n in range(FT // 2):
                pool.wait_ge(sem("conv_rows"), n + 1)
                for b in range(2):
                    cs = slice(FF * b + 2 * P * n, FF * b + 2 * P * (n + 1))
                    src = cvr[:, n % 2, 256 * b:256 * b + 256]
                    out(f"conv_stored{n % 2}", O["cv_p"][0, 0][:, cs], src[0:2, :])
                    out(f"conv_stored{n % 2}", O["cv_s"][0][:, :, cs].rearrange("n r c -> (n r) c"), src[2:18, :])
            for i in range(XQ):
                pool.wait_ge(sem("y_rows"), 2 * (i + 1))
                dst = O["y_p"][0][P * i:P * (i + 1), :] if i < 8 else O["y_s"].rearrange("n t d -> (n t) d")
                out(f"y_stored{i % 2}", dst, yrow[0:xrows(i), i % 2, :])
            for name, n in stored.items():
                pool.wait_ge(sem(name), n)


        @block.tensor
        def _(pe):
            readers = {}
            last_read = {}

            def take(*banks):
                for b in banks:
                    if b in last_read:
                        pe.wait_ge(sem(last_read[b][0]), last_read[b][1])

            def give(name, *banks):
                readers[name] = readers.get(name, 0) + 1
                for b in banks:
                    last_read[b] = (name, readers[name])

            def mm(out, lhsT, rhs, start=True, stop=True):
                return nc.tensor.matmul(out, lhsT, rhs, start=start, stop=stop, skip_group_check=True)

            def turn(out, in_):
                n = in_.shape[0]
                return nc.tensor.transpose(out, in_, ident[0:n, 0:n])

            ring = [0]

            def gemm(w, c0, nk, rhs, reader):
                for g in range(G):
                    b = ring[0] % 6
                    ring[0] += 1
                    take(b)
                    for k in range(nk):
                        m = mm(pb[b][:, 0:GW], w[:, k, c0:c0 + P], rhs(k)[:, gcol(g)], k == 0, k == nk - 1)
                    m.then_inc(sem("gemm_done"), 1)
                    give(reader, b)

            def arrived(i):
                pe.wait_ge(sem(f"w_in{i % 2}"), loads[i])

            def gates_part(c, n, k0, k1, b=None):
                b = 6 + n % 2 if b is None else b
                if k0 == 0:
                    arrived(index[("gate", c)])
                    take(b)
                w8 = wslot(index[("gate", c)], 0, 8, P * gate_tiles(c)[1])
                for k in range(k0, k1):
                    m = mm(pb[b][:, 0:GW], w8[:, k, P * (n // G):P * (n // G + 1)], hT[:, k, gcol(n % G)],
                           k == 0, k == KT - 1)
                if k1 == KT:
                    m.then_inc(sem("gemm_done"), 1)
                    give("gate_ev", b)

            pe.wait_ge(sem("consts_ready"), 1)
            pe.wait_ge(sem("ldt_spread"), 1)
            pe.wait_ge(sem("small_in"), 16 * N_SMALL)
            for t in range(3):
                m = turn(pb[6][:, P * t:P * (t + 1)], rows[:, t, :])
            m.then_inc(sem("par_turned"), 1)
            give("par_ready", 6)
            for k in range(KT):
                m = turn(pb[7][:, NSEQ * k:NSEQ * (k + 1)], crow[0:NSEQ, P * k:P * (k + 1)])
            m.then_inc(sem("c_turned"), 1)
            give("cs_ready", 7)
            take(6)
            for k in range(RT):
                turn(pb[6][:, NS * k:NS * (k + 1)], shrow[0:NS, P * k:P * (k + 1)])
            for ri in range(2):
                for j in range(NJ):
                    m = turn(pb[6][:, 128 + NS * (NJ * ri + j):128 + NS * (NJ * ri + j + 1)],
                             s5row[0:NS, 256 * j + ri:256 * (j + 1):2])
            m.then_inc(sem("st_turned"), 1)
            give("st_ready", 6)

            def turn_x(base):
                for i in range(XQ):
                    n = xrows(i)
                    pe.wait_ge(sem(f"x_in{i % 2}"), 16 * (i // 2 + 1 + base * (5 - i % 2)))
                    for half in range(2):
                        b = 2 * (i % 3) + half
                        take(b)
                        for q in range(4):
                            k = 4 * half + q
                            m = turn(pb[b][:, P * q:P * q + n], xr[0:n, i % 2, P * k:P * (k + 1)])
                        if half == 0:
                            m.then_inc(sem("x_half"), 1)
                        else:
                            m.then_inc(sem("x_turned"), 1)
                        give("x_ev", b)

            turn_x(0)
            take(7)
            def ada(c, bank, t0):
                i = index[("ada", c)]
                arrived(i)
                w = wslot(i, 0, 8, 512)
                for q in range(4):
                    t = t0 + q
                    for k in range(KT):
                        m = mm(bank[:, NSEQ * t:NSEQ * (t + 1)], w[:, k, P * q:P * (q + 1)], csT[:, k, :],
                               k == 0, k == KT - 1)
                m.then_inc(sem("gemm_done"), 1)

            def norm(n):
                pe.wait_ge(sem("acc_ready"), n + 1)
                take(0, 1, 2)
                for g in range(G):
                    m = mm(pb[g][:, 0:GW], ones[:], (sq, sq2, sq3)[n][:, 1, gcol(g)])
                m.then_inc(sem("sq_done"), 1)
                give("rstd_ready", 0, 1, 2)

            for c in range(4):
                ada(c, pb[7], 4 * c)
                if c == 0:
                    norm(0)
            give("mod_ready", 7)

            pe.wait_ge(sem("h_ready"), 1)
            h = lambda k: hT[:, k, :]
            i = index[("s5", 0)]
            arrived(i)
            for t in range(2):
                gemm(wslot(i, 0, 8, 256), P * t, 8, h, "z_ev")
            pe.wait_ge(sem("s5_bb"), 1)
            for q in range(4):
                b = 6 + q % 2
                take(b)
                for r in range(4):
                    m = turn(pb[b][:, P * r:P * (r + 1)], BB[:, q // 2, 4 * (q % 2) + r, :])
                m.then_inc(sem("bt_turned"), 1)
                give("bt_ev", b)
            take(6)
            pe.wait_ge(sem("s5_in"), 16 * 6)
            for ri in range(2):
                for a in range(2):
                    m = turn(pb[6][:, P * (2 * ri + a):P * (2 * ri + a + 1)],
                             CRI[:, ri, a, :, :].rearrange("p a b -> p (a b)"))
            m.then_inc(sem("ct_turned"), 1)
            give("ct_ev", 6)
            for c in range(2):
                i = index[("hg", c)]
                arrived(i)
                for q in range(4):
                    gemm(wslot(i, 0, 8, 512), P * q, 8, h, "z_ev")
            pe.wait_ge(sem("bt_ev"), 4)
            pe.wait_ge(sem("z_ev"), 2 * G)
            misc = [0]

            def misc_bank():
                misc[0] += 1
                take(6 + misc[0] % 2)
                return 6 + misc[0] % 2

            for j in range(NJ):
                for g in range(G):
                    for ri in range(2):
                        b = misc_bank()
                        mm(pb[b][:, 0:GW], BTl[:, ri, j, :], U5[:, j // 4, gcol(g)]).then_inc(sem("e_done"), 1)
                        give("e_ev", b)
                if j < 4:
                    for c in (4 + 2 * j, 5 + 2 * j):
                        b = ring[0] % 6
                        ring[0] += 1
                        take(b)
                        ada(c, pb[b], 0)
                        give("mod_rest", b)
                else:
                    arrived(index[("gate", 0)])
                    gemm(wslot(index[("gate", 0)], 0, 8, 512), P * (j - 4), 8, h, "gate_ev")
                pe.wait_ge(sem("s5_scanned"), j + 1)
                for g in range(G):
                    b = misc_bank()
                    mm(pb[b][:, 0:GW], CTl[:, 0, j, :], e0[:, gcol(g)], True, False)
                    mm(pb[b][:, 0:GW], CTl[:, 1, j, :], e1[:, gcol(g)], False, True).then_inc(sem("y5_done"), 1)
                    give("y5_ev", b)
            for q in range(4):
                b = misc_bank()
                for r in range(4):
                    m = turn(pb[b][0:NSEQ, P * r:P * (r + 1)], ls5[:, q // 2, 4 * (q % 2) + r, :])
                m.then_inc(sem("s5_lturned"), 1)
                give("s5_rows", b)
            pe.wait_ge(sem("s5_in"), 16 * 7)
            pe.wait_ge(sem("gelu_ready"), 2)
            for m_ in range(2):
                for g in range(G):
                    b = misc_bank()
                    for k, x in enumerate((t0, t1)):
                        m = mm(pb[b][:, 0:GW], wglu[:, k, P * m_:P * (m_ + 1)], x[:, gcol(g)], k == 0, k == 1)
                    m.then_inc(sem("glu_done"), 1)
                    give("glu_ev", b)
            for t in range(2):
                for d in range(HC):
                    w, bs = HC - d, 3 * (d % 2)
                    pe.wait_ge(sem("prod_ready"), HC * t + d + 1)
                    take(bs, bs + 1, bs + 2)
                    src = (Hp0, Hp1)[d % 2].rearrange("p (c t) -> p c t", t=HC)
                    for q in range(3):
                        m = mm(pb[bs + q][:, 0:24 * w].rearrange("p (c t) -> p c t", t=w), hones[:],
                               src[:, 24 * q:24 * (q + 1), d:HC])
                    m.then_inc(sem("att_done"), 1)
                    give("att_ev", bs, bs + 1, bs + 2)
                    if d < 12 and d % 2 == 0:
                        gates_part(*hg_group(14 * t + d // 2), 0, KT)
                pe.wait_ge(sem("hk_ready"), t + 1)

                def tokens(b):
                    k = 6 + b % 2
                    take(k)
                    turn(pb[k][:, 0:P], HK[:, P * b:P * (b + 1)])
                    turn(pb[k][:, P:2 * P], ZH[:, 2, t, P * b:P * (b + 1)]).then_inc(sem("tok_done"), 1)
                    give("tok_ev", k)

                tokens(0)
                for b in range(9):
                    if b < 8:
                        tokens(b + 1)
                    pe.wait_ge(sem("vblk_ready"), 9 * t + b + 1)
                    take(b % 2)
                    for hh in range(2):
                        m = mm(pb[b % 2][64 * hh:64 * hh + 64, :], tok[:, b % 2, 0, 64 * hh:64 * hh + 64],
                               Vblk[:, hh, :, :].rearrange("p a b -> p (a b)"))
                    m.then_inc(sem("u_done"), 1)
                    give("u_ev", b % 2)
                    if b < 8:
                        gates_part(*hg_group(14 * t + 6 + b // 2), KT // 2 * (b % 2), KT // 2 * (b % 2 + 1), 2)
                pe.wait_ge(sem("hg_states"), t + 1)
                take(3, 4, 5)
                qd = HD.rearrange("p (c t) -> p c t", t=HC)
                for c in range(HN):
                    s = c if c < 64 else c + 1
                    for hh in range(2):
                        hp = slice(64 * hh, 64 * hh + 64)
                        m = mm(pb[3 + c // 24][hp, HC * (c % 24):HC * (c % 24 + 1)], Sx[hp, s, :], qd[hp, c, :])
                m.then_inc(sem("oi_done"), 1)
                give("oi_ev", 3, 4, 5)
                pe.wait_ge(sem("hsq_ready"), t + 1)
                take(0, 1, 2)
                for q in range(3):
                    m = mm(pb[q][:, 0:384], hones[:], HK[:, 384 * q:384 * (q + 1)])
                m.then_inc(sem("hn_done"), 1)
                give("hn_ev", 0, 1, 2)
                for n in range(10, 14 if t == 0 else 10):
                    gates_part(*hg_group(n), 0, KT)
            i = index[("lora", 0)]
            arrived(i)
            gemm(wslot(i, 0, 8, 128), 0, 8, h, "z_ev")

            def heads(fn):
                for hh in range(2):
                    m = fn(slice(64 * hh, 64 * hh + 64))
                return m

            for j in range(4):
                i = index[("rkv", j)]
                arrived(i)
                for q in range(3):
                    gemm(wslot(i, 1024 * q, 8, 128), 0, 8, h, "z_ev")
                pe.wait_ge(sem("sr_in"), 32 * (j + 1))
                take(6)
                for n in range(NS):
                    m = heads(lambda hp: mm(pb[6][hp, 64 * n:64 * n + 64], SR[hp, n, :], idS[hp, :]))
                m.then_inc(sem("sin_done"), 1)
                give("sin_ev", 6)
                pe.wait_ge(sem("lora_ready"), 2)
                pe.wait_ge(sem("lw_in"), 48)
                take(0, 1, 2, 3, 4, 5)
                for g in range(G):
                    m = mm(pb[g][:, 0:GW], Lw[0:32, P * j:P * (j + 1)], Lx[0:32, gcol(g)])
                m.then_inc(sem("sum_done"), 1)
                give("lora_ev", 0, 1, 2)
                for g in range(G):
                    m = mm(pb[3 + g][:, 0:GW], Lw[32:64, P * j:P * (j + 1)], Lx[32:64, gcol(g)])
                m.then_inc(sem("sum_done"), 1)
                give("lora_ev", 3, 4, 5)
                for n in range(2):
                    gates_part(3 + j, n, 0, KT)
                pe.wait_ge(sem("ksq_ready"), j + 1)
                take(0, 1, 2)
                for g in range(G):
                    m = mm(pb[g][:, 0:GW], hones[:], Y[:, 2 + j, gcol(g)])
                m.then_inc(sem("sum_done"), 1)
                give("sum_ev", 0, 1, 2)
                gates_part(3 + j, 2, 0, KT)
                pe.wait_ge(sem("rk_ready"), j + 1)
                take(3, 4, 5)
                for g in range(G):
                    m = mm(pb[3 + g][:, 0:GW], hones[:], Rc[:, gcol(g)])
                m.then_inc(sem("sum_done"), 1)
                give("sum_ev", 3, 4, 5)
                pe.wait_ge(sem("pads_ready"), j + 1)
                for bt in range(3):
                    for x, (b, src) in enumerate(((0, Vp), (1, Bp), (2, Kp))):
                        take(b)
                        for c in range(8):
                            m = heads(lambda hp: mm(pb[b][hp, 64 * c:64 * c + 64], src[hp, 8 * bt + c, :], idS[hp, :]))
                        m.then_inc(sem("tk_done"), 1)
                        give("tk_ev", b)
                    for half in range(2):
                        take(3 + half)
                        for q in range(4):
                            c = 8 * bt + 4 * half + q
                            m = heads(lambda hp: mm(pb[3 + half][hp, P * q:P * (q + 1)], Bp[hp, c, :],
                                                    ARp[hp, c, :, :].rearrange("p a b -> p (a b)")))
                        m.then_inc(sem("la_done"), 1)
                        give("la_ev", 3 + half)
                    for half in range(2):
                        take(5 + half)
                        for q in range(4):
                            c = 8 * bt + 4 * half + q
                            m = heads(lambda hp: mm(pb[5 + half][hp, P * q:P * (q + 1)], Kp[hp, c, :],
                                                    ARp[hp, c, :, :].rearrange("p a b -> p (a b)")))
                        m.then_inc(sem("la_done"), 1)
                        give("la_ev", 5 + half)
                    take(7)
                    for c in range(8):
                        m = heads(lambda hp: mm(pb[7][hp, 64 * c:64 * c + 64], ARp[hp, 8 * bt + c, 0, :],
                                                Bp[hp, 8 * bt + c, :]))
                    m.then_inc(sem("la_done"), 1)
                    give("la_ev", 7)
                    if bt < 2:
                        take(0)
                        for c in range(8):
                            m = heads(lambda hp: mm(pb[0][hp, 64 * c:64 * c + 64], ARp[hp, 8 * bt + c, 0, :], idS[hp, :]))
                        m.then_inc(sem("tk_done"), 1)
                        give("tk_ev", 0)
                    if bt == 2:
                        gates_part(3 + j, 7, 0, KT, 2)
                    last = 5 if bt < 2 else 1
                    for l in range(1, last + 1):
                        n = lt_count(j, bt, l)
                        pe.wait_ge(sem("lt_ready"), n)

                        def half_mm(b, lhsT, rhs, half):
                            for c in range(4 * half, 4 * half + 4):
                                m = mm(pb[b][:, 64 * (c % 4):64 * (c % 4) + 64],
                                       lhsT[:, c, :, :].rearrange("p a t -> p (a t)"), rhs[:, c, :])
                            return m

                        if l == 1:
                            pe.wait_ge(sem("x_init"), 3 * j + bt + 1)
                        for half in range(2):
                            if l > 1:
                                pe.wait_ge(sem("zx_ev"), 2 * (n - 2 - 3 * j - bt) + half + 1)
                            take(half)
                            half_mm(half, LTbd, X, half).then_inc(sem("yy_done"), 1)
                            give("yy_ev", half)
                        if bt < 2:
                            for f, k in fill_parts(2 * l - 2):
                                gates_part(3 + j, 3 + 2 * bt + f, k, k + 1)
                        if bt < 2 and l == last:
                            pe.wait_ge(sem("tk_ev"), tk_count(j, bt) + 4)
                            pe.wait_ge(sem("la_ev"), 5 * (3 * j + bt) + 4)
                            take(2)
                            for c in range(8):
                                m = heads(lambda hp: mm(pb[2][hp, 64 * c:64 * c + 64], KA[hp, c, 0, :], Vt[hp, c, :]))
                            m.then_inc(sem("wy_done"), 1)
                            give("wy_ev", 2)
                        for half in range(2):
                            pe.wait_ge(sem("yy_ev"), 2 * (n - 1) + half + 1)
                            if l > 1:
                                pe.wait_ge(sem("zt_ev"), 2 * (n - 2) + half + 1)
                            if l < last:
                                take(2 + half)
                                half_mm(2 + half, XTbd, Yb, half).then_inc(sem("zx_done"), 1)
                                give("zx_ev", 2 + half)
                            take(4 + half)
                            half_mm(4 + half, Ybd, XT, half).then_inc(sem("zt_done"), 1)
                            give("zt_ev", 4 + half)
                        if bt < 2:
                            for f, k in fill_parts(2 * l - 1):
                                gates_part(3 + j, 3 + 2 * bt + f, k, k + 1)
                    pe.wait_ge(sem("zt_ev"), 2 * lt_count(j, bt, last))
                    if bt < 2:
                        take(3)
                        for c in range(8):
                            m = heads(lambda hp: mm(pb[3][hp, 64 * c:64 * c + 64], LTm[hp, c, :], XT[hp, c, :]))
                        m.then_inc(sem("wy_done"), 1)
                        give("wy_ev", 3)
                    pe.wait_ge(sem("tk_ev"), tk_count(j, bt) + (4 if bt < 2 else 3))
                    pe.wait_ge(sem("la_ev"), 5 * (3 * j + bt) + 4)
                    take(7)
                    if bt == 2:
                        take(3, 4, 5)
                        n = STEPS * j + 16
                        pe.wait_ge(sem("s_ready"), j + 1)
                        for c in range(8):
                            def g8(hp):
                                o = pb[3][hp, 64 * c:64 * c + 64]
                                mm(o, ARp[hp, 16 + c, 0, :], Sin[hp, c, :], True, False)
                                return mm(o, KA[hp, c, 0, :], Vt[hp, c, :], False, True)
                            m = heads(g8)
                        m.then_inc(sem("g_done"), 1)
                        give("g_ev", 3)
                        gates_part(3 + j, 8, 0, KT // 2)
                        pe.wait_ge(sem("g_ev"), n + 1)
                        for c in range(8):
                            m = mm(pb[4][:, 64 * c:64 * c + 64], XTbd[:, c, :, :].rearrange("p a t -> p (a t)"), LTm[:, c, :])
                        m.then_inc(sem("ub_done"), 1)
                        give("ub_ev", 4)
                        gates_part(3 + j, 8, KT // 2, KT)
                        pe.wait_ge(sem("ub_ev"), j + 1)
                        for c in range(8):
                            def d8(hp):
                                o = pb[5][hp, 64 * c:64 * c + 64]
                                mm(o, Bt[hp, c, :], Yb[hp, c, :], True, False)
                                return mm(o, Kt_[hp, c, :], Vt[hp, c, :], False, True)
                            m = heads(d8)
                        m.then_inc(sem("ds_done"), 1)
                        give("ds_ev", 5)
                        for c in range(8):
                            def y8(hp):
                                o = pb[7][hp, 64 * c:64 * c + 64]
                                mm(o, Sin[hp, c, :], ARp[hp, 16 + c, 1, :], True, False)
                                mm(o, Yb[hp, c, :], LA[hp, c, 1, :], False, False)
                                return mm(o, Vt[hp, c, :], KA[hp, c, 1, :], False, True)
                            m = heads(y8)

                    def ahead(c):
                        bu, bd = (4, 6)[c % 2], (5, 1)[c % 2]
                        take(bu, bd)
                        mm(pb[bu][:, 0:64], XTbd[:, c, :, :].rearrange("p a t -> p (a t)"), X[:, c, :], True, False)
                        heads(lambda hp: mm(pb[bd][hp, 0:64], Kt_[hp, c, :], Vt[hp, c, :], True, False))

                    if bt < 2:
                        pe.wait_ge(sem("wy_ev"), 2 * (2 * j + bt) + 1)
                        ahead(0)
                        pe.wait_ge(sem("wy_ev"), 2 * (2 * j + bt) + 2)
                    for c in range(8 if bt < 2 else 0):
                        n = STEPS * j + 8 * bt + c
                        ci = 8 * bt + c
                        bu, bd = (4, 6)[c % 2], (5, 1)[c % 2]
                        S0 = S2[:, ci % 2, :]
                        if ci:
                            pe.wait_ge(sem("ds_ev"), n)
                        heads(lambda hp: mm(pb[bu][hp, 0:64], Yb[hp, c, :], S0[hp, :], False, True))\
                            .then_inc(sem("g_done"), 1)
                        give("g_ev", bu)

                        def y_state(hp):
                            o = pb[7][hp, 64 * c:64 * c + 64]
                            mm(o, S0[hp, :], ARp[hp, ci, 1, :], True, False)
                            return mm(o, Vt[hp, c, :], KA[hp, c, 1, :], False, False)
                        heads(y_state)
                        pe.wait_ge(sem("g_ev"), n + 1)
                        heads(lambda hp: mm(pb[bd][hp, 0:64], Bt[hp, c, :], Ub[hp, :], False, True))\
                            .then_inc(sem("ds_done"), 1)
                        give("ds_ev", bd)
                        m = heads(lambda hp: mm(pb[7][hp, 64 * c:64 * c + 64], Ub[hp, :], LA[hp, c, 1, :], False, True))
                        if c < 7:
                            ahead(c + 1)
                    m.then_inc(sem("ry_done"), 1)
                    give("ry_ev", 7)
                pe.wait_ge(sem("ry_ev"), 3 * (j + 1))
                take(0, 1, 2)
                for g in range(G):
                    m = mm(pb[g][:, 0:GW], hones[:], Y[:, 2 + j, gcol(g)])
                m.then_inc(sem("sum_done"), 1)
                give("sum_ev", 0, 1, 2)
                pe.wait_ge(sem("ds_ev"), STEPS * (j + 1))
                take(6, 7)
                for n in range(NS):
                    m = heads(lambda hp: mm(pb[6][hp, 64 * n:64 * n + 64], Sout[hp, n, :], idS[hp, :]))
                m.then_inc(sem("so_done"), 1)
                give("rw_rows", 6)
                heads(lambda hp: mm(pb[7][hp, 0:64], S2[hp, 0, :], idS[hp, :])).then_inc(sem("so_done"), 1)
                give("rw_rows", 7)
                pe.wait_ge(sem("ysq_ready"), j + 1)
                take(3, 4, 5)
                for g in range(G):
                    m = mm(pb[3 + g][:, 0:GW], hones[:], C2[:, gcol(g)])
                m.then_inc(sem("sum_done"), 1)
                give("sum_ev", 3, 4, 5)
                take(0, 1, 2)
                for g in range(G):
                    m = mm(pb[g][:, 0:GW], Lw[64:128, P * j:P * (j + 1)], Lx[64:128, gcol(g)])
                m.then_inc(sem("sum_done"), 1)
                give("sum_ev", 0, 1, 2)
            pe.wait_ge(sem("sho_ready"), RT)
            for b in range(4):
                take(b)
                for q in range(4 if b < 3 else 1):
                    m = turn(pb[b][0:NSEQ, P * q:P * (q + 1)], shO[:, 4 * b + q, :])
                m.then_inc(sem("sh_turned"), 1)
                give("sh_rows", b)
            turn_x(1)
            for n in range(KT):
                i = index[("lift", n // 4)]
                if n % 4 == 0:
                    arrived(i)
                for br, (off, nk, y0) in enumerate(((0, 2, 0), (1024, 4, 2), (3072, 2, 6))):
                    b = 3 * ((3 * n + br) % 2)
                    take(b, b + 1, b + 2)
                    w = wslot(i, off, nk, 512)
                    for g in range(G):
                        for k in range(nk):
                            m = mm(pb[b + g][:, 0:GW], w[:, k, P * (n % 4):P * (n % 4 + 1)], Y[:, y0 + k, gcol(g)],
                                   k == 0, k == nk - 1)
                    m.then_inc(sem("gemm_done"), 1)
                    give("lift_ev", b, b + 1, b + 2)
            pe.wait_ge(sem("mg_ready"), KT)
            for c in range(2):
                i = index[("out", c)]
                arrived(i)
                for q in range(4):
                    gemm(wslot(i, 0, 8, 512), P * q, 8, lambda k: MG[:, k, :], "res_ev")
            norm(1)
            pe.wait_ge(sem("h_ready"), 2)

            def last_rows(n):
                pe.wait_ge(sem("cob_ready"), n + 1)
                take(7)
                for q in range(4):
                    m = turn(pb[7][0:18, P * q:P * (q + 1)], cob[:, q, :])
                m.then_inc(sem("cob_turned"), 1)
                give("conv_rows", 7)

            for half, (m0, m1) in enumerate(HALVES):
                for mt_ in range(m0, m1, 2):
                    n = mt_ // 2
                    pe.wait_ge(sem("conv_in"), 32 * (n + 1))
                    take(6)
                    for q in range(4):
                        m = turn(pb[6][:, 16 * q:16 * q + 16], crw[0:16, P * q:P * (q + 1)])
                    m.then_inc(sem("conv_turned"), 1)
                    give("cst_ev", 6)
                    i = index[("up", mt_)]
                    arrived(i)
                    for q in range(2):
                        for s in range(2):
                            gemm(wslot(i, 2048 * s, 8, 256), P * q, 8, h, "u_in")
                    if n:
                        last_rows(n - 1)
                pe.wait_ge(sem("ff_ready"), m1)
                for c in range(4):
                    i = index[("down", (m0, c))]
                    arrived(i)
                    for q in range(2):
                        gemm(wslot(i, 0, m1 - m0, 256), P * q, m1 - m0, lambda k: FFh[:, k, :], "res_ev")
            last_rows(FT // 2 - 1)
            norm(2)
            pe.wait_ge(sem("h_ready"), 3)
            for i in range(XQ):
                n = xrows(i)
                for half in range(2):
                    b = 2 * (i % 3) + half
                    take(b)
                    for q in range(4):
                        k = 4 * half + q
                        m = turn(pb[b][0:n, P * q:P * (q + 1)], hT[:, k, P * i:P * i + n])
                    m.then_inc(sem("y_turned"), 1)
                    give("y_rows", b)

        @block.scalar
        def _(act):
            done = [0]

            def step(ins):
                done[0] += 1
                ins.then_inc(sem("act_step"), 1)
                act.wait_ge(sem("act_step"), done[0])

            def copy(out, in_):
                return nc.scalar.activation(out, in_, ACT.Copy)

            act.wait_ge(sem("c_turned"), 1)
            nc.scalar.activation(csT[:].rearrange("p a b -> p (a b)"), pb[7][:, 0:KT * NSEQ], ACT.Silu)\
                .then_inc(sem("cs_ready"), 1)

            def evac_x(base):
                for i in range(XQ):
                    n = xrows(i)
                    for half in range(2):
                        b = 2 * (i % 3) + half
                        act.wait_ge(sem("x_half" if half == 0 else "x_turned"), XQ * base + i + 1)
                        copy(xT[:, 4 * half:4 * half + 4, P * i:P * i + n],
                             pb[b][:, :].rearrange("p (q t) -> p q t", q=4)[:, :, 0:n]).then_inc(sem("x_ev"), 1)

            act.wait_ge(sem("par_ready"), 1)
            V = lambda k: s5v[:, k, :]
            step(nc.scalar.activation(V(0), par("s5_log_dt", 0, NJ), ACT.Exp))
            nc.scalar.copy(V(1), V(0)).then_inc(sem("dt_ready"), 1)
            act.wait_ge(sem("low_diff"), 1)
            nc.scalar.activation(low[:, 1], low[:, 0], ACT.Exp).then_inc(sem("low_exp"), 1)
            act.wait_ge(sem("angles_ready"), 1)
            nc.scalar.activation(V(5), V(2), ACT.Exp).then_inc(sem("s5_fn"), 1)
            nc.scalar.activation(V(6), V(3), ACT.Sin).then_inc(sem("s5_fn"), 1)
            nc.scalar.activation(V(7), V(4), ACT.Sin).then_inc(sem("s5_fn"), 1)
            evac_x(0)

            def root(buf, n, scale=1.0):
                act.wait_ge(sem("var_ready"), n)
                step(nc.scalar.activation(buf, buf, ACT.Ln, scale=scale))
                nc.scalar.activation(buf, buf, ACT.Exp, scale=-0.5).then_inc(sem("rs_ready"), 1)

            def norm(n):
                root(rstd if n == 0 else rstd2, (1, 12, 13)[n])
                if n == 2:
                    return
                act.wait_ge(sem("gsc_ready"), n + 1)
                for k in range(KT):
                    act.wait_ge(sem("xn_ready"), KT * n + k + 1)
                    nc.scalar.activation(hT[:, k, 0:TP], hT[:, k, 0:TP], ACT.Identity, scale=GSC[:, n, k, 0:1],
                                         bias=MOD[:, 24 * n + k, 0:1]).then_inc(sem("hp_ready"), 1)

            norm(0)
            ring = [0]
            z_n = [0]

            def z_evac(dst_of, fn, count):
                for g in range(G):
                    b = ring[0] % 6
                    ring[0] += 1
                    act.wait_ge(sem("gemm_done"), count + g + 1)
                    for ins in dst_of(g, pb[b], fn):
                        m = ins
                    m.then_inc(sem("z_ev"), 1)

            def compact(dst):
                def go(g, bank, fn):
                    yield nc.scalar.activation(dst[:, gcol(g)], bank[:, 0:GW], fn)
                return go

            def split(prompt, decode):
                def go(g, bank, fn):
                    n = min(GW, TP - g * GW)
                    yield nc.scalar.activation(prompt[:, g * GW:g * GW + n], bank[:, 0:n], fn)
                    if n < GW:
                        yield nc.scalar.activation(decode, bank[:, n:GW].rearrange("p (a b) -> p a b", b=LS), fn)
                return go

            base = signals[index[("s5", 0)]]
            act.wait_ge(sem("h_ready"), 1)
            for t in range(2):
                z_evac(compact(U5[:, t, :]), ACT.Copy, base + G * t)
            act.wait_ge(sem("zh_padded"), 1)
            base = signals[index[("hg", 0)]]
            for q, fn in enumerate((ACT.Silu, ACT.Sigmoid, ACT.Copy, ACT.Sigmoid)):
                for t in range(2):
                    z = ZH[:, q, t, :]
                    z_evac(split(z[:, 0:TP], z[:, TP:HT].rearrange("p (c t) -> p c t", t=HC)[:, :, 0:LS]), fn,
                           base + G * (2 * q + t))
            gate_n = [0]

            def beside_s5(j):
                if j < 4:
                    for c in (4 + 2 * j, 5 + 2 * j):
                        act.wait_ge(sem("gemm_done"), signals[index[("ada", c)] + 1])
                        bank = pb[ring[0] % 6]
                        ring[0] += 1
                        for q in range(4):
                            t = 4 * c + q
                            m = nc.scalar.activation(MOD[:, t, :], bank[:, NSEQ * q:NSEQ * (q + 1)], ACT.Identity,
                                                     bias=par("b_ada", t))
                        m.then_inc(sem("mod_rest"), 1)
                for g in range(G if j >= 4 else 0):
                    bank = pb[ring[0] % 6]
                    ring[0] += 1
                    save_gate(0, G * (j - 4) + g, bank)

            def save_gate(c, n, bank):
                u = gate_n[0]
                gate_n[0] += 1
                tile, g = gate_tiles(c)[0] + n // G, n % G
                stage = gst[0 if c < 3 else 1][:, u % 3, :]
                act.wait_ge(sem("gemm_done"), signals[index[("gate", c)]] + n + 1)
                if u >= 3:
                    act.wait_ge(sem(f"gate_saved{u % 3}"), 16 * (u // 3))
                nc.scalar.activation(stage, bank[:, 0:GW], ACT.Sigmoid).then_inc(sem("gate_ev"), 1)
                act.wait_ge(sem("gate_ev"), u + 1)
                act.dma_start(gates[tile, :, gcol(g)], stage).then_inc(sem(f"gate_saved{u % 3}"), 16)

            for j in range(NJ):
                if j:
                    beside_s5(j - 1)
                for g in range(G):
                    for ri in range(2):
                        act.wait_ge(sem("e_done"), 6 * j + 2 * g + ri + 1)
                        if j == 0:
                            act.wait_ge(sem("bt_ev"), 4)
                        copy((e0, e1)[ri][:, gcol(g)], pb[6 + (9 * j + 2 * g + ri + 1) % 2][:, 0:GW])\
                            .then_inc(sem("e_ev"), 1)
            beside_s5(NJ - 1)
            act.wait_ge(sem("y5_ev"), G * NJ)
            for a in range(2):
                nc.scalar.activation((t0, t1)[a], Y[:, a, :], ACT.Gelu_apprx_tanh).then_inc(sem("gelu_ready"), 1)
            for m_ in range(2):
                for g in range(G):
                    n = G * m_ + g
                    act.wait_ge(sem("glu_done"), n + 1)
                    nc.scalar.activation((e0, e1)[m_][:, gcol(g)], pb[6 + (9 * NJ + 4 + n + 1) % 2][:, 0:GW], ACT.Sigmoid,
                                         bias=par("s5_b_glu", m_)).then_inc(sem("glu_ev"), 1)
            for t in range(2):
                for u in range(14 * t, 14 * t + 6):
                    save_gate(*hg_group(u), pb[6 + u % 2])
                for b in range(9):
                    act.wait_ge(sem("tok_done"), 9 * t + b + 1)
                    if b >= 2:
                        act.wait_ge(sem("u_done"), 9 * t + b - 1)
                    copy(tok[:, b % 2, :, :].rearrange("p a b -> p (a b)"), pb[6 + b % 2][:, 0:2 * P])\
                        .then_inc(sem("tok_ev"), 1)
                    if b >= 2 and b % 2 == 0:
                        save_gate(*hg_group(14 * t + 5 + b // 2), pb[2])
                act.wait_ge(sem("oi_ev"), t + 1)
                nc.scalar.activation(HK, Ho, ACT.Square).then_inc(sem("hsq_ready"), 1)
                root(Hn, 2 + t)
                for u in range(10, 14 if t == 0 else 10):
                    save_gate(*hg_group(u), pb[6 + u % 2])
            act.wait_ge(sem("hg_done"), 2)
            act.wait_ge(sem("hg_stored"), 128)

            def zplace(z):
                return split(z[:, 1:1 + TP], z[:, 1 + TP:1065].rearrange("p (n t) -> p n t", t=LS + 1)[:, :, 1:])

            z_evac(zplace(Z[0]), ACT.Copy, signals[index[("lora", 0)]])
            act.wait_ge(sem("lora_mixed"), 1)
            nc.scalar.activation(Lx[0:32, :], Lx[0:32, :], ACT.Tanh).then_inc(sem("lora_ready"), 1)
            nc.scalar.activation(Lx[64:128, :], Lx[64:128, :], ACT.Sigmoid).then_inc(sem("lora_ready"), 1)
            bank3 = lambda b: ps[:, b:b + 3, 0:GW]
            three = lambda x: x[:, 0:T].rearrange("p (g t) -> p g t", g=G)
            T1, T2, T3 = (z[:, 0:T] for z in Z[1:])
            for j in range(4):
                if j:
                    act.wait_ge(sem("rw_done"), j)
                for q in range(3):
                    z_evac(zplace(Z[1 + q]), ACT.Copy, signals[index[("rkv", j)]] + G * q)
                act.wait_ge(sem("sin_done"), j + 1)
                copy(Sin[:].rearrange("p a b -> p (a b)"), pb[6][:, :]).then_inc(sem("sin_ev"), 1)
                act.wait_ge(sem("mixed"), 3 * (j + 1))
                act.wait_ge(sem("sum_done"), 7 * j + 1)
                nc.scalar.activation(three(T1), bank3(0), ACT.Sigmoid, bias=par("rw_w0", j)).then_inc(sem("lora_ev"), 1)
                act.wait_ge(sem("sum_done"), 7 * j + 2)
                nc.scalar.activation(three(T2), bank3(3), ACT.Sigmoid, bias=par("rw_a0", j)).then_inc(sem("lora_ev"), 1)
                act.wait_ge(sem("kraw_ready"), j + 1)
                nc.scalar.activation(Y[:, 2 + j, :], T3, ACT.Square).then_inc(sem("ksq_ready"), 1)
                act.wait_ge(sem("cums_ready"), j + 1)
                nc.scalar.activation(C2, C1, ACT.Exp, scale=-C_DECAY).then_inc(sem("decays"), 1)
                act.wait_ge(sem("decays"), 3 * j + 1)
                nc.scalar.activation(C1, C1, ACT.Exp, scale=C_DECAY).then_inc(sem("decays"), 1)
                nc.scalar.activation(T1, T1, ACT.Exp, scale=-C_DECAY).then_inc(sem("decays"), 1)
                root(Y[:, 2 + j, :], 4 + 2 * j, 2.0 ** 30)
                for n in range(3):
                    save_gate(3 + j, n, pb[6 + n % 2])
                act.wait_ge(sem("bd_zeroed"), j + 1)
                for bt in range(3):
                    for x, dst in enumerate((Vt, Bt, Kt_, LTm)[0:4 if bt < 2 else 3]):
                        act.wait_ge(sem("tk_done"), tk_count(j, bt) + x + 1)
                        copy(dst[:].rearrange("p a b -> p (a b)"), pb[x % 3][:, :]).then_inc(sem("tk_ev"), 1)
                    for l in range(1, (5 if bt < 2 else 1) + 1):
                        for half in range(2):
                            act.wait_ge(sem("yy_done"), 2 * (lt_count(j, bt, l) - 1) + half + 1)
                            hc = slice(4 * half, 4 * half + 4)
                            copy(Yb[:, hc].rearrange("p a b -> p (a b)"), pb[half][:, 0:256])
                            for h in range(2):
                                hp = slice(64 * h, 64 * h + 64)
                                m = copy(Ybd[hp, hc, h, :], pb[half][hp, 0:256].rearrange("p (c t) -> p c t", c=4))
                            m.then_inc(sem("yy_ev"), 1)
                        if bt == 2:
                            save_gate(3 + j, 7, pb[2])
                            save_gate(3 + j, 8, pb[6])
                        for n, k in fill_parts(2 * l - 2) + fill_parts(2 * l - 1) if bt < 2 else ():
                            if k == KT - 1:
                                save_gate(3 + j, 3 + 2 * bt + n, pb[6 + (3 + 2 * bt + n) % 2])
                    for x in range(2 if bt < 2 else 0):
                        act.wait_ge(sem("wy_done"), 2 * (2 * j + bt) + x + 1)
                        copy((X, Yb)[x][:].rearrange("p a b -> p (a b)"), pb[2 + x][:, :]).then_inc(sem("wy_ev"), 1)
                act.wait_ge(sem("centred"), j + 1)
                nc.scalar.activation(C2, C1, ACT.Square).then_inc(sem("ysq_ready"), 1)
                root(Kc, 5 + 2 * j)
                act.wait_ge(sem("rw_done"), j + 1)
                act.wait_ge(sem("so_done"), 2 * (j + 1))
                copy(SO[:, 0:8, :].rearrange("p a b -> p (a b)"), pb[6][:, :]).then_inc(sem("rw_rows"), 1)
                copy(SO[:, 8, :], pb[7][:, 0:64]).then_inc(sem("rw_rows"), 1)
            for b in range(4):
                act.wait_ge(sem("sh_turned"), b + 1)
                n = 512 if b < 3 else P
                copy(shrow2[0:NSEQ, 512 * b:512 * b + n], pb[b][0:NSEQ, 0:n]).then_inc(sem("sh_rows"), 1)
            for k in range(3):
                act.wait_ge(sem(f"gate_saved{k}"), 16 * 24)
            evac_x(1)
            norm(1)

            def rows_out(n):
                act.wait_ge(sem("cob_turned"), n + 1)
                if n >= 2:
                    act.wait_ge(sem(f"conv_stored{n % 2}"), 64 * (n // 2))
                copy(cvr[0:18, n % 2, :], pb[7][0:18, :]).then_inc(sem("conv_rows"), 1)

            act.wait_ge(sem("u_zeroed"), 1)
            ring[0] = RING_UP
            for mt_ in range(0, FT, 2):
                n = mt_ // 2
                half = 0 if mt_ < HALVES[0][1] else 1
                if mt_ == HALVES[1][0]:
                    ring[0] += 8 * G
                act.wait_ge(sem("conv_turned"), n + 1)
                for q in range(4):
                    src = (q % 2) * 2 + q // 2
                    if n:
                        act.wait_ge(sem("u_used"), 4 * n + q - 3)
                    u = Uab[q]
                    dec = u[:, 2 + TP:UL].rearrange("p (n t) -> p n t", t=LS + 2)
                    m = copy(dec[:, :, 0:2], pb[6][:, 16 * src:16 * src + 16].rearrange("p (n r) -> p n r", r=2))
                    if q == 3:
                        m.then_inc(sem("cst_ev"), 1)
                    z0 = signals[index[("up", mt_)]] + G * q
                    for g in range(G):
                        b = ring[0] % 6
                        ring[0] += 1
                        act.wait_ge(sem("gemm_done"), z0 + g + 1)
                        k = min(GW, TP - g * GW)
                        m = copy(u[:, 2 + g * GW:2 + g * GW + k], pb[b][:, 0:k])
                        if k < GW:
                            m = copy(dec[:, :, 2:], pb[b][:, k:GW].rearrange("p (n t) -> p n t", t=LS))
                        m.then_inc(sem("u_in"), 1)
                    if q % 2:
                        p = 2 * n + q // 2
                        if p == HALVES[1][0]:
                            act.wait_ge(sem("res_ev"), 16 * G)
                        act.wait_ge(sem("conv_a"), p + 1)
                        nc.scalar.activation(FFh[:, p - (0 if p < HALVES[0][1] else HALVES[1][0]), :], Cab[p % 2],
                                             ACT.Gelu_apprx_tanh).then_inc(sem("gelu_done"), 1)
                act.wait_ge(sem("u_in"), G * 4 * (n + 1))
                if n:
                    rows_out(n - 1)
                    act.wait_ge(sem("cob_turned"), n)
                for q in range(4):
                    src = (q % 2) * 2 + q // 2
                    u = Uab[q]
                    dec = u[:, 2 + TP:UL].rearrange("p (n t) -> p n t", t=LS + 2)
                    copy(cob[:, src, 0:2], u[:, TP:TP + 2])
                    m = copy(cob[:, src, 2:18].rearrange("p (n r) -> p n r", r=2), dec[:, :, 4:6])
                m.then_inc(sem("cob_ready"), 1)
                act.wait_ge(sem("cob_ready"), n + 1)
            rows_out(FT // 2 - 1)
            norm(2)
            for i in range(XQ):
                n = xrows(i)
                if i >= 2:
                    act.wait_ge(sem(f"y_stored{i % 2}"), 16 * (i // 2))
                for half in range(2):
                    act.wait_ge(sem("y_turned"), 2 * i + half + 1)
                    copy(yrow[0:n, i % 2, 512 * half:512 * half + 512], pb[2 * (i % 3) + half][0:n, :])\
                        .then_inc(sem("y_rows"), 1)

        @block.vector
        def _(dve):
            counts = {}
            v = nc.vector

            def step(ins, name="dve_step"):
                counts[name] = counts.get(name, 0) + 1
                ins.then_inc(sem(name), 1)

                dve.wait_ge(sem(name), counts[name])

            bank3 = lambda b: ps[:, b:b + 3, 0:GW]
            three = lambda x: x[:, 0:T].rearrange("p (g t) -> p g t", g=G)
            dec4 = lambda x: x.rearrange("p (n t) -> p n t", t=LS)

            def tt(out, a, b, op):
                return v.tensor_tensor(out, a, b, op)

            def stt(out, a, s, b, op0, op1):
                return v.scalar_tensor_tensor(out=out, in0=a, scalar=s, in1=b, op0=op0, op1=op1)

            dve.wait_ge(sem("par_turned"), 1)
            step(v.tensor_copy(PAR[:].rearrange("p a b -> p (a b)"), pb[6][:, 0:384]), "par_ready")
            dve.wait_ge(sem("st_turned"), 1)
            step(v.tensor_copy(shT[:].rearrange("p a b -> p (a b)"), pb[6][:, 0:RT * NS]))
            step(v.tensor_copy(st5[:].rearrange("p a b c -> p (a b c)"), pb[6][:, 128:256]), "st_ready")
            V = lambda k: s5v[:, k, :]
            lr, li = par("s5_lambda_re", 0, NJ), par("s5_lambda_im", 0, NJ)
            dve.wait_ge(sem("dt_ready"), 1)
            step(tt(V(8), li, V(0), MUL))
            step(v.tensor_scalar(V(9), V(8), math.pi / 2, None, ADD))
            for src, dst, tmp in ((8, 3, 10), (9, 4, 11)):
                step(v.tensor_scalar(V(tmp), V(src), 1 / (2 * math.pi), ROUND, MUL, ADD))
                step(v.tensor_scalar(V(tmp), V(tmp), ROUND, None, SUB))
                step(stt(V(12), V(tmp), -TWO_PI_HI, V(src), MUL, ADD))
                step(stt(V(12), V(tmp), -TWO_PI_LO, V(12), MUL, ADD))
                step(v.tensor_scalar(V(dst), V(12), PI_SAFE, -PI_SAFE, ALU.min, MAX))
            step(tt(V(2), lr, V(0), MUL), "angles_ready")
            lb = par("hg_lb", 0, 2)
            step(tt(low[:, 0], lb, lb, SUB), "low_diff")
            dve.wait_ge(sem("low_exp"), 1)
            step(v.reciprocal(low[:, 2], low[:, 1]))
            step(tt(low[:, 2], low[:, 1], low[:, 2], MUL))
            step(tt(low[:, 0], low[:, 2], low[:, 2], SUB))
            step(v.tensor_scalar(low[:, 3], low[:, 0], -1.0, 1.0, MUL, ADD))
            def scales(n):
                gb = par(("g_mix", "g_ffn")[n], 0, KT).unsqueeze(2).to_broadcast([P, KT, NSEQ])
                step(stt(GSC[:, n], MOD[:, 24 * n + 8:24 * n + 16, :], 1.0, gb, ADD, MUL), "gsc_ready")

            def root(n):
                step(v.memset(flag[:], 0.0), "var_ready")
                dve.wait_ge(sem("rs_ready"), n)

            def squares(n, k):
                one, acc = (sq, sq2, sq3)[n][:, 0, :], (sq, sq2, sq3)[n][:, 1, :]
                x = xT[:, k, :]
                step(tt(one if k else acc, x, x, MUL))
                if k:
                    step(tt(acc, acc, one, ADD), "acc_ready" if k == KT - 1 else "dve_step")

            def normed(n):
                rs = rstd if n == 0 else rstd2
                dve.wait_ge(sem("sq_done"), n + 1)
                step(v.tensor_scalar(three(rs), bank3(0), 1.0 / D, RMS_EPS, MUL, ADD), "rstd_ready")
                root((1, 12, 13)[n])
                for k in range(KT):
                    if n == 2:
                        step(stt(hT[:, k, :], xT[:, k, :], par("final_g", k), rs, MUL, MUL))
                    else:
                        step(tt(hT[:, k, :], xT[:, k, :], rs, MUL), "xn_ready")

            def shifted(n):
                for k in range(KT):
                    d = dec4(hT[:, k, TP:T])
                    step(tt(d, d, GSC[:, n, k, 1:].unsqueeze(2).to_broadcast([P, NS, LS]), MUL))
                    step(tt(d, d, MOD[:, 24 * n + k, 1:].unsqueeze(2).to_broadcast([P, NS, LS]), ADD))
                dve.wait_ge(sem("hp_ready"), KT * (n + 1))
                step(v.memset(flag[:], 0.0), "h_ready")

            dve.wait_ge(sem("x_ev"), 2 * XQ)
            for k in range(KT):
                squares(0, k)
            normed(0)
            dve.wait_ge(sem("gemm_done"), 4)
            b_ada = par("b_ada", 0, 16).unsqueeze(2).to_broadcast([P, 16, NSEQ])
            step(tt(MOD[:, 0:16], pb[7][:, 0:16 * NSEQ].rearrange("p (a b) -> p a b", b=NSEQ), b_ada, ADD), "mod_ready")

            scales(0)
            shifted(0)
            dve.wait_ge(sem("h_ready"), 1)
            for q in range(4):
                for t in range(2):
                    z = ZH[:, q, t, TP:HT].rearrange("p (c t) -> p c t", t=HC)[:, :, LS:]
                    step(v.memset(z, 1.0 if q == 1 else 0.0))
            step(v.memset(flag[:], 1.0), "zh_padded")
            dve.wait_ge(sem("s5_fn"), 3)
            mag, sn, cs = V(5), V(6), V(7)
            step(tt(V(8), mag, cs, MUL))
            step(tt(V(9), mag, sn, MUL))
            step(tt(V(10), lr, lr, MUL))
            step(tt(V(11), li, li, MUL))
            step(tt(V(10), V(10), V(11), ADD))
            step(v.reciprocal(V(10), V(10)))
            step(v.tensor_scalar(V(11), V(8), 1.0, None, SUB))
            step(tt(V(12), V(11), lr, MUL))
            step(tt(V(13), V(9), li, MUL))
            step(tt(V(12), V(12), V(13), ADD))
            step(tt(V(12), V(12), V(10), MUL))
            step(tt(V(13), V(9), lr, MUL))
            step(tt(V(14), V(11), li, MUL))
            step(tt(V(13), V(13), V(14), SUB))
            step(tt(V(13), V(13), V(10), MUL))
            step(v.memset(BB[:].rearrange("p a b c -> p (a b c)"), 0.0))
            step(v.memset(CTl[:].rearrange("p a b c -> p (a b c)"), 0.0))
            dve.wait_ge(sem("s5_in"), 96)
            zr = V(12).unsqueeze(2).to_broadcast([P, NJ, 16])
            zi = V(13).unsqueeze(2).to_broadcast([P, NJ, 16])
            CB = K_tmp
            step(tt(BBt[:, 0], BRI[:, 0], zr, MUL))
            step(tt(BBt[:, 1], BRI[:, 1], zi, MUL))
            step(tt(CB[:, 0], BBt[:, 0], BBt[:, 1], SUB))
            step(tt(BBt[:, 0], BRI[:, 1], zr, MUL))
            step(tt(BBt[:, 1], BRI[:, 0], zi, MUL))
            step(tt(CB[:, 1], BBt[:, 0], BBt[:, 1], ADD))
            for b in range(4):
                for gi in range(2):
                    hp, cols = slice(64 * gi, 64 * gi + 64), slice(16 * (2 * b + gi), 16 * (2 * b + gi + 1))
                    for ri in range(2):
                        step(v.tensor_copy(BB[hp, ri, b::4, cols], CB[hp, ri, b::4, :]))
            step(v.memset(flag[:], 1.0), "s5_bb")
            step(v.tensor_copy(wpw[:, 0, 0], cs))
            step(v.tensor_copy(wpw[:, 0, 1], sn))
            for l in range(1, 10):
                c, s = wpw[:, l - 1, 0], wpw[:, l - 1, 1]
                step(tt(V(14), s, s, MUL))
                step(tt(V(15), c, c, MUL))
                step(tt(wpw[:, l, 0], V(15), V(14), SUB))
                step(stt(wpw[:, l, 1], c, 2.0, s, MUL, MUL))
            step(v.memset(flag[:], 0.0), "wpw_ready")
            ar = V(8).unsqueeze(2).to_broadcast([P, NJ, NS])
            ai = V(9).unsqueeze(2).to_broadcast([P, NJ, NS])
            step(tt(inj[:, 0], st5[:, 0], ar, MUL))
            step(tt(inj_t[:], st5[:, 1], ai, MUL))
            step(tt(inj[:, 0], inj[:, 0], inj_t[:], SUB))
            step(tt(inj[:, 1], st5[:, 1], ar, MUL))
            step(tt(inj_t[:], st5[:, 0], ai, MUL))
            step(tt(inj[:, 1], inj[:, 1], inj_t[:], ADD))
            for q in range(4):
                dve.wait_ge(sem("bt_turned"), q + 1)
                step(v.tensor_copy(BTl[:, q // 2, 4 * (q % 2):4 * (q % 2) + 4, :].rearrange("p a b -> p (a b)"),
                                   pb[6 + q % 2][:, :]), "bt_ev")
            dve.wait_ge(sem("ct_turned"), 1)
            cps = pb[6].rearrange("p (r a c) -> p r a c", r=2, a=2)
            for b in range(4):
                for gi in range(2):
                    hp, cols = slice(64 * gi, 64 * gi + 64), slice(16 * (2 * b + gi), 16 * (2 * b + gi + 1))
                    step(v.tensor_copy(CTl[hp, 0, b::4, cols], cps[hp, 0, :, cols]))
                    step(v.tensor_scalar(CTl[hp, 1, b::4, cols], cps[hp, 1, :, cols], -1.0, None, MUL))
            step(v.memset(flag[:], 1.0), "ct_ev")
            dve.wait_ge(sem("z_ev"), 2 * G)
            for a in range(2):
                step(v.tensor_scalar(Y[:, a, :], U5[:, a, :], par("s5_d", a), None, MUL))
            for j in range(NJ):
                col = lambda x: x[:, j:j + 1]
                tc, ts, Mg = tables[j % 2]
                dve.wait_ge(sem("tab_ready"), j + 1)
                dve.wait_ge(sem("e_ev"), 6 * (j + 1))
                for ri, e in enumerate((e0, e1)):
                    f = dec4(e[:, TP:T])[:, :, 0]
                    step(tt(f, f, inj[:, ri, j, :], ADD))
                step(tt(t0, e0, tc, MUL))
                step(tt(t1, e1, ts, MUL))
                step(tt(t0, t0, t1, ADD))
                step(tt(t1, e1, tc, MUL))
                step(tt(e0, e0, ts, MUL))
                step(tt(t1, t1, e0, SUB))
                step(v.tensor_tensor_scan(t0, Mg, t0, 0.0, MUL, ADD))
                step(v.tensor_tensor_scan(t1, Mg, t1, 0.0, MUL, ADD))
                step(tt(e0, t0, tc, MUL))
                step(tt(e1, t1, ts, MUL))
                step(tt(e0, e0, e1, SUB))
                step(tt(e1, t1, tc, MUL))
                step(tt(t0, t0, ts, MUL))
                step(tt(e1, e1, t0, ADD))
                for ri, e in enumerate((e0, e1)):
                    step(v.tensor_copy(ls5[:, ri, j, 0:1], e[:, TP - 1:TP]))
                    step(v.tensor_copy(ls5[:, ri, j, 1:], dec4(e[:, TP:T])[:, :, LS - 1]))
                step(v.memset(flag[:], 1.0), "s5_scanned")
                for g in range(G):
                    dve.wait_ge(sem("y5_done"), G * j + g + 1)
                    y = Y[:, j // 4, gcol(g)]
                    step(tt(y, pb[6 + (9 * j + 6 + g + 1) % 2][:, 0:GW], y, ADD), "y5_ev")
            for q in range(4):
                dve.wait_ge(sem("s5_lturned"), q + 1)
                src = pb[6 + (9 * NJ + q + 1) % 2][0:NSEQ, :].rearrange("p (j c) -> p j c", c=P)
                step(v.tensor_copy(s5out[0:NSEQ, 4 * (q % 2):4 * (q % 2) + 4, :, q // 2], src), "s5_rows")
            dve.wait_ge(sem("glu_ev"), 2 * G)
            step(tt(Y[:, 0, :], t0, e0, MUL))
            step(tt(Y[:, 1, :], t1, e1, MUL))
            dve.wait_ge(sem("s5_stored"), 32)
            dve.wait_ge(sem("z_ev"), 10 * G)
            cv = lambda x: x.rearrange("p (c t) -> p c t", t=HC)
            for t in range(2):
                if t:
                    dve.wait_ge(sem("hg_stored"), 64)
                q_, f_, v_, og = (ZH[:, i, t, :] for i in range(4))
                step(v.tensor_scalar(f_, f_, low[:, 3, t:t + 1], low[:, 0, t:t + 1], MUL, ADD))
                step(v.tensor_scalar(K0, f_, -1.0, 1.0, MUL, ADD))
                step(v.tensor_scalar(f_, f_, 1e-30, None, MAX))
                step(v.tensor_copy(Ht0, f_))
                step(v.memset(Ht1, 0.0))
                step(v.tensor_copy(cv(Ht1)[:, :, 0], cv(f_)[:, :, 0]))
                step(v.memset(cv(Ht0)[:, :, 0], 0.0))
                step(v.tensor_tensor_scan(HD, Ht0, Ht1, 0.0, MUL, ADD))
                for d in range(HC):
                    w = HC - d
                    kd = (K0, K1)[d % 2]
                    if d:
                        step(tt(cv(kd)[:, :, d:], cv((K1, K0)[d % 2])[:, :, d - 1:HC - 1], cv(f_)[:, :, d:], MUL))
                    step(v.tensor_copy(cv(HK)[:, :, HC - 1 - d], cv(kd)[:, :, HC - 1]))
                    if d >= 2:
                        dve.wait_ge(sem("att_done"), HC * t + d - 1)
                    step(tt(cv((Hp0, Hp1)[d % 2])[:, :, d:], cv(kd)[:, :, d:], cv(q_)[:, :, d:], MUL), "prod_ready")
                    if d:
                        lag_out(v, dve, step, tt, cv, t, d - 1, v_)
                lag_out(v, dve, step, tt, cv, t, HC - 1, v_)
                step(v.tensor_copy(chunk_decay[:], cv(HD)[:, :, HC - 1]))
                step(tt(HD, HD, q_, MUL))
                step(v.memset(Sx[:, 0, :], 0.0), "lags_done")
                step(v.memset(flag[:], 1.0), "hk_ready")
                dve.wait_ge(sem("hs_in"), 32 * (t + 1))
                mb = m16[:, :].unsqueeze(2).to_broadcast([P, 8, 64])
                for b in range(9):
                    dve.wait_ge(sem("tok_ev"), 9 * t + b + 1)
                    if 9 * t + b:
                        dve.wait_ge(sem("u_done"), 9 * t + b)
                    for hh in range(2):
                        vt = tok[:, b % 2, 1, 64 * hh:64 * hh + 64].unsqueeze(1).to_broadcast([P, 8, 64])
                        step(tt(Vblk[:, hh], vt, mb, MUL), "dve_step" if hh == 0 else "vblk_ready")
                    if b:
                        state_out(v, dve, step, stt, t, b - 1)
                state_out(v, dve, step, stt, t, 8)
                step(v.memset(flag[:], 1.0), "hg_states")
                dve.wait_ge(sem("oi_done"), t + 1)
                o3 = Ho.rearrange("p (g c) -> p g c", g=3)
                step(tt(o3, ps[:, 3:6, 0:384], o3, ADD), "oi_ev")
                dve.wait_ge(sem("hn_done"), t + 1)
                r3 = Hn.rearrange("p (g c) -> p g c", g=3)
                step(v.tensor_scalar(r3, ps[:, 0:3, 0:384], 1.0 / 64, RMS_EPS, MUL, ADD), "hn_ev")
                root(2 + t)
                step(stt(Ho, Ho, par("hg_norm", t), Hn, MUL, MUL))
                if t:
                    for k in range(3):
                        dve.wait_ge(sem(f"gate_saved{k}"), 16 * 12)
                y = Y[:, 6 + t, :]
                step(tt(y[:, 0:TP], Ho[:, 0:TP], og[:, 0:TP], MUL))
                step(tt(dec4(y[:, TP:T]), cv(Ho)[:, 64:, 0:LS], cv(og)[:, 64:, 0:LS], MUL), "hg_done")
            dve.wait_ge(sem("hg_stored"), 128)
            zcur = lambda z: (z[:, 1:1 + TP], z[:, 1 + TP:1065].rearrange("p (n t) -> p n t", t=LS + 1)[:, :, 1:])
            zprev = lambda z: (z[:, 0:TP], z[:, 1 + TP:1065].rearrange("p (n t) -> p n t", t=LS + 1)[:, :, 0:LS])
            pads = lambda x: (x[:, 0:16, :], x[:, 16:RN, 0:LS])
            flat = lambda x: (x[:, 0:TP], dec4(x[:, TP:T]))
            chunked = lambda x: (x[:, 0:TP].rearrange("p (c t) -> p c t", t=RCH), dec4(x[:, TP:T]))

            def mix(z, tile, tmp, dst, name):
                step(v.memset(z[:, 0:1], 0.0))
                sc = z[:, 1 + TP:1065].rearrange("p (n t) -> p n t", t=LS + 1)
                step(v.tensor_copy(sc[:, :, 0], shT[:, tile, :]))
                for o, a, b in zip(flat(tmp), zprev(z), zcur(z)):
                    step(tt(o, a, b, SUB))
                step(v.tensor_copy(shO[:, tile, 0:1], z[:, TP:TP + 1]))
                step(v.tensor_copy(shO[:, tile, 1:], sc[:, :, LS]), "sho_ready")
                for i, (o, a, b) in enumerate(zip(dst, flat(tmp), zcur(z))):
                    if len(o.shape) == 3 and len(a.shape) == 2:
                        a, b = (x.rearrange("p (c t) -> p c t", t=RCH) for x in (a, b))
                    step(stt(o, a, par("rw_mu", tile), b, MUL, ADD), name if i else "dve_step")

            dve.wait_ge(sem("z_ev"), 11 * G)
            mix(Z[0], 12, Kc, flat(Lx), "lora_mixed")
            for x in (ARp, Bp, Kp, Vp):
                n = 0 if len(x.shape) == 3 else 1
                dst = x[:, 16:RN].rearrange("p a b c -> p (a b c)") if n else x[:, 16:RN].rearrange("p a b -> p (a b)")
                step(v.memset(dst, 0.0))
            T1, T2, T3 = (z[:, 0:T] for z in Z[1:])
            pc = lambda i: ARp[:, :, i, :]
            for j in range(4):
                if j:
                    dve.wait_ge(sem("rw_stored"), 64 * j)
                dve.wait_ge(sem("sin_ev"), j + 1)
                dve.wait_ge(sem("z_ev"), (11 + 3 * (j + 1)) * G)
                mix(Z[1], j, C1, flat(Rc), "mixed")
                mix(Z[2], 4 + j, C1, flat(Kc), "mixed")
                mix(Z[3], 8 + j, C1, pads(Vp), "mixed")
                step(v.tensor_scalar(T3, Kc, par("rw_k_k", j), None, MUL), "kraw_ready")
                dve.wait_ge(sem("lora_ev"), 2 * j + 1)
                step(v.tensor_tensor_scan(C1, resets[:], T1, 0.0, MUL, ADD))
                step(tt(T1, C1, T1, SUB), "cums_ready")
                dve.wait_ge(sem("lora_ev"), 2 * j + 2)
                dve.wait_ge(sem("sum_done"), 7 * j + 3)
                kn = three(Y[:, 2 + j, :])
                step(v.tensor_scalar(kn, bank3(0), 1e-24, None, MAX), "sum_ev")
                root(4 + 2 * j)
                step(stt(T3, T3, 2.0 ** 15, Y[:, 2 + j, :], MUL, MUL))
                dve.wait_ge(sem("decays"), 3 * (j + 1))
                for o, a, b in zip(pads(pc(0)), chunked(T3), chunked(T1)):
                    step(stt(o, a, -1.0, b, MUL, MUL))
                step(tt(T1, T3, T2, MUL))
                for o, a, b in zip(pads(Bp), chunked(T1), chunked(C1)):
                    step(tt(o, a, b, MUL))
                step(v.tensor_scalar(T2, T2, 1.0, par("rw_k_a", j), SUB, MUL))
                step(stt(Kc, T2, 1.0, Kc, ADD, MUL))
                for o, a, b in zip(pads(Kp), chunked(Kc), chunked(C1)):
                    step(tt(o, a, b, MUL))
                for o, a, b in zip(pads(pc(1)), chunked(Rc), chunked(C2)):
                    step(tt(o, a, b, MUL))
                step(v.tensor_copy(PC[:, 0:16], chunked(C2)[0][:, :, RCH - 1]))
                step(v.tensor_copy(PC[:, 16:RN], chunked(C2)[1][:, :, LS - 1]))
                step(stt(Rc, Rc, par("rw_r_k", j), Kc, MUL, MUL), "rk_ready")
                step(v.memset(S2[:, 0, :], 0.0), "pads_ready")
                dve.wait_ge(sem("sum_done"), 7 * j + 4)
                step(v.tensor_copy(three(T2), bank3(3)), "sum_ev")
                for a, b in zip(chunked(T2), pads(Vp)):
                    step(tt(a, a, b, MUL))
                for bt in range(3):
                    for half in range(2):
                        dve.wait_ge(sem("la_done"), 5 * (3 * j + bt) + half + 1)
                        step(tt(LA[:, 4 * half:4 * half + 4], pb[3 + half].rearrange("p (c a t) -> p c a t", c=4, a=2),
                                m_ar[:].unsqueeze(1).to_broadcast([P, 4, 2, RCH]), MUL), "la_ev")
                    for half in range(2):
                        dve.wait_ge(sem("la_done"), 5 * (3 * j + bt) + half + 3)
                        step(tt(KA[:, 4 * half:4 * half + 4], pb[5 + half].rearrange("p (c a t) -> p c a t", c=4, a=2),
                                m_ar[:].unsqueeze(1).to_broadcast([P, 4, 2, RCH]), MUL), "la_ev")
                    dve.wait_ge(sem("la_done"), 5 * (3 * j + bt + 1))
                    m8 = lambda m: m.unsqueeze(1).to_broadcast([P, 8, RCH])
                    step(tt(X[:], pb[7].rearrange("p (c t) -> p c t", c=8), m8(m_l0[:]), MUL), "la_ev")
                    step(tt(X[:], X[:], m8(idS[:]), ADD))
                    step(tt(XT[:], LA[:, :, 0, :], m8(m_lt[:, 0, :]), MUL))
                    step(tt(XT[:], XT[:], m8(idS[:]), ADD))
                    if bt == 0:
                        dve.wait_ge(sem("bd_zeroed"), j + 1)

                    def spread(hc, name):
                        for h in range(2):
                            hp = slice(64 * h, 64 * h + 64)
                            step(v.tensor_copy(XTbd[hp, hc, h, :], XT[hp, hc, :]), name if h else "dve_step")

                    spread(slice(0, 8), "x_init")
                    last = 5 if bt < 2 else 1
                    for l in range(1, last + 1):
                        n = lt_count(j, bt, l)
                        for half in range(2):
                            hc = slice(4 * half, 4 * half + 4)
                            dve.wait_ge(sem("zt_done"), 2 * (n - 1) + half + 1)
                            zx = pb[2 + half][:, 0:256].rearrange("p (c t) -> p c t", c=4)
                            zt = pb[4 + half][:, 0:256].rearrange("p (c t) -> p c t", c=4)
                            if l < last:
                                step(tt(X[:, hc], zx, X[:, hc], ADD), "zx_ev")
                            step(tt(XT[:, hc], zt, XT[:, hc], ADD))
                            spread(hc, "zt_ev")
                    if bt == 2:
                        n = STEPS * j + 16
                        f8 = lambda x: x.rearrange("p c t -> p (c t)")
                        step(v.memset(flag[:], 0.0), "s_ready")
                        dve.wait_ge(sem("g_done"), n + 1)
                        step(v.tensor_copy(f8(LTm[:]), pb[3]), "g_ev")
                        dve.wait_ge(sem("ub_done"), j + 1)
                        step(v.tensor_copy(f8(Yb[:]), pb[4]), "ub_ev")
                        dve.wait_ge(sem("ds_done"), n + 1)
                        step(tt(f8(Sout[:]), pb[5], f8(Sin[:]), ADD))
                        step(tt(Sout[:], Sout[:], PC[:, 16:RN].unsqueeze(2).to_broadcast([P, 8, RCH]), MUL), "ds_ev")
                    for c in range(8 if bt < 2 else 0):
                        ci = 8 * bt + c
                        n = STEPS * j + ci
                        S0 = S2[:, ci % 2, :]
                        S1 = S2[:, (ci + 1) % 2, :]
                        step(v.tensor_scalar(SPc, S0, PC[:, ci:ci + 1], None, MUL))
                        dve.wait_ge(sem("g_done"), n + 1)
                        step(v.tensor_copy(Ub, pb[(4, 6)[c % 2]][:, 0:64]), "g_ev")
                        dve.wait_ge(sem("ds_done"), n + 1)
                        step(stt(S1, pb[(5, 1)[c % 2]][:, 0:64], PC[:, ci:ci + 1], SPc, MUL, ADD), "ds_ev")
                    dve.wait_ge(sem("ry_done"), 3 * j + bt + 1)
                    y = Y[:, 2 + j, :]
                    src = pb[7].rearrange("p (c t) -> p c t", c=8)
                    if bt < 2:
                        step(v.tensor_copy(y[:, 512 * bt:512 * bt + 512], pb[7]), "ry_ev")
                    else:
                        step(v.tensor_copy(dec4(y[:, TP:T]), src[:, :, 0:LS]), "ry_ev")
                y = Y[:, 2 + j, :]
                dve.wait_ge(sem("sum_done"), 7 * j + 5)
                step(stt(three(C1), bank3(0), -1.0 / 64, three(y), MUL, ADD), "sum_ev")
                step(v.memset(SPc, 0.0), "centred")
                dve.wait_ge(sem("sum_done"), 7 * j + 6)
                step(v.tensor_scalar(three(Kc), bank3(3), 1.0 / 64, GN_EPS, MUL, ADD), "sum_ev")
                root(5 + 2 * j)
                step(tt(C1, C1, Kc, MUL))
                step(v.tensor_scalar(C1, C1, par("rw_ln_w", j), par("rw_ln_b", j), MUL, ADD))
                step(tt(C1, C1, T2, ADD))
                dve.wait_ge(sem("sum_done"), 7 * j + 7)
                step(tt(three(y), bank3(0), three(C1), MUL), "sum_ev")
                step(v.memset(SPc, 0.0), "rw_done")
            dve.wait_ge(sem("rw_stored"), 256)
            for n in range(KT):
                for br in range(3):
                    u = 3 * n + br
                    dve.wait_ge(sem("gemm_done"), signals[index[("lift", 0)]] + u + 1)
                    dve.wait_ge(sem(f"sg_in{br}"), 16 * (n + 1))
                    gt, lift = sg[:, br, :], bank3(3 * (u % 2))
                    if br == 0:
                        step(tt(three(MG[:, n, :]), lift, three(gt), MUL), "lift_ev")
                        step(v.memset(flag[:], 0.0), "sg_used")
                    else:
                        step(tt(three(gt), lift, three(gt), MUL), "lift_ev")
                        step(tt(MG[:, n, :], MG[:, n, :], gt, ADD), "sg_used")
                step(v.memset(flag[:], 0.0), "mg_ready")
            dve.wait_ge(sem("mod_rest"), 8)
            scales(1)

            res = [RING_OUT]

            def residual(base, gate, n_norm=None):
                for m_ in range(KT):
                    for g in range(G):
                        b = res[0] % 6
                        res[0] += 1
                        dve.wait_ge(sem("gemm_done"), base + G * m_ + g + 1)
                        n = min(GW, TP - g * GW)
                        x = xT[:, m_, g * GW:g * GW + n]
                        gt = MOD[:, gate + m_, :]
                        ins = stt(x, pb[b][:, 0:n], gt[:, 0:1], x, MUL, ADD)
                        if n == GW:
                            step(ins, "res_ev")
                            continue
                        step(ins)
                        d = dec4(res_t[:])
                        step(tt(d, dec4(pb[b][:, n:GW]), gt[:, 1:].unsqueeze(2).to_broadcast([P, NS, LS]), MUL))
                        x = xT[:, m_, TP:T]
                        step(tt(x, x, res_t[:], ADD), "res_ev")
                    if n_norm is not None:
                        squares(n_norm, m_)

            dve.wait_ge(sem("x_ev"), 4 * XQ)
            residual(signals[index[("out", 0)]], 16, 1)
            dve.wait_ge(sem("sh_stored"), 32)
            normed(1)
            shifted(1)
            for i in range(4):
                step(v.memset(Uab[i][:, 0:2], 0.0))
            step(v.memset(res_t[:, 0:1], 0.0), "u_zeroed")
            for half, (m0, m1) in enumerate(HALVES):
                for p in range(m0, m1):
                    for s in range(2):
                        q = 4 * (p // 2) + 2 * (p % 2) + s
                        dve.wait_ge(sem("u_in"), G * (q + 1))
                        if s == 0 and p >= 2:
                            dve.wait_ge(sem("gelu_done"), p - 1)
                        u = Uab[q % 4]
                        c = Cab[p % 2] if s == 0 else Cab[2]
                        dec = u[:, 2 + TP:UL].rearrange("p (n t) -> p n t", t=LS + 2)
                        ch = FT * s + p
                        for k in range(3):
                            wk = par(f"conv_w{k}", ch)
                            for o, src in ((c[:, 0:TP], u[:, k:k + TP]), (dec4(c[:, TP:T]), dec[:, :, k:k + LS])):
                                final = k == 2 and len(o.shape) == 3
                                if k == 0:
                                    ins = v.tensor_scalar(o, src, wk, par("conv_b", ch), MUL, ADD)
                                else:
                                    ins = stt(o, src, wk, o, MUL, ADD)
                                step(ins, "u_used" if final else "dve_step")
                        if s == 0:
                            step(v.memset(res_t[:, 0:1], 0.0), "conv_a")
                    dve.wait_ge(sem("gelu_done"), p + 1)
                    f = FFh[:, p - m0, :]
                    step(tt(f, f, Cab[2], MUL), "ff_ready")
                res[0] += 2 * (m1 - m0) * G
                residual(signals[index[("down", (m0, 0))]], 40, 2 if half else None)
            normed(2)
            step(v.memset(flag[:], 0.0), "h_ready")


def build(nc, args):
    I = dict(zip(_INS, args[:len(_INS)]))
    O = dict(zip(("y_p", "y_s", "s5_p", "sh_p", "rw_p", "hg_p", "cv_p", "s5_s", "sh_s", "rw_s", "hg_s", "cv_s"),
                 args[len(_INS):]))
    trunk(nc, I, O)


_INS = ['x_prompt', 'x_sample', 'c_prompt', 'c_sample', 'state_s5', 'state_rwkv_shift', 'state_rwkv', 'state_hgrn',
        'state_ffn_conv', 'w_ada', 'b_ada', 'g_mix', 'g_ffn', 'w_in', 's5_lambda_re', 's5_lambda_im', 's5_log_dt',
        's5_b_re', 's5_b_im', 's5_c_re', 's5_c_im', 's5_d', 's5_w_glu', 's5_b_glu', 'rw_mu', 'rw_w0', 'rw_w2',
        'rw_a0', 'rw_a2', 'rw_g2', 'rw_k_k', 'rw_k_a', 'rw_r_k', 'rw_ln_w', 'rw_ln_b', 'hg_lb', 'hg_norm',
        'w_lift_a', 'w_lift_b', 'w_lift_c', 'w_out', 'w_up', 'conv_w', 'conv_b', 'w_down', 'final_g']
_OUTS = [((1, 1024, 1024), 'float32'), ((8, 4, 1024), 'float32'),
         ((1, 1, 16, 64, 2), 'float32'), ((1, 1, 1664), 'float32'), ((1, 1, 8, 64, 64), 'float32'),
         ((1, 1, 4, 64, 64), 'float32'), ((1, 1, 2, 5632), 'float32'),
         ((1, 8, 16, 64, 2), 'float32'), ((1, 8, 1664), 'float32'), ((1, 8, 8, 64, 64), 'float32'),
         ((1, 8, 4, 64, 64), 'float32'), ((1, 8, 2, 5632), 'float32')]


def kernel(**inputs):
    import numpy as _np
    import concourse.bacc as _bacc
    from concourse import mybir as _mybir
    from concourse.bass_utils import run_bass_kernel_spmd as _run

    nc = _bacc.Bacc("TRN2", target_bir_lowering=False, num_devices=1)
    arrays, args = {}, []
    for name in _INS:
        a = _np.ascontiguousarray(inputs[name])
        arrays[f"in_{name}_dram"] = a
        args.append(nc.dram_tensor(f"in_{name}_dram", a.shape, _mybir.dt.from_np(a.dtype), kind="ExternalInput").ap())
    for i, (shape, dtype) in enumerate(_OUTS):
        dt = _mybir.dt.from_np(_np.dtype(dtype))
        args.append(nc.dram_tensor(f"out_{i}_dram", shape, dt, kind="ExternalOutput").ap())
    build(nc, args)
    r = _run(nc, [arrays], core_ids=[0])
    return tuple(r.results[0][f"out_{i}_dram"] for i in range(len(_OUTS)))
```
